# Optimizing a Trainium2 kernel written in Bass

```python
import jax, jax.numpy as jnp
from jax import lax
import numpy as np

D_MODEL = 1024
BATCH = 1
SEQ = 512
DEPTH = 1
DEC_BATCH = 8
DEC_SEQ = 4
PAST_LEN = 4096
PAGE_SIZE = 128

HEAD_DIM = 64
NSA_HEADS = 8
NSA_KV_GROUPS = 2
NSA_REP = NSA_HEADS // NSA_KV_GROUPS
NSA_N_BRANCH = 3
CMP_BLOCK = 32
CMP_STRIDE = 16
CMP_SPAN = CMP_BLOCK // CMP_STRIDE
CMP_HIDDEN = 128
SEL_BLOCK = 64
N_SEL = 16
NSA_WINDOW = 512
BLOCKS_PER_PAGE = PAGE_SIZE // SEL_BLOCK
DIL_CONFIGS = ((128, 1), (512, 4), (2048, 16))
N_DIL_GROUPS = 3
DIL_HEADS = 8
SGU_CHUNK = 128
SGU_GROUPS = 8
SGU_WIDTH = SGU_GROUPS * HEAD_DIM
D_FF = 4 * D_MODEL
N_BRANCHES = 3
NSA_Q_W = NSA_HEADS * HEAD_DIM
NSA_KV_W = NSA_KV_GROUPS * HEAD_DIM
DIL_W = DIL_HEADS * HEAD_DIM
COL_SPLITS = (NSA_Q_W, 2 * NSA_N_BRANCH * NSA_KV_W, NSA_N_BRANCH * NSA_HEADS, 3 * N_DIL_GROUPS * DIL_W, 2 * SGU_WIDTH, N_BRANCHES * D_MODEL)
D_IN = sum(COL_SPLITS)
SPLIT_POINTS = tuple(int(c) for c in np.cumsum(COL_SPLITS)[:-1])
BLOCK_Q = 128
SEL_Q_BLOCK = 32
FORCED_SCORE = 1e4
RMS_EPS = 1e-6
LN_EPS = 1e-5
ATTN_SCALE = HEAD_DIM ** -0.5

kernel_name = 'hybrid_nsa_dilated_sgu_decode_step'

def rms_norm(x, g):
    x32 = x.astype(jnp.float32)
    y = x32 * lax.rsqrt(jnp.mean(x32 * x32, axis=-1, keepdims=True) + RMS_EPS)
    return (y * g.astype(jnp.float32)).astype(x.dtype)

def layer_norm(x, g, b):
    x32 = x.astype(jnp.float32)
    xc = x32 - jnp.mean(x32, axis=-1, keepdims=True)
    y = xc * lax.rsqrt(jnp.mean(xc * xc, axis=-1, keepdims=True) + LN_EPS)
    return (y * g.astype(jnp.float32) + b.astype(jnp.float32)).astype(x.dtype)

def masked_softmax(s, mask):
    s = jnp.where(mask, s, -jnp.inf)
    m = jnp.max(s, axis=-1, keepdims=True)
    m = jnp.where(jnp.isfinite(m), m, 0.0)
    e = jnp.exp(s - m)
    den = jnp.sum(e, axis=-1, keepdims=True)
    p = e / jnp.where(den > 0.0, den, 1.0)
    lse = jnp.squeeze(m + jnp.log(den), axis=-1)
    return p, lse

def banded_attention(q, k, v, window):
    n, length, g, r, dh = q.shape
    nb = -(-length // BLOCK_Q)
    lp = nb * BLOCK_Q
    front = -(-window // BLOCK_Q) * BLOCK_Q
    span = front + BLOCK_Q
    qp = jnp.pad(q, ((0, 0), (0, lp - length), (0, 0), (0, 0), (0, 0)))
    kp = jnp.pad(k, ((0, 0), (front, lp - length), (0, 0), (0, 0)))
    vp = jnp.pad(v, ((0, 0), (front, lp - length), (0, 0), (0, 0)))
    qi = jnp.arange(BLOCK_Q)[:, None]
    kj = jnp.arange(span)[None, :]
    dist = qi + front - kj
    band = (dist >= 0) & (dist <= window)

    def one_block(b):
        start = b * BLOCK_Q
        qb = lax.dynamic_slice_in_dim(qp, start, BLOCK_Q, axis=1)
        kb = lax.dynamic_slice_in_dim(kp, start, span, axis=1)
        vb = lax.dynamic_slice_in_dim(vp, start, span, axis=1)
        mask = band & (start + kj >= front)
        s = jnp.einsum('nqgrd,nkgd->nqgrk', qb, kb).astype(jnp.float32) * ATTN_SCALE
        p, lse = masked_softmax(s, mask[None, :, None, None, :])
        o = jnp.einsum('nqgrk,nkgd->nqgrd', p.astype(vb.dtype), vb)
        return o, lse

    o, lse = lax.map(one_block, jnp.arange(nb))
    o = jnp.moveaxis(o, 0, 1).reshape(n, lp, g, r, dh)[:, :length]
    lse = jnp.moveaxis(lse, 0, 1).reshape(n, lp, g, r)[:, :length]
    return o, lse

def split_residues(x, dil):
    b, t = x.shape[:2]
    y = jnp.moveaxis(x.reshape((b, t // dil, dil) + x.shape[2:]), 2, 1)
    return y.reshape((b * dil, t // dil) + x.shape[2:])

def merge_residues(y, dil, b):
    length = y.shape[1]
    x = jnp.moveaxis(y.reshape((b, dil, length) + y.shape[2:]), 1, 2)
    return x.reshape((b, length * dil) + y.shape[2:])

def combine_by_denominator(outs, lses):
    w = jax.nn.softmax(jnp.stack(lses, axis=0), axis=0)
    o = jnp.einsum('gbth,gbthd->bthd', w.astype(outs[0].dtype), jnp.stack(outs, axis=0))
    b, t = o.shape[:2]
    return o.reshape(b, t, DIL_W)

def dilated_prompt(qkv):
    b, t = qkv.shape[:2]
    outs, lses, bufs = [], [], []
    for g, (window, dil) in enumerate(DIL_CONFIGS):
        q, k, v = qkv[:, :, 0, g], qkv[:, :, 1, g], qkv[:, :, 2, g]
        o, lse = banded_attention(split_residues(q, dil)[:, :, :, None], split_residues(k, dil), split_residues(v, dil), window // dil)
        outs.append(merge_residues(o[:, :, :, 0], dil, b))
        lses.append(merge_residues(lse[:, :, :, 0], dil, b))
        bufs.append(jnp.stack([k, v], axis=2)[:, -min(window, t):])
    return combine_by_denominator(outs, lses), bufs

def dilated_sample(qkv, bufs_in):
    s_len = qkv.shape[1]
    outs, lses, bufs = [], [], []
    for g, ((window, dil), buf) in enumerate(zip(DIL_CONFIGS, bufs_in)):
        q = qkv[:, :, 0, g]
        kv_ext = jnp.concatenate([buf, jnp.stack([qkv[:, :, 1, g], qkv[:, :, 2, g]], axis=2)], axis=1)
        wb = buf.shape[1]
        idx = wb + jnp.arange(s_len)[:, None] - dil * jnp.arange(window // dil + 1)[None, :]
        valid = idx >= 0
        kvg = kv_ext[:, jnp.maximum(idx, 0)]
        s = jnp.einsum('bshd,bsnhd->bshn', q, kvg[:, :, :, 0]).astype(jnp.float32) * ATTN_SCALE
        p, lse = masked_softmax(s, valid[None, :, None, :])
        outs.append(jnp.einsum('bshn,bsnhd->bshd', p.astype(kvg.dtype), kvg[:, :, :, 1]))
        lses.append(lse)
        bufs.append(kv_ext[:, -min(window, wb + s_len):])
    return combine_by_denominator(outs, lses), bufs

def compress_rows(x, pe, w1, b1, w2):
    b, t, g, dh = x.shape
    nseg = t // CMP_STRIDE
    nc = nseg - CMP_SPAN + 1
    segs = x[:, :nseg * CMP_STRIDE].reshape(b, nseg, CMP_STRIDE, g, dh)
    blocks = jnp.concatenate([segs[:, j:j + nc] for j in range(CMP_SPAN)], axis=2)
    blocks = blocks + pe[:, None, :].astype(x.dtype)
    flat = jnp.moveaxis(blocks, 3, 2).reshape(b, nc, g, CMP_BLOCK * dh)
    return jax.nn.gelu(flat @ w1 + b1) @ w2

def nsa_compressed(q, kc, vc, qpos, cmp_pe, cmp_w1, cmp_b1, cmp_w2):
    kcmp = compress_rows(kc, cmp_pe[0], cmp_w1[0], cmp_b1[0], cmp_w2[0])
    vcmp = compress_rows(vc, cmp_pe[1], cmp_w1[1], cmp_b1[1], cmp_w2[1])
    nc = kcmp.shape[1]
    block_end = jnp.arange(nc) * CMP_STRIDE + (CMP_BLOCK - 1)
    mask = block_end[None, :] <= qpos[:, None]
    s = jnp.einsum('btgrd,bcgd->btgrc', q, kcmp).astype(jnp.float32) * ATTN_SCALE
    p, _ = masked_softmax(s, mask[None, :, None, None, :])
    o = jnp.einsum('btgrc,bcgd->btgrd', p.astype(vcmp.dtype), vcmp)
    return o, jnp.sum(p, axis=3)

def select_blocks(p_imp, qpos, n_blocks):
    nc = p_imp.shape[-1]
    ratio = SEL_BLOCK // CMP_STRIDE
    ci = jnp.arange(nc)[:, None]
    bj = jnp.arange(n_blocks)[None, :]
    overlap = sum((ci == ratio * bj + m - n).astype(jnp.float32) for m in range(ratio) for n in range(CMP_SPAN))
    score = jnp.einsum('btgc,cj->btgj', p_imp.astype(jnp.float32), overlap)
    cur = (qpos // SEL_BLOCK)[:, None]
    forced = (bj == 0) | (bj == cur) | (bj == cur - 1)
    valid = bj <= cur
    score = jnp.where(forced[None, :, None, :], FORCED_SCORE, score)
    score = jnp.where(valid[None, :, None, :], score, -jnp.inf)
    vals, idx = lax.top_k(score, min(N_SEL, n_blocks))
    return idx, jnp.isfinite(vals)

def gathered_attention(q, kg, vg, kpos, ok, qpos):
    b, nq, g, n, sb, dh = kg.shape
    kf = kg.reshape(b, nq, g, n * sb, dh)
    vf = vg.reshape(b, nq, g, n * sb, dh)
    mask = (ok[..., None] & (kpos <= qpos[None, :, None, None, None])).reshape(b, nq, g, n * sb)
    s = jnp.einsum('bqgrd,bqgkd->bqgrk', q, kf).astype(jnp.float32) * ATTN_SCALE
    p, _ = masked_softmax(s, mask[:, :, :, None, :])
    return jnp.einsum('bqgrk,bqgkd->bqgrd', p.astype(vf.dtype), vf)

def gate_branches(gates, o_cmp, o_sel, o_win):
    o = gates[..., 0:1] * o_cmp + gates[..., 1:2] * o_sel + gates[..., 2:3] * o_win
    b, t = o.shape[:2]
    return o.reshape(b, t, NSA_Q_W)

def nsa_prompt(q, kv, gates, cmp_pe, cmp_w1, cmp_b1, cmp_w2):
    b, t, g, r, dh = q.shape
    qpos = jnp.arange(t)
    kc, vc, ks, vs, kw, vw = [kv[:, :, i] for i in range(2 * NSA_N_BRANCH)]
    o_cmp, p_imp = nsa_compressed(q, kc, vc, qpos, cmp_pe, cmp_w1, cmp_b1, cmp_w2)
    n_blocks = t // SEL_BLOCK
    idx, ok = select_blocks(p_imp, qpos, n_blocks)
    kb = ks.reshape(b, n_blocks, SEL_BLOCK, g, dh)
    vb = vs.reshape(b, n_blocks, SEL_BLOCK, g, dh)
    nq = t // SEL_Q_BLOCK
    b_ix = jnp.arange(b)[:, None, None, None]
    g_ix = jnp.arange(g)[None, None, :, None]

    def to_blocks(a):
        return jnp.moveaxis(a.reshape((a.shape[0], nq, SEL_Q_BLOCK) + a.shape[2:]), 1, 0)

    def one_block(args):
        qc, ic, okc, pc = args
        kg = kb[b_ix, ic, :, g_ix]
        vg = vb[b_ix, ic, :, g_ix]
        kpos = ic[..., None] * SEL_BLOCK + jnp.arange(SEL_BLOCK)
        return gathered_attention(qc, kg, vg, kpos, okc, pc)

    o_sel = lax.map(one_block, (to_blocks(q), to_blocks(idx), to_blocks(ok), qpos.reshape(nq, SEL_Q_BLOCK)))
    o_sel = jnp.moveaxis(o_sel, 0, 1).reshape(q.shape)
    o_win, _ = banded_attention(q, kw, vw, NSA_WINDOW)
    new_cmp = jnp.stack([kc, vc], axis=2)
    new_sel = jnp.stack([ks, vs], axis=2)
    new_win = jnp.stack([kw, vw], axis=2)[:, -min(NSA_WINDOW, t):]
    return gate_branches(gates, o_cmp, o_sel, o_win), new_cmp, new_sel, new_win

def nsa_sample(q, kv, gates, cache_cmp, cache_sel, win_buf, page_table, layer, cmp_pe, cmp_w1, cmp_b1, cmp_w2):
    b, s_len, g, r, dh = q.shape
    n_pages = page_table.shape[1]
    past = n_pages * PAGE_SIZE
    qpos = past + jnp.arange(s_len)
    kc, vc, ks, vs, kw, vw = [kv[:, :, i] for i in range(2 * NSA_N_BRANCH)]
    new_cmp = jnp.stack([kc, vc], axis=2)
    cmp_rows = jnp.concatenate([cache_cmp[page_table, layer].reshape(b, past, 2, g, dh), new_cmp], axis=1)
    o_cmp, p_imp = nsa_compressed(q, cmp_rows[:, :, 0], cmp_rows[:, :, 1], qpos, cmp_pe, cmp_w1, cmp_b1, cmp_w2)
    n_past_blocks = past // SEL_BLOCK
    n_tail = -(-s_len // SEL_BLOCK)
    idx, ok = select_blocks(p_imp, qpos, n_past_blocks + n_tail)
    new_sel = jnp.stack([ks, vs], axis=2)
    tail = jnp.pad(new_sel, ((0, 0), (0, n_tail * SEL_BLOCK - s_len), (0, 0), (0, 0), (0, 0))).reshape(b, n_tail, SEL_BLOCK, 2, g, dh)
    b_ix = jnp.arange(b)[:, None, None, None]
    g_ix = jnp.arange(g)[None, None, :, None]
    in_past = idx < n_past_blocks
    jp = jnp.minimum(idx, n_past_blocks - 1)
    phys = page_table[b_ix, jp // BLOCKS_PER_PAGE]
    rows = (jp % BLOCKS_PER_PAGE)[..., None] * SEL_BLOCK + jnp.arange(SEL_BLOCK)
    past_kv = cache_sel[phys[..., None], layer, rows, :, g_ix[..., None], :]
    tail_kv = tail[b_ix, jnp.clip(idx - n_past_blocks, 0, n_tail - 1), :, :, g_ix]
    sel_kv = jnp.where(in_past[..., None, None, None], past_kv, tail_kv)
    kpos = idx[..., None] * SEL_BLOCK + jnp.arange(SEL_BLOCK)
    o_sel = gathered_attention(q, sel_kv[..., 0, :], sel_kv[..., 1, :], kpos, ok, qpos)
    win_ext = jnp.concatenate([win_buf, jnp.stack([kw, vw], axis=2)], axis=1)
    wb = win_buf.shape[1]
    dist = wb + jnp.arange(s_len)[:, None] - jnp.arange(wb + s_len)[None, :]
    mask = (dist >= 0) & (dist <= NSA_WINDOW)
    sw = jnp.einsum('bsgrd,bkgd->bsgrk', q, win_ext[:, :, 0]).astype(jnp.float32) * ATTN_SCALE
    pw, _ = masked_softmax(sw, mask[None, :, None, None, :])
    o_win = jnp.einsum('bsgrk,bkgd->bsgrd', pw.astype(win_ext.dtype), win_ext[:, :, 1])
    new_win = win_ext[:, -min(NSA_WINDOW, wb + s_len):]
    return gate_branches(gates, o_cmp, o_sel, o_win), new_cmp, new_sel, new_win

def sgu_mixer(u, v, ln_g, ln_b, w_s, b_s):
    b, t = u.shape[:2]
    u = jax.nn.gelu(u)
    v = layer_norm(jax.nn.gelu(v), ln_g, ln_b)
    nc = -(-t // SGU_CHUNK)
    vp = jnp.pad(v, ((0, 0), (0, nc * SGU_CHUNK - t), (0, 0))).reshape(b, nc, SGU_CHUNK, SGU_GROUPS, HEAD_DIM)
    causal = jnp.tril(jnp.ones((SGU_CHUNK, SGU_CHUNK), dtype=bool))
    w_c = jnp.where(causal, w_s, 0.0).astype(v.dtype)
    mixed = jnp.einsum('hts,bcshd->bcthd', w_c, vp) + jnp.transpose(b_s)[None, None, :, :, None].astype(v.dtype)
    mixed = mixed.reshape(b, nc * SGU_CHUNK, SGU_WIDTH)[:, :t]
    return u * mixed, v

def project_inputs(h, w_in_l):
    b, t = h.shape[:2]
    q_a, kv_a, gate_a, qkv_b, uv_c, gate_m = jnp.split(h @ w_in_l, SPLIT_POINTS, axis=-1)
    q_a = q_a.reshape(b, t, NSA_KV_GROUPS, NSA_REP, HEAD_DIM)
    kv_a = kv_a.reshape(b, t, 2 * NSA_N_BRANCH, NSA_KV_GROUPS, HEAD_DIM)
    gate_a = jax.nn.sigmoid(gate_a.reshape(b, t, NSA_KV_GROUPS, NSA_REP, NSA_N_BRANCH))
    qkv_b = qkv_b.reshape(b, t, 3, N_DIL_GROUPS, DIL_HEADS, HEAD_DIM)
    u_c, v_c = jnp.split(uv_c, 2, axis=-1)
    gate_m = jax.nn.sigmoid(gate_m.reshape(b, t, N_BRANCHES, D_MODEL))
    return q_a, kv_a, gate_a, qkv_b, u_c, v_c, gate_m

def merge_and_ffn(x, o_a, o_b, o_c, gate_m, wa, wb, wc, wo, g_mlp, w_up, w_down):
    m = gate_m[:, :, 0] * (o_a @ wa) + gate_m[:, :, 1] * (o_b @ wb) + gate_m[:, :, 2] * (o_c @ wc)
    x = x + m @ wo
    h = rms_norm(x, g_mlp)
    return x + jnp.square(jax.nn.relu(h @ w_up)) @ w_down

def setup_inputs(seed: int = 0) -> dict:
    key = jax.random.key(seed)
    ks = jax.random.split(key, 32)
    f32 = jnp.float32
    n_pages = PAST_LEN // PAGE_SIZE
    n_used = DEC_BATCH * n_pages
    n_pool = n_used + -(-n_used // 4)
    page_table = jax.random.permutation(ks[0], n_pool)[:n_used].reshape(DEC_BATCH, n_pages).astype(jnp.int32)

    def normal(k, shape, scale=1.0):
        return jax.random.normal(k, shape, f32) * scale

    return {
        'x_prompt': normal(ks[1], (BATCH, SEQ, D_MODEL)),
        'x_sample': normal(ks[2], (DEC_BATCH, DEC_SEQ, D_MODEL)),
        'cache_cmp_kv': normal(ks[3], (n_pool, DEPTH, PAGE_SIZE, 2, NSA_KV_GROUPS, HEAD_DIM)),
        'cache_sel_kv': normal(ks[4], (n_pool, DEPTH, PAGE_SIZE, 2, NSA_KV_GROUPS, HEAD_DIM)),
        'cache_win_kv': normal(ks[5], (DEC_BATCH, DEPTH, min(NSA_WINDOW, PAST_LEN), 2, NSA_KV_GROUPS, HEAD_DIM)),
        'cache_dil1_kv': normal(ks[6], (DEC_BATCH, DEPTH, min(DIL_CONFIGS[0][0], PAST_LEN), 2, DIL_HEADS, HEAD_DIM)),
        'cache_dil2_kv': normal(ks[7], (DEC_BATCH, DEPTH, min(DIL_CONFIGS[1][0], PAST_LEN), 2, DIL_HEADS, HEAD_DIM)),
        'cache_dil3_kv': normal(ks[8], (DEC_BATCH, DEPTH, min(DIL_CONFIGS[2][0], PAST_LEN), 2, DIL_HEADS, HEAD_DIM)),
        'page_table': page_table,
        'norm_mix_g': 1.0 + normal(ks[9], (DEPTH, D_MODEL), 0.05),
        'w_in': normal(ks[10], (DEPTH, D_MODEL, D_IN), D_MODEL ** -0.5),
        'cmp_pe': normal(ks[11], (DEPTH, 2, CMP_BLOCK, HEAD_DIM), 0.1),
        'cmp_w1': normal(ks[12], (DEPTH, 2, CMP_BLOCK * HEAD_DIM, CMP_HIDDEN), (CMP_BLOCK * HEAD_DIM) ** -0.5),
        'cmp_b1': normal(ks[13], (DEPTH, 2, CMP_HIDDEN), 0.02),
        'cmp_w2': normal(ks[14], (DEPTH, 2, CMP_HIDDEN, HEAD_DIM), CMP_HIDDEN ** -0.5),
        'sgu_ln_g': 1.0 + normal(ks[15], (DEPTH, SGU_WIDTH), 0.05),
        'sgu_ln_b': normal(ks[16], (DEPTH, SGU_WIDTH), 0.02),
        'sgu_w': normal(ks[17], (DEPTH, SGU_GROUPS, SGU_CHUNK, SGU_CHUNK), SGU_CHUNK ** -0.5),
        'sgu_b': 1.0 + normal(ks[18], (DEPTH, SGU_GROUPS, SGU_CHUNK), 0.1),
        'w_branch_a': normal(ks[19], (DEPTH, NSA_Q_W, D_MODEL), NSA_Q_W ** -0.5),
        'w_branch_b': normal(ks[20], (DEPTH, DIL_W, D_MODEL), DIL_W ** -0.5),
        'w_branch_c': normal(ks[21], (DEPTH, SGU_WIDTH, D_MODEL), SGU_WIDTH ** -0.5),
        'w_out': normal(ks[22], (DEPTH, D_MODEL, D_MODEL), D_MODEL ** -0.5),
        'norm_mlp_g': 1.0 + normal(ks[23], (DEPTH, D_MODEL), 0.05),
        'w_up': normal(ks[24], (DEPTH, D_MODEL, D_FF), D_MODEL ** -0.5),
        'w_down': normal(ks[25], (DEPTH, D_FF, D_MODEL), D_FF ** -0.5),
        'norm_final_g': 1.0 + normal(ks[26], (D_MODEL,), 0.05),
    }

def reference(x_prompt, x_sample, cache_cmp_kv, cache_sel_kv, cache_win_kv, cache_dil1_kv, cache_dil2_kv, cache_dil3_kv, page_table, norm_mix_g, w_in, cmp_pe, cmp_w1, cmp_b1, cmp_w2, sgu_ln_g, sgu_ln_b, sgu_w, sgu_b, w_branch_a, w_branch_b, w_branch_c, w_out, norm_mlp_g, w_up, w_down, norm_final_g):
    xp, xs = x_prompt, x_sample
    names = ('cmp_p', 'sel_p', 'win_p', 'dil1_p', 'dil2_p', 'dil3_p', 'cmp_s', 'sel_s', 'win_s', 'dil1_s', 'dil2_s', 'dil3_s', 'sgu_s')
    st = {nm: [] for nm in names}
    for l in range(DEPTH):
        cp = (cmp_pe[l], cmp_w1[l], cmp_b1[l], cmp_w2[l])
        sp = (sgu_ln_g[l], sgu_ln_b[l], sgu_w[l], sgu_b[l])
        op = (w_branch_a[l], w_branch_b[l], w_branch_c[l], w_out[l], norm_mlp_g[l], w_up[l], w_down[l])
        q_a, kv_a, g_a, qkv_b, u_c, v_c, g_m = project_inputs(rms_norm(xp, norm_mix_g[l]), w_in[l])
        o_a, cmp_p, sel_p, win_p = nsa_prompt(q_a, kv_a, g_a, *cp)
        o_b, dil_p = dilated_prompt(qkv_b)
        o_c, _ = sgu_mixer(u_c, v_c, *sp)
        xp = merge_and_ffn(xp, o_a, o_b, o_c, g_m, *op)
        q_a, kv_a, g_a, qkv_b, u_c, v_c, g_m = project_inputs(rms_norm(xs, norm_mix_g[l]), w_in[l])
        o_a, cmp_s, sel_s, win_s = nsa_sample(q_a, kv_a, g_a, cache_cmp_kv, cache_sel_kv, cache_win_kv[:, l], page_table, l, *cp)
        o_b, dil_s = dilated_sample(qkv_b, (cache_dil1_kv[:, l], cache_dil2_kv[:, l], cache_dil3_kv[:, l]))
        o_c, v_rows = sgu_mixer(u_c, v_c, *sp)
        xs = merge_and_ffn(xs, o_a, o_b, o_c, g_m, *op)
        for nm, val in (('cmp_p', cmp_p), ('sel_p', sel_p), ('win_p', win_p), ('dil1_p', dil_p[0]), ('dil2_p', dil_p[1]), ('dil3_p', dil_p[2]), ('cmp_s', cmp_s), ('sel_s', sel_s), ('win_s', win_s), ('dil1_s', dil_s[0]), ('dil2_s', dil_s[1]), ('dil3_s', dil_s[2]), ('sgu_s', v_rows[:, (v_rows.shape[1] // SGU_CHUNK) * SGU_CHUNK:])):
            st[nm].append(val)
    y_prompt = rms_norm(xp, norm_final_g)
    y_sample = rms_norm(xs, norm_final_g)
    new = {nm: jnp.stack(st[nm], axis=1) for nm in names}
    return (y_prompt, y_sample, new['cmp_p'], new['sel_p'], new['win_p'], new['dil1_p'], new['dil2_p'], new['dil3_p'], new['cmp_s'], new['sel_s'], new['win_s'], new['dil1_s'], new['dil2_s'], new['dil3_s'], new['sgu_s'])


_drawn_inputs = setup_inputs


def setup_inputs(seed=0):
    import zlib

    import numpy as np

    out = dict(_drawn_inputs(seed))
    spreads = {}
    factors = {'cache_cmp_kv': 3.035,
     'cache_sel_kv': 3.549,
     'cmp_pe': 3.947,
     'cmp_b1': 8.0,
     'sgu_ln_b': 2.807}
    for name, (base, spread) in spreads.items():
        noise = np.random.default_rng([zlib.crc32(name.encode()), seed]).standard_normal(out[name].shape)
        drawn = base * np.exp(spread * noise) if base else spread * noise
        out[name] = __import__('jax').numpy.asarray(drawn.astype(out[name].dtype))
    for name, factor in factors.items():
        out[name] = (out[name] * factor).astype(out[name].dtype)
    return out
```

```python
from contextlib import ExitStack

import numpy as np

import concourse.bass as bass
from concourse import mybir

F32 = mybir.dt.float32
I32 = mybir.dt.int32
ALU = mybir.AluOpType
ACT = mybir.ActivationFunctionType
AX = mybir.AxisListType

P = 128
D = 1024
KD = D // P
SEQ = 512
B = 8
S = 4
NS = B * S
NT = SEQ + NS
NI = SEQ // P
PAST = 4096
PAGE = 128
PAGES = PAST // PAGE
DH = 64
G = 2
R = 4
SCALE = DH ** -0.5
NC_P = SEQ // 16 - 1
NC_S = PAST // 16 - 1
NSEG = PAST // 16
JJ = 8
HID = 128
SELB = 64
NB = PAST // SELB + 1
FORCED = 1e4
FF = 4 * D
NEG = -1e30
TAKEN = -1e30
GELU_C = 0.7978845608028654
GELU_A = 0.044715
RMS_EPS = 1e-6
LN_EPS = 1e-5
RING = 9
UNIT = KD * P
DILK = 128 + 512 + 512
WINS = (128, 512, 2048)

C_ID = 0
C_ONE = C_ID + P
C_MC = C_ONE + P
C_M4 = C_MC + 512
C_M16 = C_M4 + 512
C_M1 = C_M16 + 512
C_CMP = C_M1 + 256
C_CMV = C_CMP + NI * 32
C_TRI = C_CMV + NI * 32
C_EPS = C_TRI + P
C_END = C_EPS + 2

R_WIN = 0
R_NEW = R_WIN + 512
R_IMP = R_NEW + 8
R_GRP = R_IMP + 32
R_SPR = R_GRP + P
R_DIL = R_SPR + 16
R_HEAD = R_DIL + DILK + 12
R_TOK = R_HEAD + 512
R_SGU = R_TOK + S
R_END = R_SGU + NS


def shape_constants():
    c = np.zeros((P, C_END), np.float32)
    p = np.arange(P)[:, None]
    c[:, C_ID:C_ID + P] = np.eye(P)
    c[:, C_ONE:C_ONE + P] = 1
    dist = p - (np.arange(512)[None, :] - 384)
    for at, d in ((C_MC, 1), (C_M4, 4), (C_M16, 16)):
        c[:, at:at + 512] = np.where((dist >= 0) & (dist % d == 0), 0, NEG)
    dist = p + 128 - np.arange(256)[None, :]
    c[:, C_M1:C_M1 + 256] = np.where((dist >= 0) & (dist <= 128), 0, NEG)
    for i in range(NI):
        ok = (np.arange(32)[None, :] * 16 + 31 <= i * P + p) & (np.arange(32)[None, :] < NC_P)
        c[:, C_CMP + 32 * i:C_CMP + 32 * i + 32] = np.where(ok, 0, NEG)
        c[:, C_CMV + 32 * i:C_CMV + 32 * i + 32] = ok
    c[:, C_TRI:C_TRI + P] = p <= np.arange(P)[None, :]
    c[:, C_EPS] = RMS_EPS
    c[:, C_EPS + 1] = LN_EPS
    r = np.zeros((NS, R_END), np.float32)
    q = np.arange(NS)
    g, s, rr = q // 16, (q // 4) % 4, q % 4
    r[:, R_WIN:R_WIN + 512] = np.where(np.arange(512)[None, :] >= s[:, None], 0, NEG)
    for k in range(2):
        r[:, R_NEW + 4 * k:R_NEW + 4 * k + 4] = np.where(np.arange(4)[None, :] <= s[:, None], 0, NEG)
    r[:, R_IMP:R_IMP + 32] = (q[:, None] // 4) == (q[None, :] // 4)
    r[:, R_GRP:R_GRP + P] = (np.arange(P)[None, :] // DH) == g[:, None]
    r[:, R_SPR:R_SPR + 16] = np.arange(16)[None, :] == (rr * 4 + s)[:, None]
    s, h = q // 8, q % 8
    m = np.full((NS, DILK + 12), NEG)
    m[:, 0:128] = np.where(np.arange(128)[None, :] >= s[:, None], 0, NEG)
    for k in range(2):
        for ss in range(S):
            m[s == ss, 128 + 512 * k + 128 * ss:128 + 512 * k + 128 * ss + 128] = 0
    for ss in range(S):
        m[:, DILK + ss] = np.where(ss <= s, 0, NEG)
        m[:, DILK + 4 + ss] = np.where(ss == s, 0, NEG)
        m[:, DILK + 8 + ss] = np.where(ss == s, 0, NEG)
    r[:, R_DIL:R_DIL + DILK + 12] = m
    r[:, R_HEAD:R_HEAD + 512] = (np.arange(512)[None, :] // DH) == h[:, None]
    r[:, R_TOK:R_TOK + S] = np.arange(S)[None, :] == s[:, None]
    b, s = q // S, q % S
    r[:, R_SGU:R_SGU + NS] = (b[:, None] == b[None, :]) & (s[:, None] <= s[None, :])
    return c, r


U_A = 0
U_U = U_A + 11
U_V = U_U + 4
U_DIL = U_V + 4
U_MIX = U_DIL + 36
U_OUT = U_MIX + 36
U_UP = U_OUT + 8
U_DN = U_UP + 32
N_UNITS = U_DN + 32


def weight_stream(w_in, w_a, w_b, w_c, w_out, w_up, w_down):
    w = np.zeros((N_UNITS, P, UNIT), np.float32)

    def cols(m, c):
        return m[:, c].reshape(-1, P, len(c)).transpose(1, 0, 2)

    def unit(u, m, c):
        w[u].reshape(P, KD, P)[:, :, :len(c)] = cols(m, c)
    d = np.arange(DH)
    for r in range(R):
        unit(U_A + r, w_in, np.concatenate([g * 256 + r * DH + d for g in range(G)]))
    for i in range(6):
        unit(U_A + 4 + i, w_in, 512 + P * i + np.arange(P))
    unit(U_A + 10, w_in, 1280 + np.arange(24))
    at = 1304 + 4608
    for i in range(4):
        unit(U_U + i, w_in, at + P * i + np.arange(P))
    v = cols(w_in, at + 512 + np.arange(512))
    for i in range(4):
        w[U_V + i] = v[:, 2 * i:2 * i + 2].reshape(P, UNIT)
    for p in range(4):
        for n in range(9):
            unit(U_DIL + 9 * p + n, w_in, 1304 + n * 512 + P * p + np.arange(P))
    at = 1304 + 4608 + 1024
    rows = np.concatenate([g * 256 + r * DH + d for r in range(R) for g in range(G)])
    br = [w_a[rows], w_b, w_c]
    for jp in range(4):
        for jj in range(2):
            j = 2 * jp + jj
            for i in range(3):
                unit(U_MIX + 9 * jp + 3 * jj + i, w_in, at + i * D + P * j + np.arange(P))
        t = [cols(br[i], P * (2 * jp + jj) + np.arange(P)) for jj in range(2) for i in range(3)]
        w[U_MIX + 9 * jp + 6:U_MIX + 9 * jp + 9] = (
            np.concatenate(t, 1).reshape(P, 3, UNIT).transpose(1, 0, 2))
    for j in range(8):
        unit(U_OUT + j, w_out, P * j + np.arange(P))
    for j in range(32):
        unit(U_UP + j, w_up, P * j + np.arange(P))
    for j in range(8):
        m = cols(w_down, P * j + np.arange(P))
        for q in range(4):
            w[U_DN + 4 * j + q] = m[:, 8 * q:8 * q + 8].reshape(P, UNIT)
    return w


def sample_caches(cmp, sel, win, dil):
    n = len(cmp)
    out = {
        "cmp_pages": cmp.reshape(n, 8, JJ, 2, 2, G, DH).transpose(0, 3, 6, 4, 5, 2, 1
                                                                  ).reshape(n, P, 256),
        "sel_pages": np.concatenate([sel[:, :, 0].reshape(n, PAGE, P).transpose(0, 2, 1),
                                     sel[:, :, 1].reshape(n, PAGE, P)], 2),
        "win_k": win[:, :, 0].reshape(B, 512, P).transpose(0, 2, 1),
        "win_v": win[:, :, 1].reshape(B, 4, P, P).transpose(0, 2, 1, 3),
    }
    k, v = [], []
    for c, dilation in zip(dil, (1, 4, 16)):
        r = min(dilation, S)
        rows = c.reshape(B, 128, dilation, 2, 512)[:, :, :r].transpose(0, 2, 1, 3, 4)
        k.append(rows[:, :, :, 0].reshape(B, r * 128, 4, P).transpose(0, 3, 2, 1))
        v.append(rows[:, :, :, 1].transpose(0, 2, 1, 3))
    out["dil_k"] = np.concatenate(k, 3)
    out["dil_v"] = np.concatenate(v, 2)
    return out


class Chain:

    def __init__(self, eng, sem):
        self.eng, self.sem, self.n, self.base, self.per = eng, sem, 0, 0, 0

    def link(self, ins):
        self.n += 1
        ins.then_inc(self.sem, 1)
        self.wait()

    def count(self, ins):
        self.n += 1
        ins.then_inc(self.sem, 1)

    def wait(self):
        at = self.base + self.n
        hold(self.eng, self.sem, at)

    def enter(self, turn, per):
        self.start, self.per, self.base = self.n, per, turn * per

    def leave(self, turns):
        got = self.n - self.start
        assert got == self.per, f"a turn of {self.sem} has {got} counts"
        self.n += self.per * (turns - 1)
        self.base = 0


MET = [None, 48]


def hold(eng, sem, value):
    if not isinstance(value, int):
        eng.wait_ge(*MET)
    eng.wait_ge(sem, value)


def trunk(nc, t):
    ctx = ExitStack()
    with ctx:
        def sb(name, shape, stack=ctx, dt=F32):
            return stack.enter_context(nc.sbuf_tensor(name, shape, dt))

        def sem(name):
            return ctx.enter_context(nc.semaphore(name))

        banks = [ctx.enter_context(nc.psum_tensor(f"bank{i}", [P, 512], F32)) for i in range(8)]
        con = sb("con", [P, C_END])
        row = sb("row", [NS, R_END])
        norm_g = sb("norm_g", [P, 3, KD])
        hT = sb("hT", [P, KD, NT])
        oaT = sb("oaT", [P, R, NT])
        obT = sb("obT", [P, 4, NT])
        ocT = sb("ocT", [P, 4, NT])
        qaS = sb("qaS", [P, R, NS])
        kvS = sb("kvS", [P, 6, NS])
        qkS = sb("qkS", [P, 4, 9, NS])
        bgate = sb("bgate", [NS, B, 3])
        ident = con[:, C_ID:C_ID + P]
        ones = con[:, C_ONE:C_ONE + P]

        names = ("const_landed x_landed g_landed sq_ready ss_ready std_ready h_ready w_used "
                 "dve_chain act_chain bulk_done out_done store_done".split())
        sm = {n: sem(n) for n in names}
        w_landed = [sem(f"w_landed{i}") for i in range(RING)]
        MET[0] = sm["const_landed"]

        def ring_slot(wr, u):
            return wr[:, u % RING, :]

        class Track:
            put = 0

        bulk = [("dil3", b) for b in range(B)] + [("dil2", b) for b in range(B)] \
            + [("dil1", b) for b in range(B)] + [("win", b) for b in range(B)]
        sent = {"n": 0}

        def bulk_copies(eng, n):
            for name, b in bulk[sent["n"]:sent["n"] + n]:
                src, dst = t["cache_" + name], t["new_" + name]
                w, c = src.shape[1], src.shape[2]
                n_el = (w - S) * c
                if sent["n"] and sent["n"] % 2 == 0:
                    eng.wait_ge(sm["bulk_done"], 16 * sent["n"])
                eng.dma_start(
                    dst[b, 0:w - S, :].rearrange("w c -> (w c)").rearrange("(a n) -> a n", a=16),
                    src[b, S:w, :].rearrange("w c -> (w c)").rearrange("(a n) -> a n", a=16),
                ).then_inc(sm["bulk_done"], 16)
                sent["n"] += 1

        def load_units(sp, wr, u0, n):
            for u in range(u0, u0 + n):
                if u >= RING:
                    sp.wait_ge(sm["w_used"], u - RING + 1)
                sp.dma_start(ring_slot(wr, u), t["w"][u]).then_inc(w_landed[u % RING], 16)

        def unit_landed(eng, u, turn=0, per=0):
            hold(eng, w_landed[u % RING], turn * (per // RING * 16) + 16 * (u // RING + 1))

        pc = ExitStack()
        w1 = sb("w1", [P, 2, 16, HID], pc)
        w2 = sb("w2", [HID, 2, DH], pc)
        pe_t = sb("pe_t", [P, 2, 16], pc)
        b1 = sb("b1", [HID, 2], pc)
        bias = sb("bias", [HID, 2], pc)
        p1 = ExitStack()
        p12 = ExitStack()
        wr = sb("wring", [P, RING, UNIT], p12)
        qaT = sb("qaT", [P, R, SEQ], p12)
        kvT = sb("kvT", [P, 6, SEQ], p12)
        v_nat = sb("v_nat", [P, 2, NI, P], p12)
        gate_n = sb("gate_n", [P, NI, 24], p12)
        xT = sb("xT", [P, KD, NT], p1)

        def sq(k):
            return oaT[:, k, :] if k < 4 else obT[:, k - 4, :]

        rstd = sb("rstd", [P, NT], p1)
        gate_t = sb("gate_t", [24, NT], p1)
        uT = sb("uT", [P, 4, NT], p1)
        vn = sb("vn", [P, NI + 1, 512], p1)
        tmp = sb("tmp", [P, NT], p1)
        tmp2 = sb("tmp2", [P, NT], p1)
        stat = sb("stat", [P, 4], p1)
        ln_gb = sb("ln_gb", [P, 2, 512], p1)
        wsT = sb("wsT", [P, 8, P], p1)
        ws4 = sb("ws4", [NS, 8, NS], p1)
        bs = sb("bs", [2, 4, P + NS], p1)
        half = sb("half", [2, P], p1)
        newn = sb("newn", [NS, 4, P], p1)

        s_t_read = sem("t_read")
        s_t_readS = sem("t_readS")
        s_tr_ready = sem("tr_ready")
        s_tr_read = sem("tr_read")
        s_gexp = sem("gate_tanh")
        s_gate = sem("gate_ready")
        s_vz = sem("v_bank_ready")
        s_vz_read = sem("v_bank_read")
        s_gel1 = sem("gelu_square")
        s_gel2 = sem("gelu_inner")
        s_gel3 = sem("gelu_tanh")
        s_ln = sem("ln_centred")
        s_lnv = sem("ln_variance")
        s_v_ready = sem("v_ready")
        s_ws = sem("spatial_weights_ready")
        s_mix = sem("mixed_ready")
        s_mix_read = sem("mixed_read")
        s_rows = sem("gate_rows_landed")
        s_scr = sem("scratch_written")
        s_sgl = sem("sgu_landed")
        s_stat = sem("rows_written")

        def rms_act(act, ch, src, sqb, n, rstd):
            for k in range(KD):
                act.activation(sqb(k), src[:, k, :], ACT.Square).then_inc(sm["sq_ready"], 1)
            act.wait_ge(sm["ss_ready"], n + 1)
            act.activation(rstd[:, 0:SEQ], banks[0][:, :], ACT.Sqrt, scale=1.0 / D,
                           bias=con[:, C_EPS:C_EPS + 1])
            act.activation(rstd[:, SEQ:NT], banks[1][:, 0:NS], ACT.Sqrt, scale=1.0 / D,
                           bias=con[:, C_EPS:C_EPS + 1]).then_inc(sm["std_ready"], 1)

        def rms_pe(pe, sqb, n):
            for k in range(KD):
                pe.wait_ge(sm["sq_ready"], KD * n + k + 1)
                pe.matmul(banks[0][:, :], ones, sqb(k)[:, 0:SEQ], start=(k == 0), stop=(k == KD - 1))
                last = pe.matmul(banks[1][:, 0:NS], ones, sqb(k)[:, SEQ:NT], start=(k == 0),
                                 stop=(k == KD - 1))
            last.then_inc(sm["ss_ready"], 1)

        def rms_dve(dve, ch, src, dst, n, rstd):
            dve.wait_ge(sm["std_ready"], n + 1)
            ch.link(dve.reciprocal(rstd[:, :], rstd[:, :]))
            for k in range(KD):
                dve.scalar_tensor_tensor(out=dst[:, k, :], in0=src[:, k, :],
                                         scalar=norm_g[:, n, k:k + 1], in1=rstd[:, :],
                                         op0=ALU.mult, op1=ALU.mult).then_inc(sm["h_ready"], 1)

        def t_tile(pe, wr, u, n, turn=0, per=0, m=P, rhs=None, banksP=(0, 1)):
            rhs = hT if rhs is None else rhs
            unit_landed(pe, u, turn, per)
            w = ring_slot(wr, u)
            for k in range(KD):
                pe.matmul(banks[banksP[n % 2]][0:m, :], w[:, k * P:k * P + m], rhs[:, k, 0:SEQ],
                          start=(k == 0), stop=(k == KD - 1))
            for k in range(KD):
                last = pe.matmul(banks[2 + n % 2][0:m, 0:NS], w[:, k * P:k * P + m],
                                 rhs[:, k, SEQ:NT], start=(k == 0), stop=(k == KD - 1))
            return last

        with nc.Block() as block:
            @block.sync
            def _(sp):
                for k in range(KD):
                    sp.dma_start(xT[:, k, :], t["xT"][:, k, :]).then_inc(sm["x_landed"], 16)
                sp.dma_start(con[:, :], t["con"]).then_inc(sm["const_landed"], 16)
                sp.dma_start(row[:, :], t["row"]).then_inc(sm["const_landed"], 16)
                sp.dma_start(norm_g[:, :, :], t["norm_g"]).then_inc(sm["const_landed"], 16)
                load_units(sp, wr, 0, 4)
                sp.dma_start(ln_gb[:, 0, :], t["ln_g"].to_broadcast([P, 512])
                             ).then_inc(s_sgl, 16)
                sp.dma_start(ln_gb[:, 1, :], t["ln_b"].to_broadcast([P, 512])
                             ).then_inc(s_sgl, 16)
                sp.dma_start(wsT[:, :, :], t["wsT"]).then_inc(s_sgl, 16)
                sp.dma_start(ws4[:, :, :], t["ws4"]).then_inc(s_sgl, 16)
                sp.dma_start(bs[:, :, :], t["bs"]).then_inc(s_sgl, 16)
                sp.dma_start(half[:, :], t["half"]).then_inc(s_sgl, 16)
                load_units(sp, wr, 4, U_DIL - 4)
                sp.wait_ge(s_t_read, 10)
                sp.dma_start(t["kvT"], kvT[:, :, :]).then_inc(sm["out_done"], 16)
                sp.wait_ge(s_t_readS, 10)
                sp.dma_start(t["kvS"], kvS[:, :, :]).then_inc(sm["out_done"], 16)
                sp.wait_ge(s_gate, 1)
                sp.dma_start(t["scr_gate"], gate_t[:, SEQ:NT]).then_inc(s_scr, 16)
                sp.wait_ge(s_tr_read, 3)
                sp.dma_start(t["scr_v"], newn[:, 0:2, :]).then_inc(s_scr, 16)
                for i in range(2):
                    for b in range(B):
                        sp.dma_start(t["new_win"][b, 512 - S:512, P * i:P * i + P],
                                     newn[S * b:S * b + S, 2 + i, :]).then_inc(sm["store_done"], 16)
                sp.wait_ge(s_scr, 32)
                for g in range(G):
                    for s in range(S):
                        for b3 in range(3):
                            src = t["scr_gate"].rearrange("(g r c) (b s) -> g c s r b", g=G, r=R, s=S)
                            sp.dma_start(
                                bgate[g * 16 + s * 4:g * 16 + s * 4 + 4, :, b3:b3 + 1],
                                src[g, b3, s].rearrange("r (b o) -> r b o", o=1),
                                allow_slow_non_contiguous=True).then_inc(s_rows, 16)
                sp.wait_ge(s_v_ready, NI + 1)
                sp.dma_start(t["sgu_v"], vn[0:NS, NI, :]).then_inc(sm["out_done"], 16)
                sp.wait_ge(s_rows, 16 * 24)

            @block.gpsimd
            def _(pool):
                bulk_copies(pool, 4)

            @block.scalar
            def _(act):
                ch = Chain(act, sm["act_chain"])
                act.wait_ge(sm["x_landed"], 16 * KD)
                act.wait_ge(sm["const_landed"], 48)
                rms_act(act, ch, xT, sq, 0, rstd)
                for n in range(10):
                    act.wait_ge(sm["w_used"], n + 1)
                    dst = qaT[:, n, :] if n < 4 else kvT[:, n - 4, :]
                    act.activation(dst, banks[n % 2][:, :], ACT.Copy).then_inc(s_t_read, 1)
                act.wait_ge(sm["w_used"], 11)
                act.activation(gate_t[:, 0:SEQ], banks[0][0:24, :], ACT.Tanh, scale=0.5)
                act.activation(gate_t[:, SEQ:NT], banks[2][0:24, 0:NS], ACT.Tanh,
                               scale=0.5).then_inc(s_t_read, 1)
                for n in range(4):
                    act.wait_ge(sm["w_used"], 12 + n)
                    if n:
                        act.wait_ge(s_gate, 1 + n)
                    bP, bS = banks[(11 + n) % 2], banks[2 + (11 + n) % 2]
                    act.activation(uT[:, n, 0:SEQ], bP[:, :], ACT.Copy)
                    act.activation(uT[:, n, SEQ:NT], bS[:, 0:NS], ACT.Copy)
                    act.activation(tmp[:, 0:SEQ], bP[:, :], ACT.Square)
                    act.activation(tmp[:, SEQ:NT], bS[:, 0:NS], ACT.Square).then_inc(s_t_read, 1)
                    act.wait_ge(s_gel2, n + 1)
                    act.activation(tmp2[:, :], tmp2[:, :], ACT.Tanh, scale=GELU_C).then_inc(s_gel3, 1)
                for i in range(NI + 1):
                    m = P if i < NI else NS
                    act.wait_ge(s_vz, i + 1)
                    act.wait_ge(s_gate, 5)
                    if i:
                        act.wait_ge(s_v_ready, i)
                    act.activation(vn[0:m, i, :], banks[4 + i % 2][0:m, :], ACT.Copy)
                    act.activation(tmp[0:m, 0:512], banks[4 + i % 2][0:m, :],
                                   ACT.Square).then_inc(s_vz_read, 1)
                    act.wait_ge(s_gel2, 5 + i)
                    act.activation(tmp2[0:m, 0:512], tmp2[0:m, 0:512], ACT.Tanh,
                                   scale=GELU_C).then_inc(s_gel3, 1)
                    act.wait_ge(s_ln, i + 1)
                    ch.link(act.activation(tmp[0:m, 0:512], vn[0:m, i, :], ACT.Square,
                                           accum_out=stat[0:m, 1:2]))
                    act.activation(stat[0:m, 2:3], stat[0:m, 1:2], ACT.Sqrt, scale=1.0 / 512,
                                   bias=con[0:m, C_EPS + 1:C_EPS + 2]).then_inc(s_lnv, 1)

            @block.vector
            def _(dve):
                ch = Chain(dve, sm["dve_chain"])
                dve.wait_ge(sm["const_landed"], 48)
                dve.wait_ge(sm["x_landed"], 16 * KD)
                rms_dve(dve, ch, xT, hT, 0, rstd)
                for n in range(10):
                    dve.wait_ge(sm["w_used"], n + 1)
                    dst = qaS[:, n, :] if n < 4 else kvS[:, n - 4, :]
                    dve.tensor_copy(dst, banks[2 + n % 2][:, 0:NS]).then_inc(s_t_readS, 1)
                dve.wait_ge(s_t_read, 11)
                dve.tensor_scalar(gate_t[:, :], gate_t[:, :], 0.5, 0.5, ALU.mult,
                                  ALU.add).then_inc(s_gate, 1)
                dve.wait_ge(s_sgl, 16 * 6)
                for h in range(8):
                    dve.tensor_tensor(wsT[:, h, :], wsT[:, h, :], con[:, C_TRI:C_TRI + P], ALU.mult)
                    last = dve.tensor_tensor(ws4[:, h, :], ws4[:, h, :], row[:, R_SGU:R_SGU + NS],
                                             ALU.mult)
                last.then_inc(s_ws, 1)
                dve.wait_ge(s_tr_ready, 1)
                for j in range(2):
                    dve.tensor_copy(v_nat[:, j, :, :].rearrange("p i d -> p (i d)"),
                                    banks[6 + j][:, :]).then_inc(s_tr_read, 1)
                dve.wait_ge(s_tr_ready, 2)
                dve.tensor_copy(newn[:, :, :].rearrange("p i d -> p (i d)"),
                                banks[6][0:NS, :]).then_inc(s_tr_read, 1)
                dve.tensor_copy(gate_n[:, :, :], banks[7][:, 0:NI * 24].rearrange(
                    "p (i c) -> p i c", i=NI)).then_inc(s_tr_read, 1)

                def inner(x, m, w):
                    ch.link(dve.tensor_scalar(tmp2[0:m, 0:w], tmp[0:m, 0:w], GELU_A, 1.0, ALU.mult,
                                              ALU.add))
                    dve.tensor_tensor(tmp2[0:m, 0:w], tmp2[0:m, 0:w], x, ALU.mult).then_inc(s_gel2, 1)

                def outer(x, m, w):
                    return dve.scalar_tensor_tensor(out=x, in0=tmp2[0:m, 0:w], scalar=1.0, in1=x,
                                                    op0=ALU.add, op1=ALU.mult)

                for n in range(4):
                    dve.wait_ge(s_t_read, 12 + n)
                    inner(uT[:, n, :], P, NT)
                    dve.wait_ge(s_gel3, n + 1)
                    outer(uT[:, n, :], P, NT).then_inc(s_gate, 1)
                for i in range(NI + 1):
                    m = P if i < NI else NS
                    v = vn[0:m, i, :]
                    dve.wait_ge(s_vz_read, i + 1)
                    inner(v, m, 512)
                    dve.wait_ge(s_gel3, 5 + i)
                    ch.link(outer(v, m, 512))
                    ch.link(dve.tensor_scalar(v, v, 0.5, None, ALU.mult))
                    ch.link(dve.tensor_reduce(stat[0:m, 0:1], v, AX.X, ALU.add))
                    ch.link(dve.tensor_scalar(stat[0:m, 0:1], stat[0:m, 0:1], 1.0 / 512, None,
                                              ALU.mult))
                    dve.tensor_scalar(v, v, stat[0:m, 0:1], None, ALU.subtract).then_inc(s_ln, 1)
                    dve.wait_ge(s_lnv, i + 1)
                    ch.link(dve.reciprocal(stat[0:m, 3:4], stat[0:m, 2:3]))
                    ch.link(dve.scalar_tensor_tensor(out=v, in0=v, scalar=stat[0:m, 3:4],
                                                     in1=ln_gb[0:m, 0, :], op0=ALU.mult,
                                                     op1=ALU.mult))
                    dve.tensor_tensor(v, v, ln_gb[0:m, 1, :], ALU.add).then_inc(s_v_ready, 1)
                for n in range(4):
                    dve.wait_ge(s_mix, n + 1)
                    dve.scalar_tensor_tensor(out=ocT[:, n, 0:SEQ], in0=banks[n % 2][:, :], scalar=0.5,
                                             in1=uT[:, n, 0:SEQ], op0=ALU.mult, op1=ALU.mult)
                    dve.scalar_tensor_tensor(out=ocT[:, n, SEQ:NT], in0=banks[2 + n % 2][:, 0:NS],
                                             scalar=0.5, in1=uT[:, n, SEQ:NT], op0=ALU.mult,
                                             op1=ALU.mult).then_inc(s_mix_read, 1)

            @block.tensor
            def _(pe):
                pe.wait_ge(sm["const_landed"], 48)
                rms_pe(pe, sq, 0)
                pe.wait_ge(sm["h_ready"], KD)
                for n in range(15):
                    if n >= 2:
                        pe.wait_ge(s_t_read, n - 1)
                        pe.wait_ge(s_t_readS, min(n - 1, 10))
                    m = 24 if n == 10 else P
                    last = t_tile(pe, wr, n, n, m=m)
                    last.then_inc(sm["w_used"], 1)
                    if n == 11:
                        pe.wait_ge(s_t_read, 10)
                        for j, kv in enumerate((3, 5)):
                            for i in range(NI):
                                last = pe.transpose(banks[6 + j][:, i * P:i * P + P],
                                                    kvT[:, kv, i * P:i * P + P], ident)
                        last.then_inc(s_tr_ready, 1)
                        pe.wait_ge(s_tr_read, 2)
                        for j, kv in enumerate((3, 5, 4, 5)):
                            pe.transpose(banks[6][0:NS, j * P:j * P + P], kvS[:, kv, :], ident)
                        pe.wait_ge(s_gate, 1)
                        for i in range(NI):
                            last = pe.transpose(banks[7][:, i * 24:i * 24 + 24],
                                                gate_t[:, i * P:i * P + P], ident[0:24, 0:24])
                        last.then_inc(s_tr_ready, 1)
                for i in range(NI + 1):
                    m = P if i < NI else NS
                    if i >= 2:
                        pe.wait_ge(s_vz_read, i - 1)
                    for k in range(KD):
                        if i == 0 and k % 2 == 0:
                            unit_landed(pe, U_V + k // 2)
                        w = ring_slot(wr, U_V + k // 2)
                        last = pe.matmul(banks[4 + i % 2][0:m, :], hT[:, k, i * P:i * P + m],
                                         w[:, (k % 2) * 512:(k % 2) * 512 + 512],
                                         start=(k == 0), stop=(k == KD - 1))
                        if i == NI and k % 2 and k < KD - 1:
                            last.then_inc(sm["w_used"], 1)
                    last.then_inc(s_vz, 1)
                pe.wait_ge(s_ws, 1)
                pe.wait_ge(s_v_ready, NI + 1)
                for n in range(4):
                    if n >= 2:
                        pe.wait_ge(s_mix_read, n - 1)
                    else:
                        pe.wait_ge(s_t_read, 15)
                    bP, bS = banks[n % 2], banks[2 + n % 2]
                    for c in range(NI + 1):
                        m = P if c < NI else NS
                        dst = bP[:, c * P:c * P + P] if c < NI else bS[:, 0:NS]
                        bb = bs[:, n, 0:P] if c < NI else bs[:, n, P:P + NS]
                        mm = pe.matmul(dst, half[:, :], bb, start=True, stop=False)
                        if n == 0 and c == 0:
                            mm.then_inc(sm["w_used"], 1)
                        for hh in range(2):
                            h = 2 * n + hh
                            w = wsT[:, h, :] if c < NI else ws4[:, h, :]
                            last = pe.matmul(dst[hh * DH:hh * DH + DH, :],
                                             vn[0:m, c, h * DH:h * DH + DH], w, start=False,
                                             stop=True)
                    last.then_inc(s_mix, 1)
        p1.close()
        s_cw = sem("cmp_weights_landed")
        s_bias = sem("cmp_bias_summed")
        s_bias2 = sem("cmp_bias_ready")
        s_cx = sem("cmp_rows_ready")
        s_hid = sem("cmp_hidden_summed")
        s_c1 = sem("cmp_first_half")
        s_c2 = sem("cmp_joined")
        s_c3 = sem("cmp_square")
        s_c4 = sem("cmp_inner")
        s_c5 = sem("cmp_tanh")
        s_c6 = sem("cmp_gelu")
        s_ck = sem("cmp_kv_summed")
        s_ckr = sem("cmp_kv_ready")

        def compress_pe(pe, cx, nseg, kc_bank, vc_bank, hidT, turn=0, base=0):
            for kv in range(2):
                for hf in range(2):
                    for jj in range(JJ):
                        last = pe.matmul(
                            banks[2 * kv + hf][:, 0:G * nseg].rearrange("p (g a s) -> p g a s", g=G, s=8),
                            w1[:, kv, 8 * hf + jj, :],
                            cx[:, :, 2 * kv:2 * kv + 2, jj, :].rearrange("p a g s -> p g a s"),
                            start=(jj == 0), stop=(jj == JJ - 1))
                last.then_inc(s_hid, 1)
            hold(pe, s_c6, turn * 2 + base + 2)
            n = nseg - 1
            for g in range(G):
                pe.matmul(kc_bank[g * DH:g * DH + DH, 0:n], w2[:, 0, :], hidT[:, 0, g, 0:n],
                          start=True, stop=True)
            for c in range(-(-n // P)):
                m = min(P, n - c * P)
                for g in range(G):
                    last = pe.matmul(vc_bank[0:m, c * P + g * DH:c * P + g * DH + DH],
                                     hidT[:, 1, g, c * P:c * P + m], w2[:, 1, :], start=True, stop=True)
            last.then_inc(s_ck, 1)

        def compress_act(act, nseg, hidT, sqT, inT, turn=0, base=0):
            for kv in range(2):
                hold(act, s_hid, turn * 2 + base + kv + 1)
                act.activation(hidT[:, kv, :, 0:nseg],
                               banks[2 * kv][:, 0:G * nseg].rearrange("p (g s) -> p g s", g=G),
                               ACT.Identity, bias=bias[:, kv:kv + 1]).then_inc(s_c1, 1)
                hold(act, s_c2, turn * 2 + base + kv + 1)
                act.activation(sqT[:, kv, :, 0:nseg - 1], hidT[:, kv, :, 0:nseg - 1],
                               ACT.Square).then_inc(s_c3, 1)
            for kv in range(2):
                hold(act, s_c4, turn * 2 + base + kv + 1)
                act.activation(inT[:, kv, :, 0:nseg - 1], inT[:, kv, :, 0:nseg - 1], ACT.Tanh,
                               scale=GELU_C).then_inc(s_c5, 1)

        def compress_dve(dve, ch, nseg, hidT, sqT, inT, turn=0, base=0):
            n = nseg - 1
            for kv in range(2):
                hold(dve, s_c1, turn * 2 + base + kv + 1)
                h = hidT[:, kv, :, 0:n]
                dve.tensor_tensor(h, h, banks[2 * kv + 1][:, 0:G * nseg].rearrange(
                    "p (g s) -> p g s", g=G)[:, :, 1:nseg], ALU.add).then_inc(s_c2, 1)
            for kv in range(2):
                h, q, i = hidT[:, kv, :, 0:n], sqT[:, kv, :, 0:n], inT[:, kv, :, 0:n]
                hold(dve, s_c3, turn * 2 + base + kv + 1)
                ch.link(dve.tensor_scalar(q, q, GELU_A, 1.0, ALU.mult, ALU.add))
                dve.tensor_tensor(i, q, h, ALU.mult).then_inc(s_c4, 1)
            for kv in range(2):
                h, i = hidT[:, kv, :, 0:n], inT[:, kv, :, 0:n]
                hold(dve, s_c5, turn * 2 + base + kv + 1)
                dve.scalar_tensor_tensor(out=h, in0=i, scalar=1.0, in1=h, op0=ALU.add,
                                         op1=ALU.mult).then_inc(s_c6, 1)

        s_sc = sem("scores_ready")
        s_sread = sem("scores_read")
        s_mx = sem("maxima_ready")
        s_exp = sem("exp_ready")
        s_prob = sem("probs_ready")
        s_tp = sem("probsT_bank_ready")
        s_ptc = sem("probsT_ready")
        s_pv = sem("block_summed")
        s_att = sem("turn_finished")
        NBLK = 2 * NI
        BLOCKS = [(hh, i) for hh in range(2) for i in range(NI)]

        def att_pe(pe, turn, base, q, kA, kB, kC, vA, vB, vC, widths):
            hold(pe, s_att, turn + base // NBLK + 1)

            def at(k):
                return turn * NBLK + base + k

            def scores(n):
                hh, i = BLOCKS[n]
                r0 = hh * DH
                if n >= 2:
                    hold(pe, s_sread, at(n - 1))
                w, wc = widths(i)
                lhs = [x[r0:r0 + DH, i * P:i * P + P] for x in q]
                pe.matmul(banks[n % 2][:, 0:w], lhs[0], kA[r0:r0 + DH, 0:w], start=True, stop=True)
                pe.matmul(banks[2 + n % 2][:, 0:w], lhs[1], kB[r0:r0 + DH, 0:w], start=True, stop=True)
                if n:
                    hold(pe, s_sread, at(n))
                pe.matmul(banks[4][:, 0:wc], lhs[2], kC(r0, i),
                          start=True, stop=True).then_inc(s_sc, 1)

            def flip(n):
                hh, i = BLOCKS[n]
                w, wc = widths(i)
                T, offB, offC = att_T[n % 2], *offs(w)
                hold(pe, s_prob, at(n + 1))
                if n >= 1:
                    hold(pe, s_ptc, (turn * NBLK + base) * 3 + 3 * n)
                for bank, off in ((5, 0), (6, offB)):
                    for kt in range(i + 1):
                        last = pe.transpose(banks[bank][:, kt * P:kt * P + P],
                                            T[:, off + kt * P:off + kt * P + P], ident)
                    last.then_inc(s_tp, 1)
                hold(pe, s_ptc, (turn * NBLK + base) * 3 + 3 * n + 1)
                for c in range(-(-wc // P)):
                    m = min(P, wc)
                    last = pe.transpose(banks[5][0:m, c * P:c * P + P],
                                        T[:, offC + c * P:offC + c * P + m], ident)
                last.then_inc(s_tp, 1)

            def values(n):
                hh, i = BLOCKS[n]
                w, wc = widths(i)
                hold(pe, s_ptc, (turn * NBLK + base) * 3 + 3 * n + 3)
                pT = att_pT[n % 2]
                o = banks[7][hh * DH:hh * DH + DH, i * P:i * P + P]
                for kt in range(i + 1):
                    pe.matmul(o, vA(hh, kt), pT[:, kt * P:kt * P + P], start=(kt == 0), stop=False)
                for kt in range(i + 1):
                    pe.matmul(o, vB(hh, kt), pT[:, 512 + kt * P:512 + kt * P + P], start=False,
                              stop=False)
                nC = -(-wc // P)
                for c in range(nC):
                    m = min(P, wc)
                    last = pe.matmul(o, vC(hh, i, c), pT[0:m, 1024 + c * P:1024 + c * P + P],
                                     start=False, stop=(c == nC - 1))
                last.then_inc(s_pv, 1)

            scores(0)
            scores(1)
            for n in range(NBLK):
                flip(n)
                if n:
                    values(n - 1)
                if n + 2 < NBLK:
                    scores(n + 2)
            values(NBLK - 1)

        def att_act(act, turn, base, widths, nsa, dst):
            def at(k):
                return turn * NBLK + base + k

            def exps(n):
                hh, i = BLOCKS[n]
                w, wc = widths(i)
                T, offB, offC = att_T[n % 2], *offs(w)
                hold(act, s_mx, at(n + 1))
                if nsa:
                    for k, (o, ww) in enumerate(((offC, wc), (0, w), (offB, w))):
                        last = act.activation(T[:, o:o + ww], T[:, o:o + ww], ACT.Exp, scale=SCALE,
                                              bias=att_m[:, n % 2, k:k + 1],
                                              accum_out=att_d[:, n % 2, k:k + 1])
                else:
                    last = act.activation(T[:, 0:offC + wc], T[:, 0:offC + wc], ACT.Exp, scale=SCALE,
                                          bias=att_m[:, n % 2, 0:1], accum_out=att_d[:, n % 2, 0:1])
                last.then_inc(s_exp, 1)

            def copies(n):
                hh, i = BLOCKS[n]
                w, wc = widths(i)
                pT = att_pT[n % 2]
                if n >= 2:
                    hold(act, s_pv, at(n - 1))
                t0 = (turn * NBLK + base) * 3 + 3 * n
                for k in range(2):
                    hold(act, s_tp, t0 + k + 1)
                    act.activation(pT[:, 512 * k:512 * k + w], banks[5 + k][:, 0:w],
                                   ACT.Copy).then_inc(s_ptc, 1)
                hold(act, s_tp, t0 + 3)
                m, nC = min(P, wc), -(-wc // P)
                act.activation(pT[0:m, 1024:1024 + nC * P], banks[5][0:m, 0:nC * P],
                               ACT.Copy).then_inc(s_ptc, 1)

            exps(0)
            for n in range(NBLK):
                if n + 1 < NBLK:
                    exps(n + 1)
                copies(n)
            hold(act, s_pv, at(NBLK))
            act.activation(dst, banks[7][:, :], ACT.Copy).then_inc(s_att, 1)

        def att_dve(dve, ch, turn, base, widths, nsa, masks, gate=None):
            def at(k):
                return turn * NBLK + base + k

            def mask(n):
                hh, i = BLOCKS[n]
                w, wc = widths(i)
                T, offB, offC = att_T[n % 2], *offs(w)
                hold(dve, s_sc, at(n + 1))
                if n >= 2:
                    hold(dve, s_tp, (turn * NBLK + base) * 3 + 3 * (n - 1))
                mA, mB, mC = masks(i)
                ch.count(dve.tensor_tensor(T[:, 0:w], banks[n % 2][:, 0:w], mA, ALU.add))
                ch.count(dve.tensor_tensor(T[:, offB:offB + w], banks[2 + n % 2][:, 0:w], mB, ALU.add))
                dve.tensor_tensor(T[:, offC:offC + wc], banks[4][:, 0:wc], mC,
                                  ALU.add).then_inc(s_sread, 1)
                hold(dve, s_sread, at(n + 1))
                m = att_m[:, n % 2, :]
                if nsa:
                    ch.count(dve.tensor_reduce(m[:, 0:1], T[:, offC:offC + wc], AX.X, ALU.max))
                    ch.count(dve.tensor_reduce(m[:, 1:2], T[:, 0:w], AX.X, ALU.max))
                    ch.link(dve.tensor_reduce(m[:, 2:3], T[:, offB:offB + w], AX.X, ALU.max))
                else:
                    ch.link(dve.tensor_reduce(m[:, 0:1], T[:, 0:offC + wc], AX.X, ALU.max))
                k = 3 if nsa else 1
                dve.tensor_scalar(m[:, 0:k], m[:, 0:k], -SCALE, None, ALU.mult).then_inc(s_mx, 1)

            def norm(n):
                hh, i = BLOCKS[n]
                w, wc = widths(i)
                T, offB, offC = att_T[n % 2], *offs(w)
                d = att_d[:, n % 2, :]
                hold(dve, s_exp, at(n + 1))
                if not nsa:
                    ch.link(dve.reciprocal(d[:, 0:1], d[:, 0:1]))
                    dve.tensor_scalar(T[:, 0:offC + wc], T[:, 0:offC + wc], d[:, 0:1], None,
                                      ALU.mult).then_inc(s_prob, 1)
                    return
                ok = con[:, C_CMV + 32 * i:C_CMV + 32 * i + wc]
                ch.link(dve.tensor_tensor(T[:, offC:offC + wc], T[:, offC:offC + wc], ok, ALU.mult))
                ch.link(dve.tensor_reduce(d[:, 0:1], T[:, offC:offC + wc], AX.X, ALU.add))
                ch.link(dve.tensor_scalar(d[:, 0:1], d[:, 0:1], 1e-30, None, ALU.max))
                ch.link(dve.reciprocal(d[:, 0:3], d[:, 0:3]))
                ch.link(dve.tensor_tensor(d[:, 0:3], d[:, 0:3], gate(hh, i), ALU.mult))
                for k, (o, ww) in enumerate(((offC, wc), (0, w), (offB, w))):
                    last = dve.tensor_scalar(T[:, o:o + ww], T[:, o:o + ww], d[:, k:k + 1], None,
                                             ALU.mult)
                    if k < 2:
                        ch.count(last)
                last.then_inc(s_prob, 1)

            mask(0)
            mask(1)
            for n in range(NBLK):
                norm(n)
                if n + 2 < NBLK:
                    mask(n + 2)

        def offs(w):
            return w, 2 * w

        p2 = ExitStack()
        att_T = [sb(f"att_T{i}", [P, 1280], p2) for i in range(2)]
        att_pT = [sb(f"att_pT{i}", [P, 1280], p2) for i in range(2)]
        att_m = sb("att_m", [P, 2, 3], p2)
        att_d = sb("att_d", [P, 2, 3], p2)
        cxp = sb("cxp", [P, SEQ // P, 4, JJ, 8], p2)
        nsegp = SEQ // 16
        hidp = sb("hidp", [HID, 2, G, nsegp], p2)
        sqp = sb("sqp", [HID, 2, G, nsegp], p2)
        inp = sb("inp", [HID, 2, G, nsegp], p2)
        kcP = sb("kcP", [P, NC_P], p2)
        vcP = sb("vcP", [NC_P, P], p2)
        qslot = sb("qslot", [P, SEQ], p2)
        s_q = sem("q_slot_ready")

        def nsa_widths(i):
            return P * (i + 1), NC_P

        with nc.Block() as block:
            @block.sync
            def _(sp):
                sp.dma_start(w1[:, :, :, :], t["w1"]).then_inc(s_cw, 16)
                sp.dma_start(w2[:, :, :], t["w2"]).then_inc(s_cw, 16)
                sp.dma_start(pe_t[:, :, :], t["pe_t"]).then_inc(s_cw, 16)
                sp.dma_start(b1[:, :], t["b1"]).then_inc(s_cw, 16)
                load_units(sp, wr, U_DIL, RING)

            @block.gpsimd
            def _(pool):
                bulk_copies(pool, 4)

            @block.scalar
            def _(act):
                act.sem_inc(s_att, 1)
                compress_act(act, nsegp, hidp, sqp, inp)
                act.wait_ge(s_ck, 1)
                act.activation(kcP[:, :], banks[4][:, 0:NC_P], ACT.Copy, scale=0.5)
                act.activation(vcP[:, :], banks[5][0:NC_P, 0:P], ACT.Copy, scale=0.5).then_inc(s_ckr, 1)
                with act.Fori(0, R) as r:
                    hold(act, s_att, r + 1)
                    act.activation(qslot[:, :], qaT[:, bass.ds(r, 1), :].rearrange("p o q -> p (o q)"),
                                   ACT.Copy).then_inc(s_q, 1)
                    att_act(act, r, 0, nsa_widths, True,
                            oaT[:, bass.ds(r, 1), 0:SEQ].rearrange("p o q -> p (o q)"))

            @block.vector
            def _(dve):
                ch = Chain(dve, sem("dve_chain2"))
                for kv in range(2):
                    for g in range(G):
                        for j2 in range(2):
                            src = kvT[g * DH:g * DH + DH, kv, :].rearrange(
                                "p (a s j t) -> p t a j s", a=SEQ // P, s=8, t=2)[:, j2]
                            last = dve.tensor_copy(cxp[j2 * DH:j2 * DH + DH, :, 2 * kv + g, :, :], src)
                last.then_inc(s_cx, 1)
                dve.wait_ge(s_bias, 1)
                dve.wait_ge(s_cw, 64)
                ch.link(dve.tensor_tensor(bias[:, :], banks[7][:, 0:2], b1[:, :], ALU.add))
                dve.sem_inc(s_bias2, 1)
                compress_dve(dve, ch, nsegp, hidp, sqp, inp)
                with dve.Fori(0, R) as r:
                    ch.enter(r, 96)
                    att_dve(dve, ch, r, 0, nsa_widths, True,
                            lambda i: (con[:, C_MC + 384 - P * i:C_MC + 512],
                                       con[:, C_MC + 384 - P * i:C_MC + 512],
                                       con[:, C_CMP + 32 * i:C_CMP + 32 * i + NC_P]),
                            gate=lambda g, i: gate_n[:, i, bass.ds(r * 3 + g * 12, 3)])
                ch.leave(R)

            @block.tensor
            def _(pe):
                pe.wait_ge(s_cw, 64)
                for kv in range(2):
                    for j in range(16):
                        last = pe.matmul(banks[7][:, kv:kv + 1], w1[:, kv, j, :], pe_t[:, kv, j:j + 1],
                                         start=(j == 0), stop=(j == 15))
                last.then_inc(s_bias, 1)
                pe.wait_ge(s_cx, 1)
                pe.wait_ge(s_bias2, 1)
                compress_pe(pe, cxp, nsegp, banks[4], banks[5], hidp)
                pe.wait_ge(s_ckr, 1)
                with pe.Fori(0, R) as r:
                    hold(pe, s_q, r + 1)
                    att_pe(pe, r, 0, (qslot,) * 3, kvT[:, 2, :], kvT[:, 4, :],
                           lambda r0, i: kcP[r0:r0 + DH, :],
                           lambda g, kt: v_nat[:, 0, kt, g * DH:g * DH + DH],
                           lambda g, kt: v_nat[:, 1, kt, g * DH:g * DH + DH],
                           lambda g, i, c: vcP[:, g * DH:g * DH + DH], nsa_widths)

        p3 = ExitStack()
        dq = sb("dq", [P, 9, SEQ], p3)
        dqS = sb("dqS", [P, 9, NS], p3)
        dv = sb("dv", [P, 3, SEQ], p3)
        newd = sb("newd", [NS, 6, P], p3)
        s_dr = sem("dil_tile_copied")
        s_drS = sem("dil_sample_copied")
        s_dtr = sem("dil_transposes_ready")
        s_dtc = sem("dil_transposes_copied")
        s_dout = sem("dil_outputs_landed")
        OUTS_PER_TURN = 16 * (1 + 6)

        def dil_widths(i):
            return P * (i + 1), P * min(2, i + 1)

        with nc.Block() as block:
            @block.sync
            def _(sp):
                def turn_io(p, more):
                    if more:
                        for n in range(RING):
                            hold(sp, sm["w_used"], p * 9 + U_DIL + n + 1)
                            sp.dma_start(ring_slot(wr, U_DIL + n),
                                         t["w"][bass.ds(p * 9 + U_DIL + 9 + n, 1)].rearrange(
                                             "o p n -> (o p) n")
                                         ).then_inc(w_landed[(U_DIL + n) % RING], 16)
                    hold(sp, s_dr, p * 9 + 9)
                    sp.dma_start(t["dilT"][bass.ds(p, 1)].rearrange("o p g q -> (o p) g q"),
                                 dq[:, 3:9, :]).then_inc(s_dout, 16)
                    hold(sp, s_dtc, p * 2 + 2)
                    for g in range(3):
                        w = WINS[g]
                        for kv in range(2):
                            sp.dma_start(
                                t[f"new_dil{g + 1}"].rearrange("b w (k p c) -> b w k p c", k=2, p=4)[
                                    :, w - S:w, kv, bass.ds(p, 1), :].rearrange("b w o c -> b w (o c)"),
                                newd[:, 3 * kv + g, :]).then_inc(s_dout, 16)
                with sp.Fori(0, 3) as p:
                    turn_io(p, True)
                turn_io(3, False)
                sp.wait_ge(s_dout, 5 * OUTS_PER_TURN)

            @block.gpsimd
            def _(pool):
                bulk_copies(pool, 8)

            @block.scalar
            def _(act):
                act.sem_inc(s_dout, OUTS_PER_TURN)
                with act.Fori(0, 4) as p:
                    hold(act, s_dout, (p + 1) * OUTS_PER_TURN)
                    for n in range(9):
                        hold(act, sm["w_used"], p * 9 + U_DIL + n + 1)
                        act.activation(dq[:, n, :], banks[n % 2][:, :], ACT.Copy).then_inc(s_dr, 1)
                    att_act(act, p, R * NBLK, dil_widths, False,
                            obT[:, bass.ds(p, 1), 0:SEQ].rearrange("p o q -> p (o q)"))

            @block.vector
            def _(dve):
                ch = Chain(dve, sem("dve_chain3"))
                with dve.Fori(0, 4) as p:
                    ch.enter(p, 34)
                    hold(dve, s_dout, (p + 1) * OUTS_PER_TURN)
                    for n in range(9):
                        hold(dve, sm["w_used"], p * 9 + U_DIL + n + 1)
                        dve.tensor_copy(dqS[:, n, :], banks[2 + n % 2][:, 0:NS]).then_inc(s_drS, 1)
                    hold(dve, s_drS, p * 9 + 9)
                    ch.count(dve.tensor_copy(
                        qkS[:, bass.ds(p, 1), :, :].rearrange("p o n q -> p (o n q)"),
                        dqS[:, :, :].rearrange("p n q -> p (n q)")))
                    hold(dve, s_dtr, p * 2 + 1)
                    for g in range(3):
                        last = dve.tensor_copy(dv[:, g, :], banks[5 + g][:, :])
                    last.then_inc(s_dtc, 1)
                    hold(dve, s_dtr, p * 2 + 2)
                    ch.count(dve.tensor_copy(newd[:, 0:4, :].rearrange("p n c -> p (n c)"),
                                             banks[4][0:NS, :]))
                    dve.tensor_copy(newd[:, 4:6, :].rearrange("p n c -> p (n c)"),
                                    banks[0][0:NS, 0:256]).then_inc(s_dtc, 1)
                    att_dve(dve, ch, p, R * NBLK, dil_widths, False,
                            lambda i: (con[:, C_M4 + 384 - P * i:C_M4 + 512],
                                       con[:, C_M16 + 384 - P * i:C_M16 + 512],
                                       con[:, C_M1 + (P if i == 0 else 0):C_M1 + 256]))
                ch.leave(4)

            @block.tensor
            def _(pe):
                with pe.Fori(0, 4) as p:
                    hold(pe, s_att, p + R + 1)
                    for n in range(9):
                        if n >= 2:
                            hold(pe, s_dr, p * 9 + n - 1)
                            hold(pe, s_drS, p * 9 + n - 1)
                        t_tile(pe, wr, U_DIL + n, n, p, 9).then_inc(sm["w_used"], 1)
                    hold(pe, s_dr, p * 9 + 9)
                    for g in range(3):
                        for i in range(NI):
                            last = pe.transpose(banks[5 + g][:, i * P:i * P + P],
                                                dq[:, 6 + g, i * P:i * P + P], ident)
                    last.then_inc(s_dtr, 1)
                    hold(pe, s_drS, p * 9 + 9)
                    for n in range(6):
                        bank = banks[4] if n < 4 else banks[0]
                        last = pe.transpose(bank[0:NS, (n % 4) * P:(n % 4) * P + P], dqS[:, 3 + n, :],
                                            ident)
                    last.then_inc(s_dtr, 1)
                    hold(pe, s_dtc, p * 2 + 2)

                    def first(i):
                        return max(0, i - 1)

                    att_pe(pe, p, R * NBLK, (dq[:, 1, :], dq[:, 2, :], dq[:, 0, :]), dq[:, 4, :],
                           dq[:, 5, :], lambda r0, i: dq[r0:r0 + DH, 3, first(i) * P:(i + 1) * P],
                           lambda hh, kt: dv[:, 1, kt * P + hh * DH:kt * P + hh * DH + DH],
                           lambda hh, kt: dv[:, 2, kt * P + hh * DH:kt * P + hh * DH + DH],
                           lambda hh, i, c: dv[:, 0, (first(i) + c) * P + hh * DH:
                                               (first(i) + c) * P + hh * DH + DH], dil_widths)
        p3.close()
        p2.close()
        p12.close()
        p4 = ExitStack()
        cx = sb("cx", [P, PAGES, 4, JJ, 8], p4)
        sx = sb("sx", [P, PAGES, 2, P], p4)
        wk = sb("wk", [P, 512], p4)
        wv = sb("wv", [P, 4, P], p4)
        vnew = sb("vnew", [2 * S, P], p4)
        pt = sb("pt", [1, B * PAGES], p4, I32)
        T_NEW, T_WIN = PAST, PAST + 2 * S
        T_CMP = T_WIN + 512
        T = sb("T", [NS, T_CMP + NC_S], p4)
        NCH = 32 + 4 + 2 + 1
        pT = sb("pT", [P, NCH * NS], p4)
        hid = sb("hid", [HID, 2, G, NSEG], p4)
        hsq = sb("hsq", [HID, 2, G, NSEG], p4)
        hin = sb("hin", [HID, 2, G, NSEG], p4)
        kcT = sb("kcT", [P, NC_S], p4)
        vc = sb("vc", [P, 2, P], p4)
        qb = sb("qb", [P, NS], p4)
        imp = sb("imp", [NS, NSEG + 1], p4)
        score = sb("score", [NS, NB], p4)
        part = sb("part", [NS, NB], p4)
        best = sb("best", [NS, 8], p4)
        mt = sb("mt", [NS, 3], p4)
        dn = sb("dn", [NS, 3], p4)
        om = sb("om", [NS, P], p4)
        s_pt = sem("page_table_landed")
        s_turn = sem("page_loads_begun")
        s_cL = sem("cmp_pages_landed")
        s_sL = sem("sel_pages_landed")
        s_wL = sem("window_landed")
        s_qb = sem("request_queries_ready")
        s_a = sem("small_scores_ready")
        s_ar = sem("small_scores_read")
        s_ce = sem("cmp_exp_ready")
        s_cm = sem("cmp_maximum_ready")
        s_pc = sem("cmp_probs_ready")
        s_im = sem("importance_ready")
        s_s = sem("sel_scores_ready")
        s_sr = sem("sel_scores_read")
        s_sm = sem("sel_maximum_ready")
        s_se = sem("sel_exp_ready")
        s_sp = sem("sel_probs_ready")
        s_ft = sem("sel_probsT_bank_ready")
        s_fc = sem("sel_probsT_ready")
        s_v = sem("request_summed")
        s_om = sem("request_masked")
        s_os = sem("request_spread")
        s_or = sem("request_finished")
        SBANK = [0, 1, 2, 3, 4, 5, 0, 1]

        with nc.Block() as block:
            @block.sync
            def _(sp):
                sp.dma_start(pt[:, :], t["page_table"]).then_inc(s_pt, 16)
                sp.wait_ge(s_pt, 16)

                def cmp_pages(b):
                    with sp.Fori(0, PAGES) as j:
                        page = sp.value_load(pt[0:1, bass.ds(b * PAGES + j, 1)], min_val=0,
                                             max_val=t["cmp_pages"].shape[0] - 1)
                        sp.dma_start(
                            cx[:, bass.ds(j, 1), :, :, :].rearrange("p o g j s -> p (o g j s)"),
                            t["cmp_pages"][bass.ds(page, 1)].rearrange("o p n -> (o p) n")
                        ).then_inc(s_cL, 16)

                def sel_pages(b):
                    sp.dma_start(wk[:, :], t["win_k"][bass.ds(b, 1)].rearrange("o p n -> (o p) n")
                                 ).then_inc(s_wL, 16)
                    sp.dma_start(wv[:, :, :],
                                 t["win_v"][bass.ds(b, 1)].rearrange("o p c n -> (o p) c n")
                                 ).then_inc(s_wL, 16)
                    for k in range(2):
                        sp.dma_start(vnew[S * k:S * k + S, :],
                                     t["scr_v"][bass.ds(b * S, S), k, :]).then_inc(s_wL, 16)
                    with sp.Fori(0, PAGES) as j:
                        page = sp.value_load(pt[0:1, bass.ds(b * PAGES + j, 1)], min_val=0,
                                             max_val=t["sel_pages"].shape[0] - 1)
                        sp.dma_start(
                            sx[:, bass.ds(j, 1), :, :].rearrange("p o k n -> p (o k n)"),
                            t["sel_pages"][bass.ds(page, 1)].rearrange("o p n -> (o p) n")
                        ).then_inc(s_sL, 16)

                with sp.Fori(0, 1) as b:
                    cmp_pages(b)
                    sel_pages(b)
                with sp.Fori(1, B) as b:
                    hold(sp, s_hid, b * 2 + 2)
                    sp.sem_inc(s_turn, 1)
                    cmp_pages(b)
                    hold(sp, s_v, b)
                    sel_pages(b)

            @block.gpsimd
            def _(pool):
                bulk_copies(pool, 16)

            @block.scalar
            def _(act):
                act.sem_inc(s_or, 1)
                with act.Fori(0, B) as b:
                    compress_act(act, NSEG, hid, hsq, hin, b, 2)
                    hold(act, s_ck, b + 2)
                    act.activation(kcT[:, :], banks[4][:, 0:NC_S], ACT.Copy, scale=0.5)
                    act.activation(vc[:, 0, :], banks[5][:, 0:P], ACT.Copy, scale=0.5)
                    act.activation(vc[0:P - 1, 1, :], banks[5][0:P - 1, P:2 * P], ACT.Copy,
                                   scale=0.5).then_inc(s_ckr, 1)
                    hold(act, s_cm, b + 1)
                    act.activation(T[:, T_CMP:], T[:, T_CMP:], ACT.Exp, scale=SCALE,
                                   bias=mt[:, 0:1], accum_out=dn[:, 0:1]).then_inc(s_ce, 1)
                    hold(act, s_sm, b + 1)
                    act.activation(T[:, 0:T_NEW + S], T[:, 0:T_NEW + S], ACT.Exp, scale=SCALE,
                                   bias=mt[:, 1:2], accum_out=dn[:, 1:2])
                    act.activation(T[:, T_NEW + S:T_CMP], T[:, T_NEW + S:T_CMP], ACT.Exp,
                                   scale=SCALE, bias=mt[:, 2:3],
                                   accum_out=dn[:, 2:3]).then_inc(s_se, 1)
                    for n in range(2):
                        hold(act, s_ft, b * 3 + n + 1)
                        act.activation(pT[:, 512 * n:512 * n + 512], banks[n][:, :],
                                       ACT.Copy).then_inc(s_fc, 1)
                    hold(act, s_ft, b * 3 + 3)
                    for k0, k1, m in ((0, 5, P), (5, 6, P - 1), (6, 7, 2 * S)):
                        last = act.activation(pT[0:m, 1024 + NS * k0:1024 + NS * k1],
                                              banks[2][0:m, NS * k0:NS * k1], ACT.Copy)
                    last.then_inc(s_fc, 1)
                    hold(act, s_os, b + 1)
                    act.activation(oaT[:, :, bass.ds(b * S + SEQ, S)],
                                   banks[6][:, 0:16].rearrange("p (r s) -> p r s", r=R),
                                   ACT.Copy).then_inc(s_or, 1)

            @block.vector
            def _(dve):
                ch = Chain(dve, sem("dve_chain4"))
                ch.link(dve.memset(qb[:, :], 0.0))
                ch.link(dve.memset(imp[:, :], 0.0))
                with dve.Fori(0, B) as b:
                    ch.enter(b, 24)
                    for g in range(G):
                        last = dve.tensor_copy(
                            qb[g * DH:g * DH + DH, 16 * g:16 * g + 16].rearrange(
                                "p (s r) -> p r s", s=S),
                            qaS[g * DH:g * DH + DH, :, bass.ds(b * S, S)])
                        if g == 0:
                            ch.count(last)
                    last.then_inc(s_qb, 1)
                    compress_dve(dve, ch, NSEG, hid, hsq, hin, b, 2)
                    hold(dve, s_a, b + 1)
                    ch.count(dve.tensor_copy(T[:, T_CMP:], banks[6][0:NS, 0:NC_S]))
                    ch.count(dve.tensor_tensor(T[:, T_NEW:T_WIN], banks[6][0:NS, 256:256 + 2 * S],
                                               row[:, R_NEW:R_NEW + 2 * S], ALU.add))
                    dve.tensor_tensor(T[:, T_WIN:T_CMP], banks[7][0:NS, :],
                                      row[:, R_WIN:R_WIN + 512], ALU.add).then_inc(s_ar, 1)
                    hold(dve, s_ar, b + 1)
                    ch.link(dve.tensor_reduce(mt[:, 0:1], T[:, T_CMP:], AX.X, ALU.max))
                    dve.tensor_scalar(mt[:, 0:1], mt[:, 0:1], -SCALE, None, ALU.mult).then_inc(s_cm, 1)
                    hold(dve, s_ce, b + 1)
                    ch.link(dve.reciprocal(dn[:, 0:1], dn[:, 0:1]))
                    dve.tensor_scalar(T[:, T_CMP:], T[:, T_CMP:], dn[:, 0:1], None,
                                      ALU.mult).then_inc(s_pc, 1)
                    hold(dve, s_im, b + 1)
                    ch.link(dve.tensor_copy(imp[:, 1:NSEG], banks[6][0:NS, 0:NC_S]))
                    n = NB - 1
                    i4 = imp[:, 0:NSEG].rearrange("p (j m) -> p j m", m=4)
                    ch.count(dve.tensor_reduce(part[:, 0:n], i4[:, :, 1:4], AX.X, ALU.add))
                    ch.link(dve.tensor_tensor(score[:, 0:n], i4[:, :, 0],
                                              imp[:, 4:NSEG + 1:4], ALU.add))
                    ch.link(dve.scalar_tensor_tensor(out=score[:, 0:n], in0=part[:, 0:n], scalar=2.0,
                                                     in1=score[:, 0:n], op0=ALU.mult, op1=ALU.add))
                    ch.count(dve.memset(score[:, 0:1], FORCED))
                    ch.count(dve.memset(score[:, NB - 2:NB], FORCED))
                    for _ in range(2):
                        dve.drain()
                        dve.max(best[:, :], score[:, :])
                        dve.drain()
                        ch.count(dve.match_replace(score[:, :], best[:, :], score[:, :], TAKEN))
                    ch.wait()
                    ch.link(dve.tensor_scalar(score[:, :], score[:, :], TAKEN, 1.0, ALU.is_equal,
                                              ALU.subtract))
                    ch.link(dve.tensor_scalar(score[:, :], score[:, :], -NEG, None, ALU.mult))
                    for c in range(8):
                        hold(dve, s_s, b * 8 + c + 1)
                        bm = score[:, 8 * c:8 * c + 8].rearrange("p (j o) -> p j o", o=1)
                        dve.tensor_tensor(
                            T[:, 512 * c:512 * c + 512].rearrange("p (j k) -> p j k", k=SELB),
                            banks[SBANK[c]][0:NS, :].rearrange("p (j k) -> p j k", k=SELB),
                            bm.to_broadcast([NS, 8, SELB]), ALU.add).then_inc(s_sr, 1)
                    hold(dve, s_sr, b * 8 + 8)
                    ch.count(dve.tensor_reduce(mt[:, 1:2], T[:, 0:T_NEW + S], AX.X, ALU.max))
                    ch.link(dve.tensor_reduce(mt[:, 2:3], T[:, T_NEW + S:T_CMP], AX.X, ALU.max))
                    dve.tensor_scalar(mt[:, 1:3], mt[:, 1:3], -SCALE, None, ALU.mult).then_inc(s_sm, 1)
                    hold(dve, s_se, b + 1)
                    ch.link(dve.reciprocal(dn[:, 1:3], dn[:, 1:3]))
                    gate = bgate[:, bass.ds(b, 1), :].rearrange("p o c -> p (o c)")
                    ch.link(dve.tensor_tensor(dn[:, 1:3], dn[:, 1:3], gate[:, 1:3], ALU.mult))
                    ch.link(dve.tensor_copy(dn[:, 0:1], gate[:, 0:1]))
                    for k, (c0, c1) in enumerate(((T_CMP, T_CMP + NC_S), (0, T_NEW + S),
                                                  (T_NEW + S, T_CMP))):
                        last = dve.tensor_scalar(T[:, c0:c1], T[:, c0:c1], dn[:, k:k + 1], None,
                                                 ALU.mult)
                        if k < 2:
                            ch.count(last)
                    last.then_inc(s_sp, 1)
                    hold(dve, s_v, b + 1)
                    dve.tensor_tensor(om[:, :], banks[7][0:NS, 0:P], row[:, R_GRP:R_GRP + P],
                                      ALU.mult).then_inc(s_om, 1)
                ch.leave(B)

            @block.tensor
            def _(pe):
                with pe.Fori(0, B) as b:
                    hold(pe, s_cL, b * 16 * PAGES + 16 * PAGES)
                    compress_pe(pe, cx, NSEG, banks[4], banks[5], hid, b, 2)
                    hold(pe, s_ckr, b + 2)
                    hold(pe, s_qb, b + 1)
                    hold(pe, s_or, b + 1)
                    hold(pe, s_wL, b * 64 + 64)
                    new = bass.ds(b * S, S)
                    pe.matmul(banks[6][0:NS, 0:NC_S], qb[:, :], kcT[:, :], start=True, stop=True)
                    pe.matmul(banks[6][0:NS, 256:256 + S], qb[:, :], kvS[:, 2, new], start=True,
                              stop=True)
                    pe.matmul(banks[6][0:NS, 256 + S:256 + 2 * S], qb[:, :], kvS[:, 4, new],
                              start=True, stop=True)
                    pe.matmul(banks[7][0:NS, :], qb[:, :], wk[:, :], start=True,
                              stop=True).then_inc(s_a, 1)
                    hold(pe, s_sL, b * 16 * PAGES + 16 * PAGES)

                    def sel_scores(c):
                        pe.matmul(banks[SBANK[c]][0:NS, :], qb[:, :], sx[:, 4 * c:4 * c + 4, 0, :],
                                  start=True, stop=True).then_inc(s_s, 1)
                    for c in range(6):
                        sel_scores(c)
                    hold(pe, s_pc, b + 1)
                    pe.matmul(banks[6][0:NS, 0:NC_S], row[:, R_IMP:R_IMP + NS], T[:, T_CMP:],
                              start=True, stop=True).then_inc(s_im, 1)
                    for c in range(6, 8):
                        hold(pe, s_sr, b * 8 + c - 5)
                        sel_scores(c)
                    hold(pe, s_sp, b + 1)
                    for n in range(2):
                        for k in range(16):
                            c = 16 * n + k
                            last = pe.transpose(banks[n][:, NS * k:NS * k + NS],
                                                T[:, P * c:P * c + P], ident[0:NS, 0:NS])
                        last.then_inc(s_ft, 1)
                    tail = [(T_WIN + P * c, P) for c in range(4)]
                    tail += [(T_CMP, P), (T_CMP + P, P - 1), (T_NEW, 2 * S)]
                    for k, (c0, m) in enumerate(tail):
                        last = pe.transpose(banks[2][0:m, NS * k:NS * k + NS], T[:, c0:c0 + m],
                                            ident[0:NS, 0:NS])
                    last.then_inc(s_ft, 1)
                    hold(pe, s_fc, b * 3 + 3)
                    vals = [(sx[:, c, 1, :], P) for c in range(PAGES)]
                    vals += [(wv[:, c, :], P) for c in range(4)]
                    vals += [(vc[:, 0, :], P), (vc[0:P - 1, 1, :], P - 1), (vnew[:, :], 2 * S)]
                    for k, (v, m) in enumerate(vals):
                        last = pe.matmul(banks[7][0:NS, 0:P], pT[0:m, NS * k:NS * k + NS], v,
                                         start=(k == 0), stop=(k == NCH - 1))
                    last.then_inc(s_v, 1)
                    hold(pe, s_om, b + 1)
                    pe.matmul(banks[6][:, 0:16], om[:, :], row[:, R_SPR:R_SPR + 16], start=True,
                              stop=True).then_inc(s_os, 1)
        p4.close()

        p5 = ExitStack()
        dk = [sb(f"dk{i}", [P, 4, DILK], p5) for i in range(2)]
        dvs = [sb(f"dvs{i}", [P, 9, 512], p5) for i in range(2)]
        dvn = [sb(f"dvn{i}", [3 * S, 512], p5) for i in range(2)]
        lq = [sb(f"lq{i}", [P, 3, 136], p5) for i in range(2)]
        TD = [sb(f"TD{i}", [NS, DILK + 12], p5) for i in range(2)]
        pTD = [sb(f"pTD{i}", [P, 10 * NS], p5) for i in range(2)]
        omD = [sb(f"omD{i}", [NS, 512], p5) for i in range(2)]
        md = sb("md", [NS, 2], p5)
        dd = sb("dd", [NS, 2], p5)
        s_kL = [sem(f"dil_keys_landed{i}") for i in range(2)]
        s_lq = sem("dil_queries_ready")
        s_ds = sem("dil_scores_ready")
        s_dsr = sem("dil_scores_read")
        s_dm = sem("dil_maximum_ready")
        s_de = sem("dil_exp_ready")
        s_dp = sem("dil_probs_ready")
        s_dt = sem("dil_probsT_bank_ready")
        s_dc = sem("dil_probsT_ready")
        s_dvv = sem("dil_request_summed")
        s_dom = sem("dil_request_masked")
        s_dos = sem("dil_request_spread")
        s_dor = sem("dil_request_finished")
        GOFF = (0, 128, 640)
        GLEN = (128, 512, 512)

        with nc.Block() as block:
            @block.sync
            def _(sp):
                def load(b, i):
                    sp.dma_start(dk[i][:, :, :], t["dil_k"][bass.ds(b, 1)].rearrange(
                        "o p c n -> (o p) c n")).then_inc(s_kL[i], 16)
                    sp.dma_start(dvs[i][:, :, :], t["dil_v"][bass.ds(b, 1)].rearrange(
                        "o p c n -> (o p) c n")).then_inc(s_kL[i], 16)
                    for g in range(3):
                        w = WINS[g]
                        sp.dma_start(dvn[i][S * g:S * g + S, :],
                                     t[f"new_dil{g + 1}"][bass.ds(b, 1), w - S:w, 512:1024].rearrange(
                                         "o w c -> (o w) c")).then_inc(s_kL[i], 16)
                with sp.Fori(0, 1) as j:
                    for i in range(2):
                        load(j + i, i)
                with sp.Fori(1, B // 2) as j:
                    for i in range(2):
                        hold(sp, s_dvv, j * 2 + i - 1)
                        load(j * 2 + i, i)

            @block.gpsimd
            def _(pool):
                bulk_copies(pool, len(bulk) - sent["n"])

            @block.scalar
            def _(act):
                act.sem_inc(s_dor, 2)
                with act.Fori(0, B // 2) as j:
                    for i in range(2):
                        hold(act, s_dm, j * 2 + i + 1)
                        act.activation(TD[i][:, :], TD[i][:, :], ACT.Exp, scale=SCALE,
                                       bias=md[:, i:i + 1],
                                       accum_out=dd[:, i:i + 1]).then_inc(s_de, 1)
                    for i in range(2):
                        hold(act, s_dt, j * 2 + i + 1)
                        act.activation(pTD[i][:, 0:9 * NS], banks[4][:, 0:9 * NS], ACT.Copy)
                        act.activation(pTD[i][0:12, 9 * NS:], banks[4][0:12, 9 * NS:10 * NS],
                                       ACT.Copy).then_inc(s_dc, 1)
                        hold(act, s_dos, j * 2 + i + 1)
                        act.activation(obT[:, :, bass.ds(j * 2 * S + (SEQ + S * i), S)],
                                       banks[6][:, 0:16].rearrange("p (h s) -> p h s", h=4),
                                       ACT.Copy).then_inc(s_dor, 1)

            @block.vector
            def _(dve):
                ch = Chain(dve, sem("dve_chain5"))
                for i in range(2):
                    ch.link(dve.memset(lq[i][:, :, :], 0.0))
                with dve.Fori(0, B // 2) as j:
                    ch.enter(j, 20)
                    for i in range(2):
                        hold(dve, s_dor, j * 2 + 2)
                        for g in range(3):
                            for hh in range(2):
                                dst = lq[i][hh * DH:hh * DH + DH, g, :].rearrange(
                                    "p (k c) -> p k c", c=34)[:, :, hh:hh + 25:8]
                                last = dve.tensor_copy(
                                    dst, qkS[hh * DH:hh * DH + DH, :, g, bass.ds(j * 2 * S + S * i, S)])
                                if (g, hh) != (2, 1):
                                    ch.count(last)
                        last.then_inc(s_lq, 1)
                    for i in range(2):
                        hold(dve, s_ds, j * 2 + i + 1)
                        for g in range(3):
                            o = GOFF[g]
                            ch.count(dve.tensor_tensor(TD[i][:, o:o + GLEN[g]],
                                                       banks[g][0:NS, 0:GLEN[g]],
                                                       row[:, R_DIL + o:R_DIL + o + GLEN[g]], ALU.add))
                        dve.tensor_tensor(TD[i][:, DILK:], banks[3][0:NS, 0:12],
                                          row[:, R_DIL + DILK:R_DIL + DILK + 12],
                                          ALU.add).then_inc(s_dsr, 1)
                        hold(dve, s_dsr, j * 2 + i + 1)
                        ch.link(dve.tensor_reduce(md[:, i:i + 1], TD[i][:, :], AX.X, ALU.max))
                        dve.tensor_scalar(md[:, i:i + 1], md[:, i:i + 1], -SCALE, None,
                                          ALU.mult).then_inc(s_dm, 1)
                    for i in range(2):
                        hold(dve, s_de, j * 2 + i + 1)
                        ch.link(dve.reciprocal(dd[:, i:i + 1], dd[:, i:i + 1]))
                        dve.tensor_scalar(TD[i][:, :], TD[i][:, :], dd[:, i:i + 1], None,
                                          ALU.mult).then_inc(s_dp, 1)
                    for i in range(2):
                        hold(dve, s_dvv, j * 2 + i + 1)
                        dve.tensor_tensor(omD[i][:, :], banks[5][0:NS, :],
                                          row[:, R_HEAD:R_HEAD + 512], ALU.mult).then_inc(s_dom, 1)
                ch.leave(B // 2)

            @block.tensor
            def _(pe):
                with pe.Fori(0, B // 2) as j:
                    def scores(i):
                        hold(pe, s_lq, j * 2 + i + 1)
                        hold(pe, s_kL[i], j * 80 + 80)
                        if i:
                            hold(pe, s_dsr, j * 2 + i)
                        for g in range(3):
                            o = GOFF[g]
                            for k in range(4):
                                pe.matmul(banks[g][0:NS, 0:GLEN[g]], lq[i][:, g, 32 * k:32 * k + 32],
                                          dk[i][:, k, o:o + GLEN[g]], start=(k == 0), stop=(k == 3))
                        for g in range(3):
                            for k in range(4):
                                last = pe.matmul(banks[3][0:NS, S * g:S * g + S],
                                                 lq[i][:, g, 32 * k:32 * k + 32],
                                                 qkS[:, k, 3 + g, bass.ds(j * 2 * S + S * i, S)],
                                                 start=(k == 0), stop=(k == 3))
                        last.then_inc(s_ds, 1)

                    for i in range(2):
                        scores(i)
                    for i in range(2):
                        hold(pe, s_dp, j * 2 + i + 1)
                        for c in range(10):
                            m = P if c < 9 else 12
                            last = pe.transpose(banks[4][0:m, NS * c:NS * c + NS],
                                                TD[i][:, P * c:P * c + m], ident[0:NS, 0:NS])
                        last.then_inc(s_dt, 1)
                        hold(pe, s_dc, j * 2 + i + 1)
                        for c in range(10):
                            m = P if c < 9 else 12
                            v = dvs[i][:, c, :] if c < 9 else dvn[i][:, :]
                            last = pe.matmul(banks[5][0:NS, :], pTD[i][0:m, NS * c:NS * c + NS], v,
                                             start=(c == 0), stop=(c == 9))
                        last.then_inc(s_dvv, 1)
                        hold(pe, s_dom, j * 2 + i + 1)
                        if i:
                            hold(pe, s_dor, j * 2 + 2 + i)
                        for k in range(4):
                            last = pe.matmul(banks[6][:, S * k:S * k + S], omD[i][:, P * k:P * k + P],
                                             row[:, R_TOK:R_TOK + S], start=True, stop=True)
                        last.then_inc(s_dos, 1)
        p5.close()
        pc.close()
        p6 = ExitStack()
        wr6 = sb("wring6", [P, RING, UNIT], p6)
        x6 = sb("x6", [P, KD, NT], p6)
        pA = ExitStack()
        mT = sb("mT", [P, KD, NT], pA)
        gm = sb("gm", [P, 2, 3, NT], pA)
        s_x6 = sem("x_again_landed")
        s_gt = sem("merge_gates_ready")
        s_bp = sem("branch_tile_ready")
        s_bq = sem("branch_tile_read")
        s_xo = sem("x_updated")
        s_mj = sem("merged_ready")

        def out_tile(pe, n, first, last_k, k, w, wk, rhs):
            pe.matmul(banks[3 + n % 2][:, :], w[:, wk * P:wk * P + P], rhs[:, k, 0:SEQ],
                      start=first, stop=last_k)
            return pe.matmul(banks[5 + n % 2][:, 0:NS], w[:, wk * P:wk * P + P], rhs[:, k, SEQ:NT],
                             start=first, stop=last_k)

        with nc.Block() as block:
            @block.sync
            def _(sp):
                for u in range(U_MIX, U_MIX + RING):
                    sp.wait_ge(sm["w_used"], U_MIX)
                    sp.dma_start(ring_slot(wr6, u), t["w"][u]).then_inc(w_landed[u % RING], 16)
                for k in range(KD):
                    sp.dma_start(x6[:, k, :], t["xT"][:, k, :]).then_inc(s_x6, 16)
                with sp.Fori(0, 3) as j:
                    for n in range(RING):
                        hold(sp, sm["w_used"], j * 9 + U_MIX + n + 1)
                        sp.dma_start(ring_slot(wr6, U_MIX + n),
                                     t["w"][bass.ds(j * 9 + U_MIX + 9 + n, 1)].rearrange(
                                         "o p n -> (o p) n")
                                     ).then_inc(w_landed[(U_MIX + n) % RING], 16)
                load_units(sp, wr6, U_OUT, 8)

            @block.scalar
            def _(act):
                with act.Fori(0, 4) as j:
                    for n in range(6):
                        hold(act, sm["w_used"], j * 9 + U_MIX + n + 1)
                        if n == 0:
                            hold(act, s_mj, j * 2 + 2)
                        g = gm[:, n // 3, n % 3, :]
                        act.activation(g[:, 0:SEQ], banks[n % 2][:, :], ACT.Tanh, scale=0.5)
                        act.activation(g[:, SEQ:NT], banks[2 if n % 2 == 0 else 7][:, 0:NS],
                                       ACT.Tanh, scale=0.5).then_inc(s_gt, 1)

            @block.vector
            def _(dve):
                ch = Chain(dve, sem("dve_chain6"))
                dve.sem_inc(s_bq, 6)
                dve.sem_inc(s_mj, 2)
                with dve.Fori(0, 4) as j:
                    ch.enter(j, 8)
                    for n in range(6):
                        hold(dve, s_bp, j * 6 + n + 1)
                        hold(dve, s_gt, j * 6 + n + 1)
                        g = gm[:, n // 3, n % 3, :]
                        ch.count(dve.scalar_tensor_tensor(
                            out=g[:, 0:SEQ], in0=g[:, 0:SEQ], scalar=1.0, in1=banks[3 + n % 2][:, :],
                            op0=ALU.add, op1=ALU.mult))
                        dve.scalar_tensor_tensor(
                            out=g[:, SEQ:NT], in0=g[:, SEQ:NT], scalar=1.0,
                            in1=banks[5 + n % 2][:, 0:NS], op0=ALU.add,
                            op1=ALU.mult).then_inc(s_bq, 1)
                        if n % 3 == 2:
                            a = gm[:, n // 3, :, :]
                            m = mT[:, bass.ds(j * 2 + n // 3, 1), :].rearrange("p o q -> p (o q)")
                            hold(dve, s_bq, j * 6 + 6 + n + 1)
                            ch.link(dve.tensor_tensor(a[:, 0, :], a[:, 0, :], a[:, 1, :], ALU.add))
                            dve.tensor_tensor(m, a[:, 0, :], a[:, 2, :], ALU.add).then_inc(s_mj, 1)
                ch.leave(4)
                dve.wait_ge(s_x6, 16 * KD)
                for n in range(KD):
                    dve.wait_ge(s_bp, 24 + n + 1)
                    x = x6[:, n, :]
                    ch.count(dve.scalar_tensor_tensor(
                        out=x[:, 0:SEQ], in0=banks[3 + n % 2][:, :], scalar=0.5, in1=x[:, 0:SEQ],
                        op0=ALU.mult, op1=ALU.add))
                    dve.scalar_tensor_tensor(
                        out=x[:, SEQ:NT], in0=banks[5 + n % 2][:, 0:NS], scalar=0.5,
                        in1=x[:, SEQ:NT], op0=ALU.mult, op1=ALU.add).then_inc(s_xo, 1)

            @block.tensor
            def _(pe):
                with pe.Fori(0, 4) as j:
                    for n in range(6):
                        if n >= 2:
                            hold(pe, s_gt, j * 6 + n - 1)
                        elif n == 0:
                            hold(pe, s_bq, j * 6 + 6)
                        u = U_MIX + n
                        unit_landed(pe, u, j, 9)
                        w = ring_slot(wr6, u)
                        for k in range(KD):
                            pe.matmul(banks[n % 2][:, :], w[:, k * P:k * P + P], hT[:, k, 0:SEQ],
                                      start=(k == 0), stop=(k == KD - 1))
                        for k in range(KD):
                            last = pe.matmul(banks[2 if n % 2 == 0 else 7][:, 0:NS],
                                             w[:, k * P:k * P + P], hT[:, k, SEQ:NT],
                                             start=(k == 0), stop=(k == KD - 1))
                        last.then_inc(sm["w_used"], 1)
                    for n in range(6):
                        if n >= 2:
                            hold(pe, s_bq, j * 6 + 6 + n - 1)
                        src = (oaT, obT, ocT)[n % 3]
                        for k in range(4):
                            at = 4 * n + k
                            u = U_MIX + 6 + at // KD
                            if at % KD == 0:
                                unit_landed(pe, u, j, 9)
                            w = ring_slot(wr6, u)
                            wk = at % KD
                            pe.matmul(banks[3 + n % 2][:, :], w[:, wk * P:wk * P + P],
                                      src[:, k, 0:SEQ], start=(k == 0), stop=(k == 3))
                            last = pe.matmul(banks[5 + n % 2][:, 0:NS], w[:, wk * P:wk * P + P],
                                             src[:, k, SEQ:NT], start=(k == 0), stop=(k == 3))
                        last.then_inc(s_bp, 1)
                    hold(pe, s_bq, j * 6 + 6 + 6)
                    pe.sem_inc(sm["w_used"], 3)
                for n in range(KD):
                    if n >= 2:
                        pe.wait_ge(s_xo, n - 1)
                    u = U_OUT + n
                    unit_landed(pe, u)
                    if n == 0:
                        pe.wait_ge(s_mj, 10)
                    for k in range(KD):
                        last = out_tile(pe, n, k == 0, k == KD - 1, k, ring_slot(wr6, u), k, mT)
                    last.then_inc(s_bp, 1)
        pA.close()

        p7 = ExitStack()
        aT = sb("aT", [P, 32, NT], p7)
        rl = sb("rl", [P, 2, NT], p7)
        rstd = sb("rstd7", [P, NT], p7)
        s_rl = sem("relu_ready")
        s_up = sem("up_ready")
        s_dn = sem("down_ready")
        s_dnr = sem("down_read")

        def slot8(n):
            return wr6[:, n, :]

        w8 = [sem(f"ffn_unit_landed{i}") for i in range(8)]
        s_u8 = sem("ffn_units_used")

        def sq7(k):
            return oaT[:, k, :] if k < 4 else obT[:, k - 4, :]

        with nc.Block() as block:
            @block.sync
            def _(sp):
                for n in range(8):
                    sp.dma_start(slot8(n), t["w"][U_UP + n]).then_inc(w8[n], 16)
                with sp.Fori(0, 7) as j:
                    for n in range(8):
                        hold(sp, s_u8, j * 8 + n + 1)
                        sp.dma_start(slot8(n), t["w"][bass.ds(j * 8 + U_UP + 8 + n, 1)].rearrange(
                            "o p n -> (o p) n")).then_inc(w8[n], 16)
                for k in range(KD):
                    sp.wait_ge(sm["h_ready"], 2 * KD + k + 1)
                    sp.dma_start(t["yT"][:, k, :], hT[:, k, :]).then_inc(sm["out_done"], 16)

            @block.scalar
            def _(act):
                ch = None
                rms_act(act, ch, x6, sq7, 1, rstd)
                with act.Fori(0, 4) as j:
                    for n in range(8):
                        hold(act, s_u8, j * 8 + n + 1)
                        hold(act, s_up, j * 8 + n + 1)
                        r = rl[:, n % 2, :]
                        act.activation(r[:, 0:SEQ], banks[n % 2][:, :], ACT.Relu)
                        act.activation(r[:, SEQ:NT], banks[2 + n % 2][:, 0:NS],
                                       ACT.Relu).then_inc(s_rl, 1)
                act.wait_ge(s_dnr, 8)
                rms_act(act, ch, x6, sq7, 2, rstd)

            @block.vector
            def _(dve):
                ch = Chain(dve, sem("dve_chain7"))
                dve.sem_inc(s_up, 2)
                rms_dve(dve, ch, x6, hT, 1, rstd)
                with dve.Fori(0, 4) as j:
                    for n in range(8):
                        hold(dve, s_rl, j * 8 + n + 1)
                        dve.tensor_tensor(
                            aT[:, bass.ds(j * 8 + n, 1), :].rearrange("p o q -> p (o q)"),
                            rl[:, n % 2, :], rl[:, n % 2, :], ALU.mult).then_inc(s_up, 1)
                with dve.Fori(0, 4) as j:
                    ch.enter(j, 2)
                    for n in range(2):
                        hold(dve, s_dn, j * 2 + n + 1)
                        x = x6[:, bass.ds(j * 2 + n, 1), :].rearrange("p o q -> p (o q)")
                        ch.count(dve.tensor_tensor(x[:, 0:SEQ], banks[3 + n % 2][:, :], x[:, 0:SEQ],
                                                   ALU.add))
                        dve.tensor_tensor(x[:, SEQ:NT], banks[5 + n % 2][:, 0:NS], x[:, SEQ:NT],
                                          ALU.add).then_inc(s_dnr, 1)
                ch.leave(4)
                dve.wait_ge(s_dnr, 8)
                rms_dve(dve, ch, x6, hT, 2, rstd)

            @block.tensor
            def _(pe):
                rms_pe(pe, sq7, 1)
                pe.wait_ge(sm["h_ready"], 2 * KD)
                with pe.Fori(0, 4) as j:
                    for n in range(8):
                        hold(pe, s_rl, j * 8 + n - 1) if n >= 2 else hold(pe, s_up, j * 8 + n + 1)
                        hold(pe, w8[n], j * 16 + 16)
                        w = slot8(n)
                        for k in range(KD):
                            pe.matmul(banks[n % 2][:, :], w[:, k * P:k * P + P], hT[:, k, 0:SEQ],
                                      start=(k == 0), stop=(k == KD - 1))
                        for k in range(KD):
                            last = pe.matmul(banks[2 + n % 2][:, 0:NS], w[:, k * P:k * P + P],
                                             hT[:, k, SEQ:NT], start=(k == 0), stop=(k == KD - 1))
                        last.then_inc(s_u8, 1)
                pe.wait_ge(s_up, 34)
                with pe.Fori(0, 4) as j:
                    for n in range(2):
                        if n == 0:
                            hold(pe, s_up, 34)
                        for q in range(4):
                            hold(pe, w8[4 * n + q], j * 16 + 16 * 5)
                            for k in range(KD):
                                kk = KD * q + k
                                w = slot8(4 * n + q)
                                pe.matmul(banks[3 + n][:, :], w[:, k * P:k * P + P],
                                          aT[:, kk, 0:SEQ], start=(kk == 0), stop=(kk == 31))
                                last = pe.matmul(banks[5 + n][:, 0:NS], w[:, k * P:k * P + P],
                                                 aT[:, kk, SEQ:NT], start=(kk == 0), stop=(kk == 31))
                            if q < 3:
                                last.then_inc(s_u8, 1)
                        last.then_inc(s_dn, 1)
                        hold(pe, s_dnr, j * 2 + n + 1)
                        pe.sem_inc(s_u8, 1)
                rms_pe(pe, sq7, 2)
        p7.close()
        p6.close()
        with nc.Block() as block:
            @block.sync
            def _(sp):
                sp.wait_ge(sm["out_done"], 48 + 16 * KD)
                sp.wait_ge(sm["store_done"], 256)
                sp.wait_ge(sm["bulk_done"], 16 * sent["n"])


_OUTS = [("yT", (P, KD, NT)), ("kvT", (P, 6, SEQ)), ("kvS", (P, 6, NS)), ("dilT", (4, P, 6, SEQ)),
         ("new_win", (B, 512, 256)), ("new_dil1", (B, 128, 1024)), ("new_dil2", (B, 512, 1024)),
         ("new_dil3", (B, 2048, 1024)), ("sgu_v", (NS, 512))]
_SCRATCH = [("scr_gate", (24, NS)), ("scr_v", (NS, 2, P))]
_IN = [("xT", (P, KD, NT)), ("con", (P, C_END)), ("row", (NS, R_END)), ("norm_g", (P, 3, KD)),
       ("w", (N_UNITS, P, UNIT)), ("ln_g", (1, 512)), ("ln_b", (1, 512)), ("wsT", (P, 8, P)),
       ("ws4", (NS, 8, NS)), ("bs", (2, 4, P + NS)), ("half", (2, P)),
       ("w1", (P, 2, 16, HID)), ("w2", (HID, 2, DH)), ("pe_t", (P, 2, 16)), ("b1", (HID, 2)),
       ("page_table", (1, B * PAGES)), ("cmp_pages", (320, P, 256)), ("sel_pages", (320, P, 256)),
       ("win_k", (B, P, 512)), ("win_v", (B, P, 4, P)), ("dil_k", (B, P, 4, DILK)),
       ("dil_v", (B, P, 9, 512)),
       ("cache_win", (B, 512, 256)), ("cache_dil1", (B, 128, 1024)), ("cache_dil2", (B, 512, 1024)),
       ("cache_dil3", (B, 2048, 1024))]
DEBUG = []


def kernel(x_prompt, x_sample, cache_cmp_kv, cache_sel_kv, cache_win_kv, cache_dil1_kv,
           cache_dil2_kv, cache_dil3_kv, page_table, norm_mix_g, w_in, cmp_pe, cmp_w1, cmp_b1,
           cmp_w2, sgu_ln_g, sgu_ln_b, sgu_w, sgu_b, w_branch_a, w_branch_b, w_branch_c, w_out,
           norm_mlp_g, w_up, w_down, norm_final_g):
    import concourse.bacc as _bacc
    from concourse.bass_utils import run_bass_kernel_spmd as _run

    f = lambda a: np.asarray(a)
    x = np.concatenate([f(x_prompt)[0], f(x_sample).reshape(NS, D)], 0)
    con, row = shape_constants()
    a = {
        "xT": x.reshape(NT, KD, P).transpose(2, 1, 0),
        "con": con, "row": row,
        "norm_g": np.stack([f(norm_mix_g)[0], f(norm_mlp_g)[0], f(norm_final_g)]
                           ).reshape(3, KD, P).transpose(2, 0, 1),
        "w": weight_stream(f(w_in)[0], f(w_branch_a)[0], f(w_branch_b)[0], f(w_branch_c)[0],
                           f(w_out)[0], f(w_up)[0], f(w_down)[0]),
        "ln_g": f(sgu_ln_g), "ln_b": f(sgu_ln_b),
        "wsT": f(sgu_w)[0].transpose(2, 0, 1),
        "ws4": np.tile(f(sgu_w)[0, :, :S, :S].transpose(2, 0, 1), (B, 1, B)),
        "bs": np.concatenate([f(sgu_b)[0], np.tile(f(sgu_b)[0, :, :S], (1, B))], 1
                             ).reshape(4, 2, P + NS).transpose(1, 0, 2),
        "half": np.repeat(np.eye(2, dtype=np.float32), DH, 1),
        "w1": f(cmp_w1)[0].reshape(2, 16, P, HID).transpose(2, 0, 1, 3),
        "w2": f(cmp_w2)[0].transpose(1, 0, 2),
        "pe_t": f(cmp_pe)[0].reshape(2, 16, P).transpose(2, 0, 1),
        "b1": f(cmp_b1)[0].T,
        **sample_caches(f(cache_cmp_kv)[:, 0], f(cache_sel_kv)[:, 0], f(cache_win_kv)[:, 0],
                        [f(c)[:, 0] for c in (cache_dil1_kv, cache_dil2_kv, cache_dil3_kv)]),
        "page_table": f(page_table).reshape(1, B * PAGES),
        "cache_win": f(cache_win_kv).reshape(B, 512, 256),
        "cache_dil1": f(cache_dil1_kv).reshape(B, 128, 1024),
        "cache_dil2": f(cache_dil2_kv).reshape(B, 512, 1024),
        "cache_dil3": f(cache_dil3_kv).reshape(B, 2048, 1024),
    }
    nc = _bacc.Bacc("TRN2", target_bir_lowering=False, num_devices=1)
    t, arrays = {}, {}
    for name, shape in _IN:
        v = np.ascontiguousarray(a[name])
        assert v.shape == shape, (name, v.shape, shape)
        arrays[f"in_{name}"] = v
        t[name] = nc.dram_tensor(f"in_{name}", shape, mybir.dt.from_np(v.dtype),
                                 kind="ExternalInput").ap()
    for name, shape in _OUTS:
        t[name] = nc.dram_tensor(f"out_{name}", shape, F32, kind="ExternalOutput").ap()
    for name, shape in _SCRATCH:
        t[name] = nc.dram_tensor(name, shape, F32, kind="Internal").ap()
    for name in DEBUG:
        t["dbg_" + name] = nc.dram_tensor("dbg_" + name, (P, 4, NT), F32, kind="ExternalOutput").ap()
    trunk(nc, t)
    r = _run(nc, [arrays], core_ids=[0]).results[0]
    o = {name: r[f"out_{name}"] for name, _ in _OUTS}
    y = o["yT"].transpose(2, 1, 0).reshape(NT, D)
    kv = o["kvT"].transpose(2, 1, 0).reshape(1, 1, SEQ, 3, 2, G, DH)
    kvs = o["kvS"].transpose(2, 1, 0).reshape(B, 1, S, 3, 2, G, DH)
    dil = o["dilT"].reshape(4, 2, DH, 2, 3, SEQ).transpose(4, 5, 3, 0, 1, 2).reshape(
        3, 1, 1, SEQ, 2, 8, DH)
    return (y[:SEQ].reshape(1, SEQ, D), y[SEQ:].reshape(B, S, D),
            kv[:, :, :, 0], kv[:, :, :, 1], kv[:, :, :, 2],
            dil[0][:, :, -WINS[0]:], dil[1], dil[2],
            kvs[:, :, :, 0], kvs[:, :, :, 1],
            o["new_win"].reshape(B, 1, 512, 2, G, DH),
            o["new_dil1"].reshape(B, 1, 128, 2, 8, DH),
            o["new_dil2"].reshape(B, 1, 512, 2, 8, DH),
            o["new_dil3"].reshape(B, 1, 2048, 2, 8, DH),
            o["sgu_v"].reshape(B, 1, S, 512))
```

```python
from contextlib import ExitStack

import numpy as np

import concourse.bass as bass
from concourse import mybir

F32 = mybir.dt.float32
I32 = mybir.dt.int32
ALU = mybir.AluOpType
ACT = mybir.ActivationFunctionType
AX = mybir.AxisListType

P = 128
D = 1024
KD = D // P
SEQ = 512
B = 8
S = 4
NS = B * S
NT = SEQ + NS
HT = NT // 2
NI = SEQ // P
PAST = 4096
PAGE = 128
PAGES = PAST // PAGE
DH = 64
G = 2
R = 4
SCALE = DH ** -0.5
NC_P = SEQ // 16 - 1
NC_S = PAST // 16 - 1
NSEG = PAST // 16
JJ = 8
HID = 128
SELB = 64
NB = PAST // SELB + 1
FORCED = 1e4
FF = 4 * D
NEG = -1e30
TAKEN = -1e30
GELU_C = 0.7978845608028654
GELU_A = 0.044715
RMS_EPS = 1e-6
LN_EPS = 1e-5
RING = 9
UNIT = KD * P
DILK = 128 + 512 + 512
WINS = (128, 512, 2048)

C_ID = 0
C_ONE = C_ID + P
C_EPS = C_ONE + P
C_HEAD = C_EPS + 2
C_MC = C_HEAD
C_M4 = C_MC + 512
C_M16 = C_M4 + 512
C_M1 = C_M16 + 512
C_CMP = C_M1 + 256
C_CMV = C_CMP + NI * 32
C_TRI = C_CMV + NI * 32
C_END = C_TRI + P

R_WIN = 0
R_NEW = R_WIN + 512
R_IMP = R_NEW + 8
R_GRP = R_IMP + 32
R_SPR = R_GRP + P
R_DIL = R_SPR + 16
R_HEAD = R_DIL + DILK + 12
R_TOK = R_HEAD + 512
R_SGU = R_TOK + S
R_END = R_SGU + NS


def shape_constants():
    c = np.zeros((P, C_END), np.float32)
    p = np.arange(P)[:, None]
    c[:, C_ID:C_ID + P] = np.eye(P)
    c[:, C_ONE:C_ONE + P] = 1
    dist = p - (np.arange(512)[None, :] - 384)
    for at, d in ((C_MC, 1), (C_M4, 4), (C_M16, 16)):
        c[:, at:at + 512] = np.where((dist >= 0) & (dist % d == 0), 0, NEG)
    dist = p + 128 - np.arange(256)[None, :]
    c[:, C_M1:C_M1 + 256] = np.where((dist >= 0) & (dist <= 128), 0, NEG)
    for i in range(NI):
        ok = (np.arange(32)[None, :] * 16 + 31 <= i * P + p) & (np.arange(32)[None, :] < NC_P)
        c[:, C_CMP + 32 * i:C_CMP + 32 * i + 32] = np.where(ok, 0, NEG)
        c[:, C_CMV + 32 * i:C_CMV + 32 * i + 32] = ok
    c[:, C_TRI:C_TRI + P] = p <= np.arange(P)[None, :]
    c[:, C_EPS] = RMS_EPS
    c[:, C_EPS + 1] = LN_EPS
    r = np.zeros((NS, R_END), np.float32)
    q = np.arange(NS)
    g, s, rr = q // 16, (q // 4) % 4, q % 4
    r[:, R_WIN:R_WIN + 512] = np.where(np.arange(512)[None, :] >= s[:, None], 0, NEG)
    for k in range(2):
        r[:, R_NEW + 4 * k:R_NEW + 4 * k + 4] = np.where(np.arange(4)[None, :] <= s[:, None], 0, NEG)
    r[:, R_IMP:R_IMP + 32] = (q[:, None] // 4) == (q[None, :] // 4)
    r[:, R_GRP:R_GRP + P] = (np.arange(P)[None, :] // DH) == g[:, None]
    r[:, R_SPR:R_SPR + 16] = np.arange(16)[None, :] == (rr * 4 + s)[:, None]
    s, h = q // 8, q % 8
    m = np.full((NS, DILK + 12), NEG)
    m[:, 0:128] = np.where(np.arange(128)[None, :] >= s[:, None], 0, NEG)
    for k in range(2):
        for ss in range(S):
            m[s == ss, 128 + 512 * k + 128 * ss:128 + 512 * k + 128 * ss + 128] = 0
    for ss in range(S):
        m[:, DILK + ss] = np.where(ss <= s, 0, NEG)
        m[:, DILK + 4 + ss] = np.where(ss == s, 0, NEG)
        m[:, DILK + 8 + ss] = np.where(ss == s, 0, NEG)
    r[:, R_DIL:R_DIL + DILK + 12] = m
    r[:, R_HEAD:R_HEAD + 512] = (np.arange(512)[None, :] // DH) == h[:, None]
    r[:, R_TOK:R_TOK + S] = np.arange(S)[None, :] == s[:, None]
    b, s = q // S, q % S
    r[:, R_SGU:R_SGU + NS] = (b[:, None] == b[None, :]) & (s[:, None] <= s[None, :])
    return c, r


U_A = 0
U_U = U_A + 11
U_V = U_U + 4
U_DIL = U_V + 4
U_MIX = U_DIL + 36
U_OUT = U_MIX + 36
U_UP = U_OUT + 8
U_DN = U_UP + 32
N_UNITS = U_DN + 32


def weight_stream(w_in, w_a, w_b, w_c, w_out, w_up, w_down):
    w = np.zeros((N_UNITS, P, UNIT), np.float32)

    def cols(m, c):
        return m[:, c].reshape(-1, P, len(c)).transpose(1, 0, 2)

    def unit(u, m, c):
        w[u].reshape(P, KD, P)[:, :, :len(c)] = cols(m, c)
    d = np.arange(DH)
    for r in range(R):
        unit(U_A + r, w_in, np.concatenate([g * 256 + r * DH + d for g in range(G)]))
    for i in range(6):
        unit(U_A + 4 + i, w_in, 512 + P * i + np.arange(P))
    unit(U_A + 10, w_in, 1280 + np.arange(24))
    at = 1304 + 4608
    for i in range(4):
        unit(U_U + i, w_in, at + P * i + np.arange(P))
    v = cols(w_in, at + 512 + np.arange(512))
    for i in range(4):
        w[U_V + i] = v[:, 2 * i:2 * i + 2].reshape(P, UNIT)
    for p in range(4):
        for n in range(9):
            unit(U_DIL + 9 * p + n, w_in, 1304 + n * 512 + P * p + np.arange(P))
    at = 1304 + 4608 + 1024
    rows = np.concatenate([g * 256 + r * DH + d for r in range(R) for g in range(G)])
    br = [w_a[rows], w_b, w_c]
    for jp in range(4):
        for jj in range(2):
            j = 2 * jp + jj
            for i in range(3):
                unit(U_MIX + 9 * jp + 3 * jj + i, w_in, at + i * D + P * j + np.arange(P))
        t = [cols(br[i], P * (2 * jp + jj) + np.arange(P)) for jj in range(2) for i in range(3)]
        w[U_MIX + 9 * jp + 6:U_MIX + 9 * jp + 9] = (
            np.concatenate(t, 1).reshape(P, 3, UNIT).transpose(1, 0, 2))
    for j in range(8):
        unit(U_OUT + j, w_out, P * j + np.arange(P))
    for j in range(32):
        unit(U_UP + j, w_up, P * j + np.arange(P))
    for j in range(8):
        m = cols(w_down, P * j + np.arange(P))
        for q in range(4):
            w[U_DN + 4 * j + q] = m[:, 8 * q:8 * q + 8].reshape(P, UNIT)
    return w


def sample_caches(cmp, sel, win, dil):
    n = len(cmp)
    out = {
        "cmp_pages": cmp.reshape(n, 8, JJ, 2, 2, G, DH).transpose(0, 3, 6, 4, 5, 2, 1
                                                                  ).reshape(n, P, 256),
        "sel_pages": np.concatenate([sel[:, :, 0].reshape(n, PAGE, P).transpose(0, 2, 1),
                                     sel[:, :, 1].reshape(n, PAGE, P)], 2),
        "win_k": win[:, :, 0].reshape(B, 512, P).transpose(0, 2, 1),
        "win_v": win[:, :, 1].reshape(B, 4, P, P).transpose(0, 2, 1, 3),
    }
    k, v = [], []
    for c, dilation in zip(dil, (1, 4, 16)):
        r = min(dilation, S)
        rows = c.reshape(B, 128, dilation, 2, 512)[:, :, :r].transpose(0, 2, 1, 3, 4)
        k.append(rows[:, :, :, 0].reshape(B, r * 128, 4, P).transpose(0, 3, 2, 1))
        v.append(rows[:, :, :, 1].transpose(0, 2, 1, 3))
    out["dil_k"] = np.concatenate(k, 3)
    out["dil_v"] = np.concatenate(v, 2)
    return out


class Chain:

    def __init__(self, eng, sem):
        self.eng, self.sem, self.n, self.base, self.per = eng, sem, 0, 0, 0

    def link(self, ins):
        self.n += 1
        ins.then_inc(self.sem, 1)
        self.wait()

    def count(self, ins):
        self.n += 1
        ins.then_inc(self.sem, 1)

    def wait(self):
        at = self.base + self.n
        hold(self.eng, self.sem, at)

    def enter(self, turn, per):
        self.start, self.per, self.base = self.n, per, turn * per

    def leave(self, turns):
        got = self.n - self.start
        assert got == self.per, f"a turn of {self.sem} has {got} counts"
        self.n += self.per * (turns - 1)
        self.base = 0


MET = [None, 32]


def hold(eng, sem, value):
    if not isinstance(value, int):
        eng.wait_ge(*MET)
    eng.wait_ge(sem, value)


def trunk(nc, t):
    ctx = ExitStack()
    with ctx:
        def sb(name, shape, stack=ctx, dt=F32):
            return stack.enter_context(nc.sbuf_tensor(name, shape, dt))

        def sem(name):
            return ctx.enter_context(nc.semaphore(name))

        banks = [ctx.enter_context(nc.psum_tensor(f"bank{i}", [P, 512], F32)) for i in range(8)]
        con = sb("con", [P, C_END])
        row = sb("row", [NS, R_END])
        norm_g = sb("norm_g", [P, 3, KD])
        hT = sb("hT", [P, KD, NT])
        oaT = sb("oaT", [P, R, NT])
        obT = sb("obT", [P, 4, NT])
        ocT = sb("ocT", [P, 4, NT])
        qaS = sb("qaS", [P, R, NS])
        kvS = sb("kvS", [P, 6, NS])
        qkS = sb("qkS", [P, 4, 9, NS])
        bgate = sb("bgate", [NS, B, 3])
        ident = con[:, C_ID:C_ID + P]
        ones = con[:, C_ONE:C_ONE + P]

        names = ("const_landed g_landed sq_ready ss_ready std_ready h_ready w_used "
                 "dve_chain act_chain bulk_done out_done store_done".split())
        sm = {n: sem(n) for n in names}
        x_landed = [sem(f"x_landed{k}") for k in range(KD)]
        w_landed = [sem(f"w_landed{i}") for i in range(RING)]
        MET[0] = sm["const_landed"]

        def ring_slot(wr, u):
            return wr[:, u % RING, :]

        class Track:
            put = 0

        bulk = [("dil3", b) for b in range(B)] + [("dil2", b) for b in range(B)] \
            + [("dil1", b) for b in range(B)] + [("win", b) for b in range(B)]
        sent = {"n": 0}

        def bulk_copies(eng, n):
            for name, b in bulk[sent["n"]:sent["n"] + n]:
                src, dst = t["cache_" + name], t["new_" + name]
                w, c = src.shape[1], src.shape[2]
                n_el = (w - S) * c
                if sent["n"] and sent["n"] % 2 == 0:
                    eng.wait_ge(sm["bulk_done"], 16 * sent["n"])
                eng.dma_start(
                    dst[b, 0:w - S, :].rearrange("w c -> (w c)").rearrange("(a n) -> a n", a=16),
                    src[b, S:w, :].rearrange("w c -> (w c)").rearrange("(a n) -> a n", a=16),
                ).then_inc(sm["bulk_done"], 16)
                sent["n"] += 1

        def load_units(sp, wr, u0, n):
            for u in range(u0, u0 + n):
                if u >= RING:
                    sp.wait_ge(sm["w_used"], u - RING + 1)
                sp.dma_start(ring_slot(wr, u), t["w"][u]).then_inc(w_landed[u % RING], 16)

        def unit_landed(eng, u, turn=0, per=0):
            hold(eng, w_landed[u % RING], turn * (per // RING * 16) + 16 * (u // RING + 1))

        pc = ExitStack()
        w1 = sb("w1", [P, 2, 16, HID], pc)
        w2 = sb("w2", [HID, 2, DH], pc)
        pe_t = sb("pe_t", [P, 2, 16], pc)
        b1 = sb("b1", [HID, 2], pc)
        bias = sb("bias", [HID, 2], pc)
        p1 = ExitStack()
        p12 = ExitStack()
        wr = sb("wring", [P, RING, UNIT], p12)
        qaT = sb("qaT", [P, R, SEQ], p12)
        kvT = sb("kvT", [P, 6, SEQ], p12)
        v_nat = sb("v_nat", [P, 2, NI, P], p12)
        gate_n = sb("gate_n", [P, NI, 24], p12)
        xT = sb("xT", [P, KD, NT], p1)

        def sq(k):
            return oaT[:, k, :] if k < 4 else obT[:, k - 4, :]

        rstd = sb("rstd", [P, NT], p1)
        gate_t = sb("gate_t", [24, NT], p1)
        uT = sb("uT", [P, 4, NT], p1)
        vn = sb("vn", [P, NI + 1, 512], p1)
        tmp = sb("tmp", [P, NT], p1)
        tmp2 = sb("tmp2", [P, NT], p1)
        stat = sb("stat", [P, 4], p1)
        ln_gb = sb("ln_gb", [P, 2, 512], p1)
        wsT = sb("wsT", [P, 8, P], p1)
        ws4 = sb("ws4", [NS, 8, NS], p1)
        bs = sb("bs", [2, 4, P + NS], p1)
        half = sb("half", [2, P], p1)
        newn = sb("newn", [NS, 4, P], p1)

        s_t_read = sem("t_read")
        s_t_readS = sem("t_readS")
        s_tr_ready = sem("tr_ready")
        s_tr_read = sem("tr_read")
        s_gexp = sem("gate_tanh")
        s_gate = sem("gate_ready")
        s_vz = sem("v_bank_ready")
        s_vz_read = sem("v_bank_read")
        s_gel1 = sem("gelu_square")
        s_gel2 = sem("gelu_inner")
        s_gel3 = sem("gelu_tanh")
        s_ln = sem("ln_centred")
        s_lnv = sem("ln_variance")
        s_v_ready = sem("v_ready")
        s_ws = sem("spatial_weights_ready")
        s_mix = sem("mixed_ready")
        s_mix_read = sem("mixed_read")
        s_rows = sem("gate_rows_landed")
        s_scr = sem("scratch_written")
        s_sgl = sem("sgu_landed")
        s_cw = sem("cmp_weights_landed")
        s_stat = sem("rows_written")

        def rms_act(act, ch, src, sqb, n, rstd, squares=True):
            for k in range(KD if squares else 0):
                act.activation(sqb(k), src[:, k, :], ACT.Square).then_inc(sm["sq_ready"], 1)
            act.wait_ge(sm["ss_ready"], n + 1)
            for hf in range(2):
                last = act.activation(rstd[:, HT * hf:HT * hf + HT], banks[hf][:, 0:HT], ACT.Sqrt,
                                      scale=1.0 / D, bias=con[:, C_EPS:C_EPS + 1])
            last.then_inc(sm["std_ready"], 1)

        def rms_pe(pe, sqb, n):
            for k in range(KD):
                pe.wait_ge(sm["sq_ready"], KD * n + k + 1)
                for hf in range(2):
                    last = pe.matmul(banks[hf][:, 0:HT], ones, sqb(k)[:, HT * hf:HT * hf + HT],
                                     start=(k == 0), stop=(k == KD - 1))
            last.then_inc(sm["ss_ready"], 1)

        def rms_dve(dve, ch, src, dst, n, rstd):
            dve.wait_ge(sm["std_ready"], n + 1)
            ch.link(dve.reciprocal(rstd[:, :], rstd[:, :]))
            for k in range(KD):
                dve.scalar_tensor_tensor(out=dst[:, k, :], in0=src[:, k, :],
                                         scalar=norm_g[:, n, k:k + 1], in1=rstd[:, :],
                                         op0=ALU.mult, op1=ALU.mult).then_inc(sm["h_ready"], 1)

        def t_tile(pe, wr, u, n, turn=0, per=0, m=P, rhs=None, banksP=(0, 1)):
            rhs = hT if rhs is None else rhs
            unit_landed(pe, u, turn, per)
            w = ring_slot(wr, u)
            for k in range(KD):
                pe.matmul(banks[banksP[n % 2]][0:m, :], w[:, k * P:k * P + m], rhs[:, k, 0:SEQ],
                          start=(k == 0), stop=(k == KD - 1))
            for k in range(KD):
                last = pe.matmul(banks[2 + n % 2][0:m, 0:NS], w[:, k * P:k * P + m],
                                 rhs[:, k, SEQ:NT], start=(k == 0), stop=(k == KD - 1))
            return last

        with nc.Block() as block:
            @block.sync
            def _(sp):
                sp.dma_start(con[:, 0:C_HEAD], t["con"][:, 0:C_HEAD]).then_inc(sm["const_landed"], 16)
                sp.dma_start(norm_g[:, :, :], t["norm_g"]).then_inc(sm["const_landed"], 16)
                for k in range(KD):
                    sp.dma_start(xT[:, k, :], t["xT"][:, k, :]).then_inc(x_landed[k], 16)
                load_units(sp, wr, 0, RING)
                sp.dma_start(con[:, C_HEAD:], t["con"][:, C_HEAD:]).then_inc(s_sgl, 16)
                sp.dma_start(row[:, :], t["row"]).then_inc(s_sgl, 16)
                sp.dma_start(ln_gb[:, 0, :], t["ln_g"].to_broadcast([P, 512])
                             ).then_inc(s_sgl, 16)
                sp.dma_start(ln_gb[:, 1, :], t["ln_b"].to_broadcast([P, 512])
                             ).then_inc(s_sgl, 16)
                sp.dma_start(wsT[:, :, :], t["wsT"]).then_inc(s_sgl, 16)
                sp.dma_start(ws4[:, :, :], t["ws4"]).then_inc(s_sgl, 16)
                sp.dma_start(bs[:, :, :], t["bs"]).then_inc(s_sgl, 16)
                sp.dma_start(half[:, :], t["half"]).then_inc(s_sgl, 16)
                load_units(sp, wr, RING, U_DIL - RING)
                sp.dma_start(w1[:, :, :, :], t["w1"]).then_inc(s_cw, 16)
                sp.dma_start(w2[:, :, :], t["w2"]).then_inc(s_cw, 16)
                sp.dma_start(pe_t[:, :, :], t["pe_t"]).then_inc(s_cw, 16)
                sp.dma_start(b1[:, :], t["b1"]).then_inc(s_cw, 16)
                sp.wait_ge(s_t_read, 10)
                sp.dma_start(t["kvT"], kvT[:, :, :]).then_inc(sm["out_done"], 16)
                sp.wait_ge(s_t_readS, 10)
                sp.dma_start(t["kvS"], kvS[:, :, :]).then_inc(sm["out_done"], 16)
                sp.wait_ge(s_gate, 1)
                sp.dma_start(t["scr_gate"], gate_t[:, SEQ:NT]).then_inc(s_scr, 16)
                sp.wait_ge(s_tr_read, 3)
                sp.dma_start(t["scr_v"], newn[:, 0:2, :]).then_inc(s_scr, 16)
                for i in range(2):
                    for b in range(B):
                        sp.dma_start(t["new_win"][b, 512 - S:512, P * i:P * i + P],
                                     newn[S * b:S * b + S, 2 + i, :]).then_inc(sm["store_done"], 16)
                sp.wait_ge(s_scr, 32)
                for g in range(G):
                    for s in range(S):
                        for b3 in range(3):
                            src = t["scr_gate"].rearrange("(g r c) (b s) -> g c s r b", g=G, r=R, s=S)
                            sp.dma_start(
                                bgate[g * 16 + s * 4:g * 16 + s * 4 + 4, :, b3:b3 + 1],
                                src[g, b3, s].rearrange("r (b o) -> r b o", o=1),
                                allow_slow_non_contiguous=True).then_inc(s_rows, 16)
                sp.wait_ge(s_v_ready, NI + 1)
                sp.dma_start(t["sgu_v"], vn[0:NS, NI, :]).then_inc(sm["out_done"], 16)
                sp.wait_ge(s_rows, 16 * 24)

            @block.gpsimd
            def _(pool):
                pool.wait_ge(s_sgl, 16 * 8)
                bulk_copies(pool, 4)

            @block.scalar
            def _(act):
                ch = Chain(act, sm["act_chain"])
                for k in range(KD):
                    act.wait_ge(x_landed[k], 16)
                    act.activation(sq(k), xT[:, k, :], ACT.Square).then_inc(sm["sq_ready"], 1)
                act.wait_ge(sm["const_landed"], 32)
                rms_act(act, ch, xT, sq, 0, rstd, squares=False)
                for n in range(10):
                    act.wait_ge(sm["w_used"], n + 1)
                    dst = qaT[:, n, :] if n < 4 else kvT[:, n - 4, :]
                    act.activation(dst, banks[n % 2][:, :], ACT.Copy).then_inc(s_t_read, 1)
                act.wait_ge(sm["w_used"], 11)
                act.activation(gate_t[:, 0:SEQ], banks[0][0:24, :], ACT.Tanh, scale=0.5)
                act.activation(gate_t[:, SEQ:NT], banks[2][0:24, 0:NS], ACT.Tanh,
                               scale=0.5).then_inc(s_t_read, 1)
                for n in range(4):
                    act.wait_ge(sm["w_used"], 12 + n)
                    if n:
                        act.wait_ge(s_gate, 1 + n)
                    bP, bS = banks[(11 + n) % 2], banks[2 + (11 + n) % 2]
                    act.activation(uT[:, n, 0:SEQ], bP[:, :], ACT.Copy)
                    act.activation(uT[:, n, SEQ:NT], bS[:, 0:NS], ACT.Copy)
                    act.activation(tmp[:, 0:SEQ], bP[:, :], ACT.Square)
                    act.activation(tmp[:, SEQ:NT], bS[:, 0:NS], ACT.Square).then_inc(s_t_read, 1)
                    act.wait_ge(s_gel2, n + 1)
                    act.activation(tmp2[:, :], tmp2[:, :], ACT.Tanh, scale=GELU_C).then_inc(s_gel3, 1)
                for i in range(NI + 1):
                    m = P if i < NI else NS
                    act.wait_ge(s_vz, i + 1)
                    act.wait_ge(s_gate, 5)
                    if i:
                        act.wait_ge(s_v_ready, i)
                    act.activation(vn[0:m, i, :], banks[4 + i % 2][0:m, :], ACT.Copy)
                    act.activation(tmp[0:m, 0:512], banks[4 + i % 2][0:m, :],
                                   ACT.Square).then_inc(s_vz_read, 1)
                    act.wait_ge(s_gel2, 5 + i)
                    act.activation(tmp2[0:m, 0:512], tmp2[0:m, 0:512], ACT.Tanh,
                                   scale=GELU_C).then_inc(s_gel3, 1)
                    act.wait_ge(s_ln, i + 1)
                    ch.link(act.activation(tmp[0:m, 0:512], vn[0:m, i, :], ACT.Square,
                                           accum_out=stat[0:m, 1:2]))
                    act.activation(stat[0:m, 2:3], stat[0:m, 1:2], ACT.Sqrt, scale=1.0 / 512,
                                   bias=con[0:m, C_EPS + 1:C_EPS + 2]).then_inc(s_lnv, 1)

            @block.vector
            def _(dve):
                ch = Chain(dve, sm["dve_chain"])
                dve.wait_ge(sm["const_landed"], 32)
                for k in range(KD):
                    dve.wait_ge(x_landed[k], 16)
                rms_dve(dve, ch, xT, hT, 0, rstd)
                for n in range(10):
                    dve.wait_ge(sm["w_used"], n + 1)
                    dst = qaS[:, n, :] if n < 4 else kvS[:, n - 4, :]
                    dve.tensor_copy(dst, banks[2 + n % 2][:, 0:NS]).then_inc(s_t_readS, 1)
                dve.wait_ge(s_t_read, 11)
                dve.tensor_scalar(gate_t[:, :], gate_t[:, :], 0.5, 0.5, ALU.mult,
                                  ALU.add).then_inc(s_gate, 1)
                dve.wait_ge(s_sgl, 16 * 8)
                for h in range(8):
                    dve.tensor_tensor(wsT[:, h, :], wsT[:, h, :], con[:, C_TRI:C_TRI + P], ALU.mult)
                    last = dve.tensor_tensor(ws4[:, h, :], ws4[:, h, :], row[:, R_SGU:R_SGU + NS],
                                             ALU.mult)
                last.then_inc(s_ws, 1)
                dve.wait_ge(s_tr_ready, 1)
                for j in range(2):
                    dve.tensor_copy(v_nat[:, j, :, :].rearrange("p i d -> p (i d)"),
                                    banks[6 + j][:, :]).then_inc(s_tr_read, 1)
                dve.wait_ge(s_tr_ready, 2)
                dve.tensor_copy(newn[:, :, :].rearrange("p i d -> p (i d)"),
                                banks[6][0:NS, :]).then_inc(s_tr_read, 1)
                dve.tensor_copy(gate_n[:, :, :], banks[7][:, 0:NI * 24].rearrange(
                    "p (i c) -> p i c", i=NI)).then_inc(s_tr_read, 1)

                def inner(x, m, w):
                    ch.link(dve.tensor_scalar(tmp2[0:m, 0:w], tmp[0:m, 0:w], GELU_A, 1.0, ALU.mult,
                                              ALU.add))
                    dve.tensor_tensor(tmp2[0:m, 0:w], tmp2[0:m, 0:w], x, ALU.mult).then_inc(s_gel2, 1)

                def outer(x, m, w):
                    return dve.scalar_tensor_tensor(out=x, in0=tmp2[0:m, 0:w], scalar=1.0, in1=x,
                                                    op0=ALU.add, op1=ALU.mult)

                for n in range(4):
                    dve.wait_ge(s_t_read, 12 + n)
                    inner(uT[:, n, :], P, NT)
                    dve.wait_ge(s_gel3, n + 1)
                    outer(uT[:, n, :], P, NT).then_inc(s_gate, 1)
                for i in range(NI + 1):
                    m = P if i < NI else NS
                    v = vn[0:m, i, :]
                    dve.wait_ge(s_vz_read, i + 1)
                    inner(v, m, 512)
                    dve.wait_ge(s_gel3, 5 + i)
                    ch.link(outer(v, m, 512))
                    ch.link(dve.tensor_scalar(v, v, 0.5, None, ALU.mult))
                    ch.link(dve.tensor_reduce(stat[0:m, 0:1], v, AX.X, ALU.add))
                    ch.link(dve.tensor_scalar(stat[0:m, 0:1], stat[0:m, 0:1], 1.0 / 512, None,
                                              ALU.mult))
                    dve.tensor_scalar(v, v, stat[0:m, 0:1], None, ALU.subtract).then_inc(s_ln, 1)
                    dve.wait_ge(s_lnv, i + 1)
                    ch.link(dve.reciprocal(stat[0:m, 3:4], stat[0:m, 2:3]))
                    ch.link(dve.scalar_tensor_tensor(out=v, in0=v, scalar=stat[0:m, 3:4],
                                                     in1=ln_gb[0:m, 0, :], op0=ALU.mult,
                                                     op1=ALU.mult))
                    dve.tensor_tensor(v, v, ln_gb[0:m, 1, :], ALU.add).then_inc(s_v_ready, 1)
                for n in range(4):
                    dve.wait_ge(s_mix, n + 1)
                    dve.scalar_tensor_tensor(out=ocT[:, n, 0:SEQ], in0=banks[n % 2][:, :], scalar=0.5,
                                             in1=uT[:, n, 0:SEQ], op0=ALU.mult, op1=ALU.mult)
                    dve.scalar_tensor_tensor(out=ocT[:, n, SEQ:NT], in0=banks[2 + n % 2][:, 0:NS],
                                             scalar=0.5, in1=uT[:, n, SEQ:NT], op0=ALU.mult,
                                             op1=ALU.mult).then_inc(s_mix_read, 1)

            @block.tensor
            def _(pe):
                pe.wait_ge(sm["const_landed"], 32)
                rms_pe(pe, sq, 0)
                pe.wait_ge(sm["h_ready"], KD)
                for n in range(15):
                    if n >= 2:
                        pe.wait_ge(s_t_read, n - 1)
                        pe.wait_ge(s_t_readS, min(n - 1, 10))
                    m = 24 if n == 10 else P
                    last = t_tile(pe, wr, n, n, m=m)
                    last.then_inc(sm["w_used"], 1)
                    if n == 11:
                        pe.wait_ge(s_t_read, 10)
                        for j, kv in enumerate((3, 5)):
                            for i in range(NI):
                                last = pe.transpose(banks[6 + j][:, i * P:i * P + P],
                                                    kvT[:, kv, i * P:i * P + P], ident)
                        last.then_inc(s_tr_ready, 1)
                        pe.wait_ge(s_tr_read, 2)
                        for j, kv in enumerate((3, 5, 4, 5)):
                            pe.transpose(banks[6][0:NS, j * P:j * P + P], kvS[:, kv, :], ident)
                        pe.wait_ge(s_gate, 1)
                        for i in range(NI):
                            last = pe.transpose(banks[7][:, i * 24:i * 24 + 24],
                                                gate_t[:, i * P:i * P + P], ident[0:24, 0:24])
                        last.then_inc(s_tr_ready, 1)
                for i in range(NI + 1):
                    m = P if i < NI else NS
                    if i >= 2:
                        pe.wait_ge(s_vz_read, i - 1)
                    for k in range(KD):
                        if i == 0 and k % 2 == 0:
                            unit_landed(pe, U_V + k // 2)
                        w = ring_slot(wr, U_V + k // 2)
                        last = pe.matmul(banks[4 + i % 2][0:m, :], hT[:, k, i * P:i * P + m],
                                         w[:, (k % 2) * 512:(k % 2) * 512 + 512],
                                         start=(k == 0), stop=(k == KD - 1))
                        if i == NI and k % 2 and k < KD - 1:
                            last.then_inc(sm["w_used"], 1)
                    last.then_inc(s_vz, 1)
                pe.wait_ge(s_ws, 1)
                pe.wait_ge(s_v_ready, NI + 1)
                for n in range(4):
                    if n >= 2:
                        pe.wait_ge(s_mix_read, n - 1)
                    else:
                        pe.wait_ge(s_t_read, 15)
                    bP, bS = banks[n % 2], banks[2 + n % 2]
                    for c in range(NI + 1):
                        m = P if c < NI else NS
                        dst = bP[:, c * P:c * P + P] if c < NI else bS[:, 0:NS]
                        bb = bs[:, n, 0:P] if c < NI else bs[:, n, P:P + NS]
                        mm = pe.matmul(dst, half[:, :], bb, start=True, stop=False)
                        if n == 0 and c == 0:
                            mm.then_inc(sm["w_used"], 1)
                        for hh in range(2):
                            h = 2 * n + hh
                            w = wsT[:, h, :] if c < NI else ws4[:, h, :]
                            last = pe.matmul(dst[hh * DH:hh * DH + DH, :],
                                             vn[0:m, c, h * DH:h * DH + DH], w, start=False,
                                             stop=True)
                    last.then_inc(s_mix, 1)
        p1.close()
        s_bias = sem("cmp_bias_summed")
        s_bias2 = sem("cmp_bias_ready")
        s_cx = sem("cmp_rows_ready")
        s_hid = sem("cmp_hidden_summed")
        s_c1 = sem("cmp_first_half")
        s_c2 = sem("cmp_joined")
        s_c3 = sem("cmp_square")
        s_c4 = sem("cmp_inner")
        s_c5 = sem("cmp_tanh")
        s_c6 = sem("cmp_gelu")
        s_ck = sem("cmp_kv_summed")
        s_ckr = sem("cmp_kv_ready")
        s_kk = sem("sample_cmp_k_summed")
        s_kkr = sem("sample_cmp_k_ready")

        def hidden_pe(pe, cx, nseg, kv, n0):
            if kv:
                hold(pe, s_c2, n0 + 1)
            for hf in range(2):
                for jj in range(JJ):
                    last = pe.matmul(
                        banks[hf][:, 0:G * nseg].rearrange("p (g a s) -> p g a s", g=G, s=8),
                        w1[:, kv, 8 * hf + jj, :],
                        cx[:, :, 2 * kv:2 * kv + 2, jj, :].rearrange("p a g s -> p g a s"),
                        start=(jj == 0), stop=(jj == JJ - 1))
            last.then_inc(s_hid, 1)

        def second_pe(pe, nseg, hidT, n0):
            hold(pe, s_c6, n0 + 2)
            n = nseg - 1
            for g in range(G):
                pe.matmul(banks[0][g * DH:g * DH + DH, 0:n], w2[:, 0, :], hidT[:, 0, g, 0:n],
                          start=True, stop=True)
            for c in range(-(-n // P)):
                m = min(P, n - c * P)
                for g in range(G):
                    last = pe.matmul(banks[1][0:m, c * P + g * DH:c * P + g * DH + DH],
                                     hidT[:, 1, g, c * P:c * P + m], w2[:, 1, :], start=True, stop=True)
            last.then_inc(s_ck, 1)

        def second_k_pe(pe, hidT, n0):
            hold(pe, s_c6, n0 + 1)
            for g in range(G):
                last = pe.matmul(banks[5][g * DH:g * DH + DH, 0:NC_S], w2[:, 0, :],
                                 hidT[:, 0, g, 0:NC_S], start=True, stop=True)
            last.then_inc(s_kk, 1)

        def second_v_pe(pe, hidT, n0):
            hold(pe, s_c6, n0 + 2)
            for c, m in enumerate((P, NC_S - P)):
                for g in range(G):
                    last = pe.matmul(banks[7][0:m, c * P + g * DH:c * P + g * DH + DH],
                                     hidT[:, 1, g, c * P:c * P + m], w2[:, 1, :], start=True,
                                     stop=True)
            last.then_inc(s_ck, 1)

        def hidden_act(act, nseg, hidT, sqT, kv, n0):
            hold(act, s_hid, n0 + kv + 1)
            act.activation(hidT[:, kv, :, 0:nseg],
                           banks[0][:, 0:G * nseg].rearrange("p (g s) -> p g s", g=G),
                           ACT.Identity, bias=bias[:, kv:kv + 1]).then_inc(s_c1, 1)
            hold(act, s_c2, n0 + kv + 1)
            act.activation(sqT[:, kv, :, 0:nseg - 1], hidT[:, kv, :, 0:nseg - 1],
                           ACT.Square).then_inc(s_c3, 1)

        def tanh_act(act, nseg, inT, kv, n0):
            hold(act, s_c4, n0 + kv + 1)
            act.activation(inT[:, kv, :, 0:nseg - 1], inT[:, kv, :, 0:nseg - 1], ACT.Tanh,
                           scale=GELU_C).then_inc(s_c5, 1)

        def join_dve(dve, nseg, hidT, kv, n0):
            hold(dve, s_c1, n0 + kv + 1)
            h = hidT[:, kv, :, 0:nseg - 1]
            dve.tensor_tensor(h, h, banks[1][:, 0:G * nseg].rearrange(
                "p (g s) -> p g s", g=G)[:, :, 1:nseg], ALU.add).then_inc(s_c2, 1)

        def inner_dve(dve, ch, nseg, hidT, sqT, inT, kv, n0):
            n = nseg - 1
            h, q, i = hidT[:, kv, :, 0:n], sqT[:, kv, :, 0:n], inT[:, kv, :, 0:n]
            hold(dve, s_c3, n0 + kv + 1)
            ch.link(dve.tensor_scalar(q, q, GELU_A, 1.0, ALU.mult, ALU.add))
            dve.tensor_tensor(i, q, h, ALU.mult).then_inc(s_c4, 1)

        def outer_dve(dve, nseg, hidT, inT, kv, n0):
            h, i = hidT[:, kv, :, 0:nseg - 1], inT[:, kv, :, 0:nseg - 1]
            hold(dve, s_c5, n0 + kv + 1)
            dve.scalar_tensor_tensor(out=h, in0=i, scalar=1.0, in1=h, op0=ALU.add,
                                     op1=ALU.mult).then_inc(s_c6, 1)

        def compress_act(act, nseg, hidT, sqT, inT, n0):
            for kv in range(2):
                hidden_act(act, nseg, hidT, sqT, kv, n0)
            for kv in range(2):
                tanh_act(act, nseg, inT, kv, n0)

        def compress_dve(dve, ch, nseg, hidT, sqT, inT, n0):
            for kv in range(2):
                join_dve(dve, nseg, hidT, kv, n0)
            for kv in range(2):
                inner_dve(dve, ch, nseg, hidT, sqT, inT, kv, n0)
            for kv in range(2):
                outer_dve(dve, nseg, hidT, inT, kv, n0)

        s_sc = sem("scores_ready")
        s_sread = sem("scores_read")
        s_mx = sem("maxima_ready")
        s_exp = sem("exp_ready")
        s_prob = sem("probs_ready")
        s_tp = sem("probsT_bank_ready")
        s_ptc = sem("probsT_ready")
        s_pv = sem("block_summed")
        s_att = sem("turn_finished")
        NBLK = 2 * NI
        PBUF = 3
        BLOCKS = [(hh, i) for hh in range(2) for i in range(NI)]

        def att_pe(pe, turn, base, q, kA, kB, kC, vA, vB, vC, widths):
            hold(pe, s_att, turn + base // NBLK + 1)

            def at(k):
                return turn * NBLK + base + k

            def scores(n):
                hh, i = BLOCKS[n]
                r0 = hh * DH
                if n >= 2:
                    hold(pe, s_sread, at(n - 1))
                w, wc = widths(i)
                lhs = [x[r0:r0 + DH, i * P:i * P + P] for x in q]
                pe.matmul(banks[n % 2][:, 0:w], lhs[0], kA[r0:r0 + DH, 0:w], start=True, stop=True)
                pe.matmul(banks[2 + n % 2][:, 0:w], lhs[1], kB[r0:r0 + DH, 0:w], start=True, stop=True)
                if n:
                    hold(pe, s_sread, at(n))
                pe.matmul(banks[4][:, 0:wc], lhs[2], kC(r0, i),
                          start=True, stop=True).then_inc(s_sc, 1)

            def flip(n):
                hh, i = BLOCKS[n]
                w, wc = widths(i)
                T, offB, offC = att_T[n % PBUF], *offs(w)
                hold(pe, s_prob, at(n + 1))
                if n >= 1:
                    hold(pe, s_ptc, (turn * NBLK + base) * 3 + 3 * n)
                for bank, off in ((5, 0), (6, offB)):
                    for kt in range(i + 1):
                        last = pe.transpose(banks[bank][:, kt * P:kt * P + P],
                                            T[:, off + kt * P:off + kt * P + P], ident)
                    last.then_inc(s_tp, 1)
                hold(pe, s_ptc, (turn * NBLK + base) * 3 + 3 * n + 1)
                for c in range(-(-wc // P)):
                    m = min(P, wc)
                    last = pe.transpose(banks[5][0:m, c * P:c * P + P],
                                        T[:, offC + c * P:offC + c * P + m], ident)
                last.then_inc(s_tp, 1)

            def values(n):
                hh, i = BLOCKS[n]
                w, wc = widths(i)
                hold(pe, s_ptc, (turn * NBLK + base) * 3 + 3 * n + 3)
                pT = att_pT[n % 2]
                o = banks[7][hh * DH:hh * DH + DH, i * P:i * P + P]
                for kt in range(i + 1):
                    pe.matmul(o, vA(hh, kt), pT[:, kt * P:kt * P + P], start=(kt == 0), stop=False)
                for kt in range(i + 1):
                    pe.matmul(o, vB(hh, kt), pT[:, 512 + kt * P:512 + kt * P + P], start=False,
                              stop=False)
                nC = -(-wc // P)
                for c in range(nC):
                    m = min(P, wc)
                    last = pe.matmul(o, vC(hh, i, c), pT[0:m, 1024 + c * P:1024 + c * P + P],
                                     start=False, stop=(c == nC - 1))
                last.then_inc(s_pv, 1)

            scores(0)
            scores(1)
            for n in range(NBLK):
                if n + 2 < NBLK:
                    scores(n + 2)
                flip(n)
                if n:
                    values(n - 1)
            values(NBLK - 1)

        def att_act(act, turn, base, widths, nsa, dst):
            def at(k):
                return turn * NBLK + base + k

            def exps(n):
                hh, i = BLOCKS[n]
                w, wc = widths(i)
                T, offB, offC = att_T[n % PBUF], *offs(w)
                hold(act, s_mx, at(n + 1))
                if nsa:
                    for k, (o, ww) in enumerate(((offC, wc), (0, w), (offB, w))):
                        last = act.activation(T[:, o:o + ww], T[:, o:o + ww], ACT.Exp, scale=SCALE,
                                              bias=att_m[:, n % PBUF, k:k + 1],
                                              accum_out=att_d[:, n % PBUF, k:k + 1])
                else:
                    last = act.activation(T[:, 0:offC + wc], T[:, 0:offC + wc], ACT.Exp, scale=SCALE,
                                          bias=att_m[:, n % PBUF, 0:1], accum_out=att_d[:, n % PBUF, 0:1])
                last.then_inc(s_exp, 1)

            def copies(n):
                hh, i = BLOCKS[n]
                w, wc = widths(i)
                pT = att_pT[n % 2]
                if n >= 2:
                    hold(act, s_pv, at(n - 1))
                t0 = (turn * NBLK + base) * 3 + 3 * n
                for k in range(2):
                    hold(act, s_tp, t0 + k + 1)
                    act.activation(pT[:, 512 * k:512 * k + w], banks[5 + k][:, 0:w],
                                   ACT.Copy).then_inc(s_ptc, 1)
                hold(act, s_tp, t0 + 3)
                m, nC = min(P, wc), -(-wc // P)
                act.activation(pT[0:m, 1024:1024 + nC * P], banks[5][0:m, 0:nC * P],
                               ACT.Copy).then_inc(s_ptc, 1)

            exps(0)
            for n in range(NBLK):
                if n + 1 < NBLK:
                    exps(n + 1)
                copies(n)
            hold(act, s_pv, at(NBLK))
            act.activation(dst, banks[7][:, :], ACT.Copy).then_inc(s_att, 1)

        def att_dve(dve, ch, turn, base, widths, nsa, masks, gate=None):
            def at(k):
                return turn * NBLK + base + k

            def mask(n):
                hh, i = BLOCKS[n]
                w, wc = widths(i)
                T, offB, offC = att_T[n % PBUF], *offs(w)
                hold(dve, s_sc, at(n + 1))
                if n >= PBUF:
                    hold(dve, s_tp, (turn * NBLK + base) * 3 + 3 * (n - PBUF + 1))
                mA, mB, mC = masks(i)
                ch.count(dve.tensor_tensor(T[:, 0:w], banks[n % 2][:, 0:w], mA, ALU.add))
                ch.count(dve.tensor_tensor(T[:, offB:offB + w], banks[2 + n % 2][:, 0:w], mB, ALU.add))
                dve.tensor_tensor(T[:, offC:offC + wc], banks[4][:, 0:wc], mC,
                                  ALU.add).then_inc(s_sread, 1)
                hold(dve, s_sread, at(n + 1))
                m = att_m[:, n % PBUF, :]
                if nsa:
                    ch.count(dve.tensor_reduce(m[:, 0:1], T[:, offC:offC + wc], AX.X, ALU.max))
                    ch.count(dve.tensor_reduce(m[:, 1:2], T[:, 0:w], AX.X, ALU.max))
                    ch.link(dve.tensor_reduce(m[:, 2:3], T[:, offB:offB + w], AX.X, ALU.max))
                else:
                    ch.link(dve.tensor_reduce(m[:, 0:1], T[:, 0:offC + wc], AX.X, ALU.max))
                k = 3 if nsa else 1
                dve.tensor_scalar(m[:, 0:k], m[:, 0:k], -SCALE, None, ALU.mult).then_inc(s_mx, 1)

            def norm(n):
                hh, i = BLOCKS[n]
                w, wc = widths(i)
                T, offB, offC = att_T[n % PBUF], *offs(w)
                d = att_d[:, n % PBUF, :]
                hold(dve, s_exp, at(n + 1))
                if not nsa:
                    ch.link(dve.reciprocal(d[:, 0:1], d[:, 0:1]))
                    dve.tensor_scalar(T[:, 0:offC + wc], T[:, 0:offC + wc], d[:, 0:1], None,
                                      ALU.mult).then_inc(s_prob, 1)
                    return
                ok = con[:, C_CMV + 32 * i:C_CMV + 32 * i + wc]
                ch.link(dve.tensor_tensor(T[:, offC:offC + wc], T[:, offC:offC + wc], ok, ALU.mult))
                ch.link(dve.tensor_reduce(d[:, 0:1], T[:, offC:offC + wc], AX.X, ALU.add))
                ch.link(dve.tensor_scalar(d[:, 0:1], d[:, 0:1], 1e-30, None, ALU.max))
                ch.link(dve.reciprocal(d[:, 0:3], d[:, 0:3]))
                ch.link(dve.tensor_tensor(d[:, 0:3], d[:, 0:3], gate(hh, i), ALU.mult))
                for k, (o, ww) in enumerate(((offC, wc), (0, w), (offB, w))):
                    last = dve.tensor_scalar(T[:, o:o + ww], T[:, o:o + ww], d[:, k:k + 1], None,
                                             ALU.mult)
                    if k < 2:
                        ch.count(last)
                last.then_inc(s_prob, 1)

            mask(0)
            mask(1)
            for n in range(NBLK):
                norm(n)
                if n + 2 < NBLK:
                    mask(n + 2)

        def offs(w):
            return w, 2 * w

        p2 = ExitStack()
        att_T = [sb(f"att_T{i}", [P, 1280], p2) for i in range(PBUF)]
        att_pT = [sb(f"att_pT{i}", [P, 1280], p2) for i in range(2)]
        att_m = sb("att_m", [P, PBUF, 3], p2)
        att_d = sb("att_d", [P, PBUF, 3], p2)
        cxp = sb("cxp", [P, SEQ // P, 4, JJ, 8], p2)
        nsegp = SEQ // 16
        hidp = sb("hidp", [HID, 2, G, nsegp], p2)
        sqp = sb("sqp", [HID, 2, G, nsegp], p2)
        inp = sb("inp", [HID, 2, G, nsegp], p2)
        kcP = sb("kcP", [P, NC_P], p2)
        vcP = sb("vcP", [NC_P, P], p2)
        qslot = sb("qslot", [P, SEQ], p2)
        s_q = sem("q_slot_ready")

        def nsa_widths(i):
            return P * (i + 1), NC_P

        with nc.Block() as block:
            @block.sync
            def _(sp):
                load_units(sp, wr, U_DIL, RING)

            @block.gpsimd
            def _(pool):
                bulk_copies(pool, 4)

            @block.scalar
            def _(act):
                act.sem_inc(s_att, 1)
                compress_act(act, nsegp, hidp, sqp, inp, 0)
                act.wait_ge(s_ck, 1)
                act.activation(kcP[:, :], banks[0][:, 0:NC_P], ACT.Copy, scale=0.5)
                act.activation(vcP[:, :], banks[1][0:NC_P, 0:P], ACT.Copy, scale=0.5).then_inc(s_ckr, 1)
                with act.Fori(0, R) as r:
                    hold(act, s_att, r + 1)
                    act.activation(qslot[:, :], qaT[:, bass.ds(r, 1), :].rearrange("p o q -> p (o q)"),
                                   ACT.Copy).then_inc(s_q, 1)
                    att_act(act, r, 0, nsa_widths, True,
                            oaT[:, bass.ds(r, 1), 0:SEQ].rearrange("p o q -> p (o q)"))

            @block.vector
            def _(dve):
                ch = Chain(dve, sem("dve_chain2"))
                for kv in range(2):
                    for g in range(G):
                        for j2 in range(2):
                            src = kvT[g * DH:g * DH + DH, kv, :].rearrange(
                                "p (a s j t) -> p t a j s", a=SEQ // P, s=8, t=2)[:, j2]
                            last = dve.tensor_copy(cxp[j2 * DH:j2 * DH + DH, :, 2 * kv + g, :, :], src)
                last.then_inc(s_cx, 1)
                dve.wait_ge(s_bias, 1)
                dve.wait_ge(s_cw, 64)
                ch.link(dve.tensor_tensor(bias[:, :], banks[7][:, 0:2], b1[:, :], ALU.add))
                dve.sem_inc(s_bias2, 1)
                compress_dve(dve, ch, nsegp, hidp, sqp, inp, 0)
                with dve.Fori(0, R) as r:
                    ch.enter(r, 96)
                    att_dve(dve, ch, r, 0, nsa_widths, True,
                            lambda i: (con[:, C_MC + 384 - P * i:C_MC + 512],
                                       con[:, C_MC + 384 - P * i:C_MC + 512],
                                       con[:, C_CMP + 32 * i:C_CMP + 32 * i + NC_P]),
                            gate=lambda g, i: gate_n[:, i, bass.ds(r * 3 + g * 12, 3)])
                ch.leave(R)

            @block.tensor
            def _(pe):
                pe.wait_ge(s_cw, 64)
                for kv in range(2):
                    for j in range(16):
                        last = pe.matmul(banks[7][:, kv:kv + 1], w1[:, kv, j, :], pe_t[:, kv, j:j + 1],
                                         start=(j == 0), stop=(j == 15))
                last.then_inc(s_bias, 1)
                pe.wait_ge(s_cx, 1)
                pe.wait_ge(s_bias2, 1)
                for kv in range(2):
                    hidden_pe(pe, cxp, nsegp, kv, 0)
                second_pe(pe, nsegp, hidp, 0)
                pe.wait_ge(s_ckr, 1)
                with pe.Fori(0, R) as r:
                    hold(pe, s_q, r + 1)
                    att_pe(pe, r, 0, (qslot,) * 3, kvT[:, 2, :], kvT[:, 4, :],
                           lambda r0, i: kcP[r0:r0 + DH, :],
                           lambda g, kt: v_nat[:, 0, kt, g * DH:g * DH + DH],
                           lambda g, kt: v_nat[:, 1, kt, g * DH:g * DH + DH],
                           lambda g, i, c: vcP[:, g * DH:g * DH + DH], nsa_widths)

        p3 = ExitStack()
        dq = sb("dq", [P, 9, SEQ], p3)
        dqS = sb("dqS", [P, 9, NS], p3)
        dv = sb("dv", [P, 3, SEQ], p3)
        newd = sb("newd", [NS, 6, P], p3)
        s_dr = sem("dil_tile_copied")
        s_drS = sem("dil_sample_copied")
        s_dtr = sem("dil_transposes_ready")
        s_dtc = sem("dil_transposes_copied")
        s_dout = sem("dil_outputs_landed")
        OUTS_PER_TURN = 16 * (1 + 6)

        def dil_widths(i):
            return P * (i + 1), P * min(2, i + 1)

        with nc.Block() as block:
            @block.sync
            def _(sp):
                def turn_io(p, more):
                    if more:
                        for n in range(RING):
                            hold(sp, sm["w_used"], p * 9 + U_DIL + n + 1)
                            sp.dma_start(ring_slot(wr, U_DIL + n),
                                         t["w"][bass.ds(p * 9 + U_DIL + 9 + n, 1)].rearrange(
                                             "o p n -> (o p) n")
                                         ).then_inc(w_landed[(U_DIL + n) % RING], 16)
                    hold(sp, s_dr, p * 9 + 9)
                    sp.dma_start(t["dilT"][bass.ds(p, 1)].rearrange("o p g q -> (o p) g q"),
                                 dq[:, 3:9, :]).then_inc(s_dout, 16)
                    hold(sp, s_dtc, p * 2 + 2)
                    for g in range(3):
                        w = WINS[g]
                        for kv in range(2):
                            sp.dma_start(
                                t[f"new_dil{g + 1}"].rearrange("b w (k p c) -> b w k p c", k=2, p=4)[
                                    :, w - S:w, kv, bass.ds(p, 1), :].rearrange("b w o c -> b w (o c)"),
                                newd[:, 3 * kv + g, :]).then_inc(s_dout, 16)
                with sp.Fori(0, 3) as p:
                    turn_io(p, True)
                turn_io(3, False)
                sp.wait_ge(s_dout, 5 * OUTS_PER_TURN)

            @block.gpsimd
            def _(pool):
                bulk_copies(pool, 8)

            @block.scalar
            def _(act):
                act.sem_inc(s_dout, OUTS_PER_TURN)
                with act.Fori(0, 4) as p:
                    hold(act, s_dout, (p + 1) * OUTS_PER_TURN)
                    for n in range(9):
                        hold(act, sm["w_used"], p * 9 + U_DIL + n + 1)
                        act.activation(dq[:, n, :], banks[n % 2][:, :], ACT.Copy).then_inc(s_dr, 1)
                    att_act(act, p, R * NBLK, dil_widths, False,
                            obT[:, bass.ds(p, 1), 0:SEQ].rearrange("p o q -> p (o q)"))

            @block.vector
            def _(dve):
                ch = Chain(dve, sem("dve_chain3"))
                with dve.Fori(0, 4) as p:
                    ch.enter(p, 34)
                    hold(dve, s_dout, (p + 1) * OUTS_PER_TURN)
                    for n in range(9):
                        hold(dve, sm["w_used"], p * 9 + U_DIL + n + 1)
                        dve.tensor_copy(dqS[:, n, :], banks[2 + n % 2][:, 0:NS]).then_inc(s_drS, 1)
                    hold(dve, s_drS, p * 9 + 9)
                    ch.count(dve.tensor_copy(
                        qkS[:, bass.ds(p, 1), :, :].rearrange("p o n q -> p (o n q)"),
                        dqS[:, :, :].rearrange("p n q -> p (n q)")))
                    hold(dve, s_dtr, p * 2 + 1)
                    for g in range(3):
                        last = dve.tensor_copy(dv[:, g, :], banks[5 + g][:, :])
                    last.then_inc(s_dtc, 1)
                    hold(dve, s_dtr, p * 2 + 2)
                    ch.count(dve.tensor_copy(newd[:, 0:4, :].rearrange("p n c -> p (n c)"),
                                             banks[4][0:NS, :]))
                    dve.tensor_copy(newd[:, 4:6, :].rearrange("p n c -> p (n c)"),
                                    banks[0][0:NS, 0:256]).then_inc(s_dtc, 1)
                    att_dve(dve, ch, p, R * NBLK, dil_widths, False,
                            lambda i: (con[:, C_M4 + 384 - P * i:C_M4 + 512],
                                       con[:, C_M16 + 384 - P * i:C_M16 + 512],
                                       con[:, C_M1 + (P if i == 0 else 0):C_M1 + 256]))
                ch.leave(4)

            @block.tensor
            def _(pe):
                with pe.Fori(0, 4) as p:
                    hold(pe, s_att, p + R + 1)
                    for n in range(9):
                        if n >= 2:
                            hold(pe, s_dr, p * 9 + n - 1)
                            hold(pe, s_drS, p * 9 + n - 1)
                        t_tile(pe, wr, U_DIL + n, n, p, 9).then_inc(sm["w_used"], 1)
                    hold(pe, s_dr, p * 9 + 9)
                    for g in range(3):
                        for i in range(NI):
                            last = pe.transpose(banks[5 + g][:, i * P:i * P + P],
                                                dq[:, 6 + g, i * P:i * P + P], ident)
                    last.then_inc(s_dtr, 1)
                    hold(pe, s_drS, p * 9 + 9)
                    for n in range(6):
                        bank = banks[4] if n < 4 else banks[0]
                        last = pe.transpose(bank[0:NS, (n % 4) * P:(n % 4) * P + P], dqS[:, 3 + n, :],
                                            ident)
                    last.then_inc(s_dtr, 1)
                    hold(pe, s_dtc, p * 2 + 2)

                    def first(i):
                        return max(0, i - 1)

                    att_pe(pe, p, R * NBLK, (dq[:, 1, :], dq[:, 2, :], dq[:, 0, :]), dq[:, 4, :],
                           dq[:, 5, :], lambda r0, i: dq[r0:r0 + DH, 3, first(i) * P:(i + 1) * P],
                           lambda hh, kt: dv[:, 1, kt * P + hh * DH:kt * P + hh * DH + DH],
                           lambda hh, kt: dv[:, 2, kt * P + hh * DH:kt * P + hh * DH + DH],
                           lambda hh, i, c: dv[:, 0, (first(i) + c) * P + hh * DH:
                                               (first(i) + c) * P + hh * DH + DH], dil_widths)
        p3.close()
        p2.close()
        p12.close()
        p4 = ExitStack()
        cx = sb("cx", [P, PAGES, 4, JJ, 8], p4)
        sx = sb("sx", [P, PAGES, 2, P], p4)
        wk = sb("wk", [P, 512], p4)
        wv = sb("wv", [P, 4, P], p4)
        vnew = sb("vnew", [2 * S, P], p4)
        pt = sb("pt", [1, B * PAGES], p4, I32)
        T_NEW, T_WIN = PAST, PAST + 2 * S
        T_CMP = T_WIN + 512
        T = sb("T", [NS, T_CMP + NC_S], p4)
        NCH = 32 + 4 + 2 + 1
        pT = sb("pT", [P, NCH * NS], p4)
        hid = sb("hid", [HID, 2, G, NSEG], p4)
        hsq = sb("hsq", [HID, 2, G, NSEG], p4)
        hin = sb("hin", [HID, 2, G, NSEG], p4)
        kcT = sb("kcT", [P, NC_S], p4)
        vc = sb("vc", [P, 2, P], p4)
        qb = sb("qb", [P, NS], p4)
        imp = sb("imp", [NS, NSEG + 1], p4)
        score = sb("score", [NS, NB], p4)
        part = sb("part", [NS, NB], p4)
        best = sb("best", [NS, 8], p4)
        mt = sb("mt", [NS, 3], p4)
        dn = sb("dn", [NS, 3], p4)
        om = sb("om", [NS, P], p4)
        s_pt = sem("page_table_landed")
        s_turn = sem("page_loads_begun")
        s_turn2 = sem("pool_page_loads_begun")
        s_cL = [sem("cmp_pages_landed"), sem("cmp_pages_landed_pool")]
        s_sL = [[sem("sel_keys_landed"), sem("sel_keys_landed_pool")],
                [sem("sel_values_landed"), sem("sel_values_landed_pool")]]
        s_wk = sem("window_keys_landed")
        s_wL = sem("window_values_landed")
        s_qb = sem("request_queries_ready")
        s_a = sem("small_scores_ready")
        s_ar = sem("small_scores_read")
        s_ce = sem("cmp_exp_ready")
        s_cm = sem("cmp_maximum_ready")
        s_pc = sem("cmp_probs_ready")
        s_im = sem("importance_ready")
        s_s = sem("sel_scores_ready")
        s_sr = sem("sel_scores_read")
        s_sm = sem("sel_maximum_ready")
        s_se = sem("sel_exp_ready")
        s_sp = sem("sel_probs_ready")
        s_ft = sem("sel_probsT_bank_ready")
        s_fc = sem("sel_probsT_ready")
        s_v = sem("request_summed")
        s_om = sem("request_masked")
        s_os = sem("request_spread")
        s_or = sem("request_finished")
        SBANK = [2, 3, 4, 5, 2, 3, 4, 5]
        N0 = 2

        SHARE = 20

        def pages_landed(eng, sems, requests):
            hold(eng, sems[0], requests * 16 * SHARE)
            hold(eng, sems[1], requests * 16 * (PAGES - SHARE))

        class Pages:

            def __init__(self, eng, engine, who, turns):
                self.eng, self.engine, self.who, self.turns = eng, engine, who, turns
                self.lo = SHARE * who
                self.hi = (SHARE, PAGES)[who]

            def numbers(self, b, n):
                return enumerate(nc.values_load_multi_w_load_instructions(
                    pt[0:1, bass.ds(b * PAGES + self.lo, self.hi - self.lo)],
                    engines=(self.engine,), min_val=0, max_val=n - 1)[1], self.lo)

            def cmp(self, b):
                for i, page in self.numbers(b, t["cmp_pages"].shape[0]):
                    self.eng.dma_start(
                        cx[:, i, :, :, :].rearrange("p g j s -> p (g j s)"),
                        t["cmp_pages"][bass.ds(page, 1)].rearrange("o p n -> (o p) n")
                    ).then_inc(s_cL[self.who], 16)

            def sel(self, b, kv):
                for i, page in self.numbers(b, t["sel_pages"].shape[0]):
                    self.eng.dma_start(
                        sx[:, i, kv, :],
                        t["sel_pages"][bass.ds(page, 1), :, P * kv:P * kv + P]
                        .rearrange("o p n -> (o p) n")
                    ).then_inc(s_sL[kv][self.who], 16)

            def turn(self, b, ahead, win_k, win_v):
                hold(self.eng, s_sr, b * 8)
                self.eng.sem_inc(self.turns, 1)
                win_k(b)
                self.sel(b, 0)
                hold(self.eng, s_v, b)
                self.eng.sem_inc(self.turns, 1)
                win_v(b)
                self.sel(b, 1)
                if ahead:
                    hold(self.eng, s_hid, b * 2 + 2 + N0)
                    self.eng.sem_inc(self.turns, 1)
                    self.cmp(b + 1)

            def run(self, win_k, win_v):
                self.eng.wait_ge(s_pt, 16)
                self.cmp(0)
                win_k(0)
                self.sel(0, 0)
                win_v(0)
                self.sel(0, 1)
                self.eng.wait_ge(s_hid, 2 + N0)
                self.cmp(1)
                with self.eng.Fori(1, B - 1) as b:
                    self.turn(b, True, win_k, win_v)
                with self.eng.Fori(B - 1, B) as b:
                    self.turn(b, False, win_k, win_v)

        with nc.Block() as block:
            @block.sync
            def _(sp):
                def win_k(b):
                    sp.dma_start(wk[:, :], t["win_k"][bass.ds(b, 1)].rearrange("o p n -> (o p) n")
                                 ).then_inc(s_wk, 16)

                def win_v(b):
                    sp.dma_start(wv[:, :, :],
                                 t["win_v"][bass.ds(b, 1)].rearrange("o p c n -> (o p) c n")
                                 ).then_inc(s_wL, 16)
                    for k in range(2):
                        sp.dma_start(vnew[S * k:S * k + S, :],
                                     t["scr_v"][bass.ds(b * S, S), k, :]).then_inc(s_wL, 16)

                sp.dma_start(pt[:, :], t["page_table"]).then_inc(s_pt, 16)
                Pages(sp, mybir.EngineType.SP, 0, s_turn).run(win_k, win_v)

            @block.gpsimd
            def _(pool):
                def none(b):
                    pass
                Pages(pool, mybir.EngineType.Pool, 1, s_turn2).run(none, none)

            @block.scalar
            def _(act):
                def compress_k(n0):
                    hidden_act(act, NSEG, hid, hsq, 0, n0)
                    tanh_act(act, NSEG, hin, 0, n0)

                def copy_k(n):
                    hold(act, s_kk, n)
                    act.activation(kcT[:, :], banks[5][:, 0:NC_S], ACT.Copy,
                                   scale=0.5).then_inc(s_kkr, 1)

                def turn(b, ahead):
                    n0 = b * 2 + N0
                    hold(act, s_cm, b + 1)
                    act.activation(T[:, T_CMP:], T[:, T_CMP:], ACT.Exp, scale=SCALE,
                                   bias=mt[:, 0:1], accum_out=dn[:, 0:1]).then_inc(s_ce, 1)
                    tanh_act(act, NSEG, hin, 1, n0)
                    hold(act, s_ck, b + 2)
                    act.activation(vc[:, 0, :], banks[7][:, 0:P], ACT.Copy, scale=0.5)
                    act.activation(vc[0:P - 1, 1, :], banks[7][0:P - 1, P:2 * P], ACT.Copy,
                                   scale=0.5).then_inc(s_ckr, 1)
                    hold(act, s_sm, b + 1)
                    act.activation(T[:, 0:T_NEW + S], T[:, 0:T_NEW + S], ACT.Exp, scale=SCALE,
                                   bias=mt[:, 1:2], accum_out=dn[:, 1:2])
                    act.activation(T[:, T_NEW + S:T_CMP], T[:, T_NEW + S:T_CMP], ACT.Exp,
                                   scale=SCALE, bias=mt[:, 2:3],
                                   accum_out=dn[:, 2:3]).then_inc(s_se, 1)
                    if ahead:
                        compress_k(n0 + 2)
                    for n in range(2):
                        hold(act, s_ft, b * 3 + n + 1)
                        act.activation(pT[:, 512 * n:512 * n + 512], banks[2 + n][:, :],
                                       ACT.Copy).then_inc(s_fc, 1)
                    hold(act, s_ft, b * 3 + 3)
                    for k0, k1, m in ((0, 5, P), (5, 6, P - 1), (6, 7, 2 * S)):
                        last = act.activation(pT[0:m, 1024 + NS * k0:1024 + NS * k1],
                                              banks[4][0:m, NS * k0:NS * k1], ACT.Copy)
                    last.then_inc(s_fc, 1)
                    if ahead:
                        copy_k(b + 2)
                    hold(act, s_os, b + 1)
                    act.activation(oaT[:, :, bass.ds(b * S + SEQ, S)],
                                   banks[6][:, 0:16].rearrange("p (r s) -> p r s", r=R),
                                   ACT.Copy).then_inc(s_or, 1)
                    if ahead:
                        hidden_act(act, NSEG, hid, hsq, 1, n0 + 2)

                act.sem_inc(s_or, 1)
                compress_k(N0)
                copy_k(1)
                hidden_act(act, NSEG, hid, hsq, 1, N0)
                with act.Fori(0, B - 1) as b:
                    turn(b, True)
                with act.Fori(B - 1, B) as b:
                    turn(b, False)

            @block.vector
            def _(dve):
                ch = Chain(dve, sem("dve_chain4"))
                ch.link(dve.memset(qb[:, :], 0.0))
                ch.link(dve.memset(imp[:, :], 0.0))

                def compress_k(n0):
                    join_dve(dve, NSEG, hid, 0, n0)
                    inner_dve(dve, ch, NSEG, hid, hsq, hin, 0, n0)
                    outer_dve(dve, NSEG, hid, hin, 0, n0)

                def turn(b, ahead):
                    n0 = b * 2 + N0
                    for g in range(G):
                        last = dve.tensor_copy(
                            qb[g * DH:g * DH + DH, 16 * g:16 * g + 16].rearrange(
                                "p (s r) -> p r s", s=S),
                            qaS[g * DH:g * DH + DH, :, bass.ds(b * S, S)])
                        if g == 0:
                            ch.count(last)
                    last.then_inc(s_qb, 1)
                    join_dve(dve, NSEG, hid, 1, n0)
                    hold(dve, s_a, b + 1)
                    ch.link(dve.tensor_copy(T[:, T_CMP:], banks[6][0:NS, 0:NC_S]))
                    ch.link(dve.tensor_reduce(mt[:, 0:1], T[:, T_CMP:], AX.X, ALU.max))
                    dve.tensor_scalar(mt[:, 0:1], mt[:, 0:1], -SCALE, None, ALU.mult).then_inc(s_cm, 1)
                    ch.count(dve.tensor_tensor(T[:, T_NEW:T_WIN], banks[6][0:NS, 256:256 + 2 * S],
                                               row[:, R_NEW:R_NEW + 2 * S], ALU.add))
                    dve.tensor_tensor(T[:, T_WIN:T_CMP], banks[7][0:NS, :],
                                      row[:, R_WIN:R_WIN + 512], ALU.add).then_inc(s_ar, 1)
                    hold(dve, s_ce, b + 1)
                    ch.link(dve.reciprocal(dn[:, 0:1], dn[:, 0:1]))
                    dve.tensor_scalar(T[:, T_CMP:], T[:, T_CMP:], dn[:, 0:1], None,
                                      ALU.mult).then_inc(s_pc, 1)
                    inner_dve(dve, ch, NSEG, hid, hsq, hin, 1, n0)
                    hold(dve, s_im, b + 1)
                    ch.link(dve.tensor_copy(imp[:, 1:NSEG], banks[6][0:NS, 0:NC_S]))
                    n = NB - 1
                    i4 = imp[:, 0:NSEG].rearrange("p (j m) -> p j m", m=4)
                    ch.count(dve.tensor_reduce(part[:, 0:n], i4[:, :, 1:4], AX.X, ALU.add))
                    ch.link(dve.tensor_tensor(score[:, 0:n], i4[:, :, 0],
                                              imp[:, 4:NSEG + 1:4], ALU.add))
                    ch.link(dve.scalar_tensor_tensor(out=score[:, 0:n], in0=part[:, 0:n], scalar=2.0,
                                                     in1=score[:, 0:n], op0=ALU.mult, op1=ALU.add))
                    ch.count(dve.memset(score[:, 0:1], FORCED))
                    ch.count(dve.memset(score[:, NB - 2:NB], FORCED))
                    for _ in range(2):
                        dve.drain()
                        dve.max(best[:, :], score[:, :])
                        dve.drain()
                        ch.count(dve.match_replace(score[:, :], best[:, :], score[:, :], TAKEN))
                    ch.wait()
                    ch.link(dve.tensor_scalar(score[:, :], score[:, :], TAKEN, 1.0, ALU.is_equal,
                                              ALU.subtract))
                    ch.link(dve.tensor_scalar(score[:, :], score[:, :], -NEG, None, ALU.mult))
                    outer_dve(dve, NSEG, hid, hin, 1, n0)
                    for c in range(8):
                        hold(dve, s_s, b * 8 + c + 1)
                        bm = score[:, 8 * c:8 * c + 8].rearrange("p (j o) -> p j o", o=1)
                        dve.tensor_tensor(
                            T[:, 512 * c:512 * c + 512].rearrange("p (j k) -> p j k", k=SELB),
                            banks[SBANK[c]][0:NS, :].rearrange("p (j k) -> p j k", k=SELB),
                            bm.to_broadcast([NS, 8, SELB]), ALU.add).then_inc(s_sr, 1)
                    hold(dve, s_sr, b * 8 + 8)
                    ch.count(dve.tensor_reduce(mt[:, 1:2], T[:, 0:T_NEW + S], AX.X, ALU.max))
                    ch.link(dve.tensor_reduce(mt[:, 2:3], T[:, T_NEW + S:T_CMP], AX.X, ALU.max))
                    dve.tensor_scalar(mt[:, 1:3], mt[:, 1:3], -SCALE, None, ALU.mult).then_inc(s_sm, 1)
                    hold(dve, s_se, b + 1)
                    ch.link(dve.reciprocal(dn[:, 1:3], dn[:, 1:3]))
                    gate = bgate[:, bass.ds(b, 1), :].rearrange("p o c -> p (o c)")
                    ch.link(dve.tensor_tensor(dn[:, 1:3], dn[:, 1:3], gate[:, 1:3], ALU.mult))
                    ch.link(dve.tensor_copy(dn[:, 0:1], gate[:, 0:1]))
                    for k, (c0, c1) in enumerate(((T_CMP, T_CMP + NC_S), (0, T_NEW + S),
                                                  (T_NEW + S, T_CMP))):
                        last = dve.tensor_scalar(T[:, c0:c1], T[:, c0:c1], dn[:, k:k + 1], None,
                                                 ALU.mult)
                        if k < 2:
                            ch.count(last)
                    last.then_inc(s_sp, 1)
                    if ahead:
                        compress_k(n0 + 2)
                    hold(dve, s_v, b + 1)
                    dve.tensor_tensor(om[:, :], banks[7][0:NS, 0:P], row[:, R_GRP:R_GRP + P],
                                      ALU.mult).then_inc(s_om, 1)

                compress_k(N0)
                with dve.Fori(0, B - 1) as b:
                    ch.enter(b, 24)
                    turn(b, True)
                ch.leave(B - 1)
                with dve.Fori(B - 1, B) as b:
                    turn(b, False)

            @block.tensor
            def _(pe):
                def turn(b, ahead):
                    n0 = b * 2 + N0
                    hold(pe, s_kkr, b + 1)
                    hold(pe, s_qb, b + 1)
                    hold(pe, s_or, b + 1)
                    hold(pe, s_wk, b * 16 + 16)
                    new = bass.ds(b * S, S)
                    pe.matmul(banks[6][0:NS, 0:NC_S], qb[:, :], kcT[:, :], start=True, stop=True)
                    pe.matmul(banks[6][0:NS, 256:256 + S], qb[:, :], kvS[:, 2, new], start=True,
                              stop=True)
                    pe.matmul(banks[6][0:NS, 256 + S:256 + 2 * S], qb[:, :], kvS[:, 4, new],
                              start=True, stop=True)
                    pe.matmul(banks[7][0:NS, :], qb[:, :], wk[:, :], start=True,
                              stop=True).then_inc(s_a, 1)
                    hold(pe, s_pc, b + 1)
                    pe.matmul(banks[6][0:NS, 0:NC_S], row[:, R_IMP:R_IMP + NS], T[:, T_CMP:],
                              start=True, stop=True).then_inc(s_im, 1)
                    pages_landed(pe, s_sL[0], b + 1)
                    for c in range(8):
                        if c >= 4:
                            hold(pe, s_sr, b * 8 + c - 3)
                        pe.matmul(banks[SBANK[c]][0:NS, :], qb[:, :], sx[:, 4 * c:4 * c + 4, 0, :],
                                  start=True, stop=True).then_inc(s_s, 1)
                    second_v_pe(pe, hid, n0)
                    if ahead:
                        pages_landed(pe, s_cL, b + 2)
                        hidden_pe(pe, cx, NSEG, 0, n0 + 2)
                    hold(pe, s_sp, b + 1)
                    for n in range(2):
                        for k in range(16):
                            c = 16 * n + k
                            last = pe.transpose(banks[2 + n][:, NS * k:NS * k + NS],
                                                T[:, P * c:P * c + P], ident[0:NS, 0:NS])
                        last.then_inc(s_ft, 1)
                    tail = [(T_WIN + P * c, P) for c in range(4)]
                    tail += [(T_CMP, P), (T_CMP + P, P - 1), (T_NEW, 2 * S)]
                    for k, (c0, m) in enumerate(tail):
                        last = pe.transpose(banks[4][0:m, NS * k:NS * k + NS], T[:, c0:c0 + m],
                                            ident[0:NS, 0:NS])
                    last.then_inc(s_ft, 1)
                    hold(pe, s_ckr, b + 2)
                    hold(pe, s_wL, b * 48 + 48)
                    pages_landed(pe, s_sL[1], b + 1)
                    vals = [(sx[:, c, 1, :], P) for c in range(PAGES)]
                    vals += [(wv[:, c, :], P) for c in range(4)]
                    vals += [(vc[:, 0, :], P), (vc[0:P - 1, 1, :], P - 1), (vnew[:, :], 2 * S)]
                    for k, (v, m) in enumerate(vals):
                        if k % 16 == 0:
                            hold(pe, s_fc, b * 3 + k // 16 + 1)
                        last = pe.matmul(banks[7][0:NS, 0:P], pT[0:m, NS * k:NS * k + NS], v,
                                         start=(k == 0), stop=(k == NCH - 1))
                    last.then_inc(s_v, 1)
                    if ahead:
                        hidden_pe(pe, cx, NSEG, 1, n0 + 2)
                        second_k_pe(pe, hid, n0 + 2)
                    hold(pe, s_om, b + 1)
                    pe.matmul(banks[6][:, 0:16], om[:, :], row[:, R_SPR:R_SPR + 16], start=True,
                              stop=True).then_inc(s_os, 1)

                pages_landed(pe, s_cL, 1)
                for kv in range(2):
                    hidden_pe(pe, cx, NSEG, kv, N0)
                second_k_pe(pe, hid, N0)
                with pe.Fori(0, B - 1) as b:
                    turn(b, True)
                with pe.Fori(B - 1, B) as b:
                    turn(b, False)
        p4.close()

        p5 = ExitStack()
        dk = [sb(f"dk{i}", [P, 4, DILK], p5) for i in range(2)]
        dvs = [sb(f"dvs{i}", [P, 9, 512], p5) for i in range(2)]
        dvn = [sb(f"dvn{i}", [3 * S, 512], p5) for i in range(2)]
        lq = [sb(f"lq{i}", [P, 3, 136], p5) for i in range(2)]
        TD = [sb(f"TD{i}", [NS, DILK + 12], p5) for i in range(2)]
        pTD = [sb(f"pTD{i}", [P, 10 * NS], p5) for i in range(2)]
        omD = [sb(f"omD{i}", [NS, 512], p5) for i in range(2)]
        md = sb("md", [NS, 2], p5)
        dd = sb("dd", [NS, 2], p5)
        s_kL = [sem(f"dil_keys_landed{i}") for i in range(2)]
        s_lq = sem("dil_queries_ready")
        s_ds = sem("dil_scores_ready")
        s_dsr = sem("dil_scores_read")
        s_dm = sem("dil_maximum_ready")
        s_de = sem("dil_exp_ready")
        s_dp = sem("dil_probs_ready")
        s_dt = sem("dil_probsT_bank_ready")
        s_dc = sem("dil_probsT_ready")
        s_dvv = sem("dil_request_summed")
        s_dom = sem("dil_request_masked")
        s_dos = sem("dil_request_spread")
        s_dor = sem("dil_request_finished")
        GOFF = (0, 128, 640)
        GLEN = (128, 512, 512)

        with nc.Block() as block:
            @block.sync
            def _(sp):
                def load(b, i):
                    sp.dma_start(dk[i][:, :, :], t["dil_k"][bass.ds(b, 1)].rearrange(
                        "o p c n -> (o p) c n")).then_inc(s_kL[i], 16)
                    sp.dma_start(dvs[i][:, :, :], t["dil_v"][bass.ds(b, 1)].rearrange(
                        "o p c n -> (o p) c n")).then_inc(s_kL[i], 16)
                    for g in range(3):
                        w = WINS[g]
                        sp.dma_start(dvn[i][S * g:S * g + S, :],
                                     t[f"new_dil{g + 1}"][bass.ds(b, 1), w - S:w, 512:1024].rearrange(
                                         "o w c -> (o w) c")).then_inc(s_kL[i], 16)
                with sp.Fori(0, 1) as j:
                    for i in range(2):
                        load(j + i, i)
                with sp.Fori(1, B // 2) as j:
                    for i in range(2):
                        hold(sp, s_dvv, j * 2 + i - 1)
                        load(j * 2 + i, i)

            @block.gpsimd
            def _(pool):
                bulk_copies(pool, len(bulk) - sent["n"])

            @block.scalar
            def _(act):
                act.sem_inc(s_dor, 2)
                with act.Fori(0, B // 2) as j:
                    for i in range(2):
                        hold(act, s_dm, j * 2 + i + 1)
                        act.activation(TD[i][:, :], TD[i][:, :], ACT.Exp, scale=SCALE,
                                       bias=md[:, i:i + 1],
                                       accum_out=dd[:, i:i + 1]).then_inc(s_de, 1)
                    for i in range(2):
                        hold(act, s_dt, j * 2 + i + 1)
                        act.activation(pTD[i][:, 0:9 * NS], banks[4][:, 0:9 * NS], ACT.Copy)
                        act.activation(pTD[i][0:12, 9 * NS:], banks[4][0:12, 9 * NS:10 * NS],
                                       ACT.Copy).then_inc(s_dc, 1)
                        hold(act, s_dos, j * 2 + i + 1)
                        act.activation(obT[:, :, bass.ds(j * 2 * S + (SEQ + S * i), S)],
                                       banks[6][:, 0:16].rearrange("p (h s) -> p h s", h=4),
                                       ACT.Copy).then_inc(s_dor, 1)

            @block.vector
            def _(dve):
                ch = Chain(dve, sem("dve_chain5"))
                for i in range(2):
                    ch.link(dve.memset(lq[i][:, :, :], 0.0))
                with dve.Fori(0, B // 2) as j:
                    ch.enter(j, 20)
                    for i in range(2):
                        hold(dve, s_dor, j * 2 + 2)
                        for g in range(3):
                            for hh in range(2):
                                dst = lq[i][hh * DH:hh * DH + DH, g, :].rearrange(
                                    "p (k c) -> p k c", c=34)[:, :, hh:hh + 25:8]
                                last = dve.tensor_copy(
                                    dst, qkS[hh * DH:hh * DH + DH, :, g, bass.ds(j * 2 * S + S * i, S)])
                                if (g, hh) != (2, 1):
                                    ch.count(last)
                        last.then_inc(s_lq, 1)
                    for i in range(2):
                        hold(dve, s_ds, j * 2 + i + 1)
                        for g in range(3):
                            o = GOFF[g]
                            ch.count(dve.tensor_tensor(TD[i][:, o:o + GLEN[g]],
                                                       banks[g][0:NS, 0:GLEN[g]],
                                                       row[:, R_DIL + o:R_DIL + o + GLEN[g]], ALU.add))
                        dve.tensor_tensor(TD[i][:, DILK:], banks[3][0:NS, 0:12],
                                          row[:, R_DIL + DILK:R_DIL + DILK + 12],
                                          ALU.add).then_inc(s_dsr, 1)
                        hold(dve, s_dsr, j * 2 + i + 1)
                        ch.link(dve.tensor_reduce(md[:, i:i + 1], TD[i][:, :], AX.X, ALU.max))
                        dve.tensor_scalar(md[:, i:i + 1], md[:, i:i + 1], -SCALE, None,
                                          ALU.mult).then_inc(s_dm, 1)
                    for i in range(2):
                        hold(dve, s_de, j * 2 + i + 1)
                        ch.link(dve.reciprocal(dd[:, i:i + 1], dd[:, i:i + 1]))
                        dve.tensor_scalar(TD[i][:, :], TD[i][:, :], dd[:, i:i + 1], None,
                                          ALU.mult).then_inc(s_dp, 1)
                    for i in range(2):
                        hold(dve, s_dvv, j * 2 + i + 1)
                        dve.tensor_tensor(omD[i][:, :], banks[5][0:NS, :],
                                          row[:, R_HEAD:R_HEAD + 512], ALU.mult).then_inc(s_dom, 1)
                ch.leave(B // 2)

            @block.tensor
            def _(pe):
                with pe.Fori(0, B // 2) as j:
                    def scores(i):
                        hold(pe, s_lq, j * 2 + i + 1)
                        hold(pe, s_kL[i], j * 80 + 80)
                        if i:
                            hold(pe, s_dsr, j * 2 + i)
                        for g in range(3):
                            o = GOFF[g]
                            for k in range(4):
                                pe.matmul(banks[g][0:NS, 0:GLEN[g]], lq[i][:, g, 32 * k:32 * k + 32],
                                          dk[i][:, k, o:o + GLEN[g]], start=(k == 0), stop=(k == 3))
                        for g in range(3):
                            for k in range(4):
                                last = pe.matmul(banks[3][0:NS, S * g:S * g + S],
                                                 lq[i][:, g, 32 * k:32 * k + 32],
                                                 qkS[:, k, 3 + g, bass.ds(j * 2 * S + S * i, S)],
                                                 start=(k == 0), stop=(k == 3))
                        last.then_inc(s_ds, 1)

                    for i in range(2):
                        scores(i)
                    for i in range(2):
                        hold(pe, s_dp, j * 2 + i + 1)
                        for c in range(10):
                            m = P if c < 9 else 12
                            last = pe.transpose(banks[4][0:m, NS * c:NS * c + NS],
                                                TD[i][:, P * c:P * c + m], ident[0:NS, 0:NS])
                        last.then_inc(s_dt, 1)
                        hold(pe, s_dc, j * 2 + i + 1)
                        for c in range(10):
                            m = P if c < 9 else 12
                            v = dvs[i][:, c, :] if c < 9 else dvn[i][:, :]
                            last = pe.matmul(banks[5][0:NS, :], pTD[i][0:m, NS * c:NS * c + NS], v,
                                             start=(c == 0), stop=(c == 9))
                        last.then_inc(s_dvv, 1)
                        hold(pe, s_dom, j * 2 + i + 1)
                        if i:
                            hold(pe, s_dor, j * 2 + 2 + i)
                        for k in range(4):
                            last = pe.matmul(banks[6][:, S * k:S * k + S], omD[i][:, P * k:P * k + P],
                                             row[:, R_TOK:R_TOK + S], start=True, stop=True)
                        last.then_inc(s_dos, 1)
        p5.close()
        pc.close()
        p6 = ExitStack()
        wr6 = sb("wring6", [P, RING, UNIT], p6)
        x6 = sb("x6", [P, KD, NT], p6)
        pA = ExitStack()
        mT = sb("mT", [P, KD, NT], pA)
        gm = sb("gm", [P, 2, 3, NT], pA)
        s_x6 = sem("x_again_landed")
        s_gt = sem("merge_gates_ready")
        s_bp = sem("branch_tile_ready")
        s_bq = sem("branch_tile_read")
        s_xo = sem("x_updated")
        s_mj = sem("merged_ready")

        def sq7(k):
            return oaT[:, k, :] if k < 4 else obT[:, k - 4, :]

        def out_tile(pe, n, first, last_k, k, w, wk, rhs):
            pe.matmul(banks[3 + n % 2][:, 0:HT], w[:, wk * P:wk * P + P], rhs[:, k, 0:HT],
                      start=first, stop=last_k)
            return pe.matmul(banks[5 + n % 2][:, 0:HT], w[:, wk * P:wk * P + P], rhs[:, k, HT:NT],
                             start=first, stop=last_k)

        with nc.Block() as block:
            @block.sync
            def _(sp):
                for u in range(U_MIX, U_MIX + RING):
                    sp.wait_ge(sm["w_used"], U_MIX)
                    sp.dma_start(ring_slot(wr6, u), t["w"][u]).then_inc(w_landed[u % RING], 16)
                for k in range(KD):
                    sp.dma_start(x6[:, k, :], t["xT"][:, k, :]).then_inc(s_x6, 16)
                with sp.Fori(0, 3) as j:
                    for n in range(RING):
                        hold(sp, sm["w_used"], j * 9 + U_MIX + n + 1)
                        sp.dma_start(ring_slot(wr6, U_MIX + n),
                                     t["w"][bass.ds(j * 9 + U_MIX + 9 + n, 1)].rearrange(
                                         "o p n -> (o p) n")
                                     ).then_inc(w_landed[(U_MIX + n) % RING], 16)
                load_units(sp, wr6, U_OUT, 8)

            @block.scalar
            def _(act):
                with act.Fori(0, 4) as j:
                    for n in range(6):
                        hold(act, sm["w_used"], j * 9 + U_MIX + n + 1)
                        if n == 0:
                            hold(act, s_mj, j * 2 + 2)
                        g = gm[:, n // 3, n % 3, :]
                        act.activation(g[:, 0:HT], banks[n % 2][:, 0:HT], ACT.Tanh, scale=0.5)
                        act.activation(g[:, HT:NT], banks[2 if n % 2 == 0 else 7][:, 0:HT],
                                       ACT.Tanh, scale=0.5).then_inc(s_gt, 1)
                act.wait_ge(s_bq, 30)
                for k in range(KD):
                    act.wait_ge(s_xo, k + 1)
                    act.activation(sq7(k), x6[:, k, :], ACT.Square).then_inc(sm["sq_ready"], 1)

            @block.vector
            def _(dve):
                ch = Chain(dve, sem("dve_chain6"))
                dve.sem_inc(s_bq, 6)
                dve.sem_inc(s_mj, 2)
                with dve.Fori(0, 4) as j:
                    ch.enter(j, 8)
                    for n in range(6):
                        hold(dve, s_bp, j * 6 + n + 1)
                        hold(dve, s_gt, j * 6 + n + 1)
                        g = gm[:, n // 3, n % 3, :]
                        ch.count(dve.scalar_tensor_tensor(
                            out=g[:, 0:HT], in0=g[:, 0:HT], scalar=1.0, in1=banks[3 + n % 2][:, 0:HT],
                            op0=ALU.add, op1=ALU.mult))
                        dve.scalar_tensor_tensor(
                            out=g[:, HT:NT], in0=g[:, HT:NT], scalar=1.0,
                            in1=banks[5 + n % 2][:, 0:HT], op0=ALU.add,
                            op1=ALU.mult).then_inc(s_bq, 1)
                        if n % 3 == 2:
                            a = gm[:, n // 3, :, :]
                            m = mT[:, bass.ds(j * 2 + n // 3, 1), :].rearrange("p o q -> p (o q)")
                            hold(dve, s_bq, j * 6 + 6 + n + 1)
                            ch.link(dve.tensor_tensor(a[:, 0, :], a[:, 0, :], a[:, 1, :], ALU.add))
                            dve.tensor_tensor(m, a[:, 0, :], a[:, 2, :], ALU.add).then_inc(s_mj, 1)
                ch.leave(4)
                dve.wait_ge(s_x6, 16 * KD)
                for n in range(KD):
                    dve.wait_ge(s_bp, 24 + n + 1)
                    x = x6[:, n, :]
                    ch.count(dve.scalar_tensor_tensor(
                        out=x[:, 0:HT], in0=banks[3 + n % 2][:, 0:HT], scalar=0.5, in1=x[:, 0:HT],
                        op0=ALU.mult, op1=ALU.add))
                    dve.scalar_tensor_tensor(
                        out=x[:, HT:NT], in0=banks[5 + n % 2][:, 0:HT], scalar=0.5,
                        in1=x[:, HT:NT], op0=ALU.mult, op1=ALU.add).then_inc(s_xo, 1)

            @block.tensor
            def _(pe):
                with pe.Fori(0, 4) as j:
                    for n in range(6):
                        if n >= 2:
                            hold(pe, s_gt, j * 6 + n - 1)
                        elif n == 0:
                            hold(pe, s_bq, j * 6 + 6)
                        u = U_MIX + n
                        unit_landed(pe, u, j, 9)
                        w = ring_slot(wr6, u)
                        for k in range(KD):
                            pe.matmul(banks[n % 2][:, 0:HT], w[:, k * P:k * P + P], hT[:, k, 0:HT],
                                      start=(k == 0), stop=(k == KD - 1))
                        for k in range(KD):
                            last = pe.matmul(banks[2 if n % 2 == 0 else 7][:, 0:HT],
                                             w[:, k * P:k * P + P], hT[:, k, HT:NT],
                                             start=(k == 0), stop=(k == KD - 1))
                        last.then_inc(sm["w_used"], 1)
                    for n in range(6):
                        if n >= 2:
                            hold(pe, s_bq, j * 6 + 6 + n - 1)
                        src = (oaT, obT, ocT)[n % 3]
                        for k in range(4):
                            at = 4 * n + k
                            u = U_MIX + 6 + at // KD
                            if at % KD == 0:
                                unit_landed(pe, u, j, 9)
                            w = ring_slot(wr6, u)
                            wk = at % KD
                            pe.matmul(banks[3 + n % 2][:, 0:HT], w[:, wk * P:wk * P + P],
                                      src[:, k, 0:HT], start=(k == 0), stop=(k == 3))
                            last = pe.matmul(banks[5 + n % 2][:, 0:HT], w[:, wk * P:wk * P + P],
                                             src[:, k, HT:NT], start=(k == 0), stop=(k == 3))
                        last.then_inc(s_bp, 1)
                    hold(pe, s_bq, j * 6 + 6 + 6)
                    pe.sem_inc(sm["w_used"], 3)
                for n in range(KD):
                    if n >= 2:
                        pe.wait_ge(s_xo, n - 1)
                    u = U_OUT + n
                    unit_landed(pe, u)
                    if n == 0:
                        pe.wait_ge(s_mj, 10)
                    for k in range(KD):
                        last = out_tile(pe, n, k == 0, k == KD - 1, k, ring_slot(wr6, u), k, mT)
                    last.then_inc(s_bp, 1)
        pA.close()

        p7 = ExitStack()
        aT = sb("aT", [P, 32, NT], p7)
        rl = sb("rl", [P, 2, NT], p7)
        rstd = sb("rstd7", [P, NT], p7)
        s_rl = sem("relu_ready")
        s_up = sem("up_ready")
        s_dn = sem("down_ready")
        s_dnr = sem("down_read")

        def slot8(n):
            return wr6[:, n, :]

        w8 = [sem(f"ffn_unit_landed{i}") for i in range(8)]
        s_u8 = sem("ffn_units_used")

        with nc.Block() as block:
            @block.sync
            def _(sp):
                for n in range(8):
                    sp.dma_start(slot8(n), t["w"][U_UP + n]).then_inc(w8[n], 16)
                with sp.Fori(0, 7) as j:
                    for n in range(8):
                        hold(sp, s_u8, j * 8 + n + 1)
                        sp.dma_start(slot8(n), t["w"][bass.ds(j * 8 + U_UP + 8 + n, 1)].rearrange(
                            "o p n -> (o p) n")).then_inc(w8[n], 16)
                for k in range(KD):
                    sp.wait_ge(sm["h_ready"], 2 * KD + k + 1)
                    sp.dma_start(t["yT"][:, k, :], hT[:, k, :]).then_inc(sm["out_done"], 16)

            @block.scalar
            def _(act):
                ch = None
                rms_act(act, ch, x6, sq7, 1, rstd, squares=False)
                with act.Fori(0, 4) as j:
                    for n in range(8):
                        hold(act, s_u8, j * 8 + n + 1)
                        hold(act, s_up, j * 8 + n + 1)
                        r = rl[:, n % 2, :]
                        act.activation(r[:, 0:HT], banks[n % 2][:, 0:HT], ACT.Relu)
                        act.activation(r[:, HT:NT], banks[2 + n % 2][:, 0:HT],
                                       ACT.Relu).then_inc(s_rl, 1)
                for k in range(KD):
                    act.wait_ge(s_dnr, k + 1)
                    act.activation(sq7(k), x6[:, k, :], ACT.Square).then_inc(sm["sq_ready"], 1)
                rms_act(act, ch, x6, sq7, 2, rstd, squares=False)

            @block.vector
            def _(dve):
                ch = Chain(dve, sem("dve_chain7"))
                dve.sem_inc(s_up, 2)
                rms_dve(dve, ch, x6, hT, 1, rstd)
                with dve.Fori(0, 4) as j:
                    for n in range(8):
                        hold(dve, s_rl, j * 8 + n + 1)
                        dve.tensor_tensor(
                            aT[:, bass.ds(j * 8 + n, 1), :].rearrange("p o q -> p (o q)"),
                            rl[:, n % 2, :], rl[:, n % 2, :], ALU.mult).then_inc(s_up, 1)
                with dve.Fori(0, 4) as j:
                    ch.enter(j, 2)
                    for n in range(2):
                        hold(dve, s_dn, j * 2 + n + 1)
                        x = x6[:, bass.ds(j * 2 + n, 1), :].rearrange("p o q -> p (o q)")
                        ch.count(dve.tensor_tensor(x[:, 0:HT], banks[3 + n % 2][:, 0:HT], x[:, 0:HT],
                                                   ALU.add))
                        dve.tensor_tensor(x[:, HT:NT], banks[5 + n % 2][:, 0:HT], x[:, HT:NT],
                                          ALU.add).then_inc(s_dnr, 1)
                ch.leave(4)
                dve.wait_ge(s_dnr, 8)
                rms_dve(dve, ch, x6, hT, 2, rstd)

            @block.tensor
            def _(pe):
                rms_pe(pe, sq7, 1)
                pe.wait_ge(sm["h_ready"], 2 * KD)
                with pe.Fori(0, 4) as j:
                    for n in range(8):
                        hold(pe, s_rl, j * 8 + n - 1) if n >= 2 else hold(pe, s_up, j * 8 + n + 1)
                        hold(pe, w8[n], j * 16 + 16)
                        w = slot8(n)
                        for k in range(KD):
                            pe.matmul(banks[n % 2][:, 0:HT], w[:, k * P:k * P + P], hT[:, k, 0:HT],
                                      start=(k == 0), stop=(k == KD - 1))
                        for k in range(KD):
                            last = pe.matmul(banks[2 + n % 2][:, 0:HT], w[:, k * P:k * P + P],
                                             hT[:, k, HT:NT], start=(k == 0), stop=(k == KD - 1))
                        last.then_inc(s_u8, 1)
                pe.wait_ge(s_up, 34)

                def down_tiles(j, first):
                    for n in range(2):
                        if not first:
                            hold(pe, s_dnr, j * 2 + n - 1)
                        for q in range(4):
                            hold(pe, w8[4 * n + q], j * 16 + 16 * 5)
                            for k in range(KD):
                                kk = KD * q + k
                                w = slot8(4 * n + q)
                                mm = pe.matmul(banks[3 + n][:, 0:HT], w[:, k * P:k * P + P],
                                               aT[:, kk, 0:HT], start=(kk == 0), stop=(kk == 31))
                                if kk == 0 and not (first and n == 0):
                                    mm.then_inc(s_u8, 1)
                                last = pe.matmul(banks[5 + n][:, 0:HT], w[:, k * P:k * P + P],
                                                 aT[:, kk, HT:NT], start=(kk == 0), stop=(kk == 31))
                            if q < 3:
                                last.then_inc(s_u8, 1)
                        last.then_inc(s_dn, 1)

                with pe.Fori(0, 1) as j:
                    down_tiles(j, True)
                with pe.Fori(1, 4) as j:
                    down_tiles(j, False)
                rms_pe(pe, sq7, 2)
        p7.close()
        p6.close()
        with nc.Block() as block:
            @block.sync
            def _(sp):
                sp.wait_ge(sm["out_done"], 48 + 16 * KD)
                sp.wait_ge(sm["store_done"], 256)
                sp.wait_ge(sm["bulk_done"], 16 * sent["n"])


_OUTS = [("yT", (P, KD, NT)), ("kvT", (P, 6, SEQ)), ("kvS", (P, 6, NS)), ("dilT", (4, P, 6, SEQ)),
         ("new_win", (B, 512, 256)), ("new_dil1", (B, 128, 1024)), ("new_dil2", (B, 512, 1024)),
         ("new_dil3", (B, 2048, 1024)), ("sgu_v", (NS, 512))]
_SCRATCH = [("scr_gate", (24, NS)), ("scr_v", (NS, 2, P))]
_IN = [("xT", (P, KD, NT)), ("con", (P, C_END)), ("row", (NS, R_END)), ("norm_g", (P, 3, KD)),
       ("w", (N_UNITS, P, UNIT)), ("ln_g", (1, 512)), ("ln_b", (1, 512)), ("wsT", (P, 8, P)),
       ("ws4", (NS, 8, NS)), ("bs", (2, 4, P + NS)), ("half", (2, P)),
       ("w1", (P, 2, 16, HID)), ("w2", (HID, 2, DH)), ("pe_t", (P, 2, 16)), ("b1", (HID, 2)),
       ("page_table", (1, B * PAGES)), ("cmp_pages", (320, P, 256)), ("sel_pages", (320, P, 256)),
       ("win_k", (B, P, 512)), ("win_v", (B, P, 4, P)), ("dil_k", (B, P, 4, DILK)),
       ("dil_v", (B, P, 9, 512)),
       ("cache_win", (B, 512, 256)), ("cache_dil1", (B, 128, 1024)), ("cache_dil2", (B, 512, 1024)),
       ("cache_dil3", (B, 2048, 1024))]
DEBUG = []


def kernel(x_prompt, x_sample, cache_cmp_kv, cache_sel_kv, cache_win_kv, cache_dil1_kv,
           cache_dil2_kv, cache_dil3_kv, page_table, norm_mix_g, w_in, cmp_pe, cmp_w1, cmp_b1,
           cmp_w2, sgu_ln_g, sgu_ln_b, sgu_w, sgu_b, w_branch_a, w_branch_b, w_branch_c, w_out,
           norm_mlp_g, w_up, w_down, norm_final_g):
    import concourse.bacc as _bacc
    from concourse.bass_utils import run_bass_kernel_spmd as _run

    f = lambda a: np.asarray(a)
    x = np.concatenate([f(x_prompt)[0], f(x_sample).reshape(NS, D)], 0)
    con, row = shape_constants()
    a = {
        "xT": x.reshape(NT, KD, P).transpose(2, 1, 0),
        "con": con, "row": row,
        "norm_g": np.stack([f(norm_mix_g)[0], f(norm_mlp_g)[0], f(norm_final_g)]
                           ).reshape(3, KD, P).transpose(2, 0, 1),
        "w": weight_stream(f(w_in)[0], f(w_branch_a)[0], f(w_branch_b)[0], f(w_branch_c)[0],
                           f(w_out)[0], f(w_up)[0], f(w_down)[0]),
        "ln_g": f(sgu_ln_g), "ln_b": f(sgu_ln_b),
        "wsT": f(sgu_w)[0].transpose(2, 0, 1),
        "ws4": np.tile(f(sgu_w)[0, :, :S, :S].transpose(2, 0, 1), (B, 1, B)),
        "bs": np.concatenate([f(sgu_b)[0], np.tile(f(sgu_b)[0, :, :S], (1, B))], 1
                             ).reshape(4, 2, P + NS).transpose(1, 0, 2),
        "half": np.repeat(np.eye(2, dtype=np.float32), DH, 1),
        "w1": f(cmp_w1)[0].reshape(2, 16, P, HID).transpose(2, 0, 1, 3),
        "w2": f(cmp_w2)[0].transpose(1, 0, 2),
        "pe_t": f(cmp_pe)[0].reshape(2, 16, P).transpose(2, 0, 1),
        "b1": f(cmp_b1)[0].T,
        **sample_caches(f(cache_cmp_kv)[:, 0], f(cache_sel_kv)[:, 0], f(cache_win_kv)[:, 0],
                        [f(c)[:, 0] for c in (cache_dil1_kv, cache_dil2_kv, cache_dil3_kv)]),
        "page_table": f(page_table).reshape(1, B * PAGES),
        "cache_win": f(cache_win_kv).reshape(B, 512, 256),
        "cache_dil1": f(cache_dil1_kv).reshape(B, 128, 1024),
        "cache_dil2": f(cache_dil2_kv).reshape(B, 512, 1024),
        "cache_dil3": f(cache_dil3_kv).reshape(B, 2048, 1024),
    }
    nc = _bacc.Bacc("TRN2", target_bir_lowering=False, num_devices=1)
    t, arrays = {}, {}
    for name, shape in _IN:
        v = np.ascontiguousarray(a[name])
        assert v.shape == shape, (name, v.shape, shape)
        arrays[f"in_{name}"] = v
        t[name] = nc.dram_tensor(f"in_{name}", shape, mybir.dt.from_np(v.dtype),
                                 kind="ExternalInput").ap()
    for name, shape in _OUTS:
        t[name] = nc.dram_tensor(f"out_{name}", shape, F32, kind="ExternalOutput").ap()
    for name, shape in _SCRATCH:
        t[name] = nc.dram_tensor(name, shape, F32, kind="Internal").ap()
    for name in DEBUG:
        t["dbg_" + name] = nc.dram_tensor("dbg_" + name, (P, 4, NT), F32, kind="ExternalOutput").ap()
    trunk(nc, t)
    r = _run(nc, [arrays], core_ids=[0]).results[0]
    o = {name: r[f"out_{name}"] for name, _ in _OUTS}
    y = o["yT"].transpose(2, 1, 0).reshape(NT, D)
    kv = o["kvT"].transpose(2, 1, 0).reshape(1, 1, SEQ, 3, 2, G, DH)
    kvs = o["kvS"].transpose(2, 1, 0).reshape(B, 1, S, 3, 2, G, DH)
    dil = o["dilT"].reshape(4, 2, DH, 2, 3, SEQ).transpose(4, 5, 3, 0, 1, 2).reshape(
        3, 1, 1, SEQ, 2, 8, DH)
    return (y[:SEQ].reshape(1, SEQ, D), y[SEQ:].reshape(B, S, D),
            kv[:, :, :, 0], kv[:, :, :, 1], kv[:, :, :, 2],
            dil[0][:, :, -WINS[0]:], dil[1], dil[2],
            kvs[:, :, :, 0], kvs[:, :, :, 1],
            o["new_win"].reshape(B, 1, 512, 2, G, DH),
            o["new_dil1"].reshape(B, 1, 128, 2, 8, DH),
            o["new_dil2"].reshape(B, 1, 512, 2, 8, DH),
            o["new_dil3"].reshape(B, 1, 2048, 2, 8, DH),
            o["sgu_v"].reshape(B, 1, S, 512))
```
